# Optimizing a Trainium2 kernel written in Bass

```python
import jax
import jax.numpy as jnp
from jax import lax
import numpy as np

D_MODEL = 1024
BATCH = 1
SEQ = 1024
DEPTH = 1

HEAD_DIM = 64
N_Q_HEADS = 8
N_KV_HEADS = 2
Q_PER_KV = N_Q_HEADS // N_KV_HEADS
ATTN_WIDTH = N_Q_HEADS * HEAD_DIM
ATTN_KV_WIDTH = N_KV_HEADS * HEAD_DIM
ATTN_COLS = ATTN_WIDTH + 2 * ATTN_KV_WIDTH
WINDOW = 128
ATTN_BLOCK = 128
ROPE_THETA = 10000.0
N_RWKV_HEADS = 8
RWKV_WIDTH = N_RWKV_HEADS * HEAD_DIM
DECAY_RANK = 32
ICLR_RANK = 32
GATE_RANK = 96
RWKV_COLS = 3 * RWKV_WIDTH + 2 * DECAY_RANK + 2 * ICLR_RANK + GATE_RANK
IN_COLS = ATTN_COLS + RWKV_COLS
MIX_WIDTH = ATTN_WIDTH + RWKV_WIDTH
RWKV_GN_EPS = 64e-5
PEER_HEADS = 8
PEER_NKEYS = 128
PEER_EXPERTS = PEER_NKEYS * PEER_NKEYS
PEER_QDIM = 256
PEER_HALF = PEER_QDIM // 2
PEER_TOPK = 16
PEER_CHUNK = 128
LN_EPS = 1e-5
DEEPNORM_ALPHA = (2.0 * DEPTH) ** 0.25
DEEPNORM_BETA = (8.0 * DEPTH) ** -0.25

kernel_name = 'hybrid_attn_rwkv7_peer_encoder_layer'

def layer_norm(x, g, b):
    xf = x.astype(jnp.float32)
    mu = jnp.mean(xf, -1, keepdims=True)
    var = jnp.mean(jnp.square(xf - mu), -1, keepdims=True)
    y = (xf - mu) * lax.rsqrt(var + LN_EPS) * g.astype(jnp.float32) + b.astype(jnp.float32)
    return y.astype(x.dtype)

def rotary(t):
    s = t.shape[1]
    pos = jnp.arange(s, dtype=jnp.float32)
    inv_freq = ROPE_THETA ** (-jnp.arange(0, HEAD_DIM, 2, dtype=jnp.float32) / HEAD_DIM)
    ang = pos[:, None] * inv_freq[None, :]
    ang = jnp.concatenate([ang, ang], -1)[:, None, :]
    tf = t.astype(jnp.float32)
    t1, t2 = jnp.split(tf, 2, -1)
    rot = jnp.concatenate([-t2, t1], -1)
    return (tf * jnp.cos(ang) + rot * jnp.sin(ang)).astype(t.dtype)

def banded_window_attention(q, k, v, sink):
    b, s = q.shape[:2]
    nb = s // ATTN_BLOCK
    qb = q.reshape(b, nb, ATTN_BLOCK, N_KV_HEADS, Q_PER_KV, HEAD_DIM)

    def neighbours(t):
        tp = jnp.pad(t, ((0, 0), (ATTN_BLOCK, ATTN_BLOCK), (0, 0), (0, 0)))
        tb = tp.reshape(b, nb + 2, ATTN_BLOCK, N_KV_HEADS, HEAD_DIM)
        return jnp.concatenate([tb[:, :-2], tb[:, 1:-1], tb[:, 2:]], axis=2)

    kw = neighbours(k)
    vw = neighbours(v)
    logits = jnp.einsum('bnqhgd,bnkhd->bnhgqk', qb, kw).astype(jnp.float32) * (HEAD_DIM ** -0.5)
    qpos = jnp.arange(s).reshape(nb, ATTN_BLOCK)
    kpos = (jnp.arange(nb)[:, None] - 1) * ATTN_BLOCK + jnp.arange(3 * ATTN_BLOCK)[None, :]
    valid = ((jnp.abs(qpos[:, :, None] - kpos[:, None, :]) <= WINDOW)
             & (kpos[:, None, :] >= 0) & (kpos[:, None, :] < s))
    logits = jnp.where(valid[None, :, None, None], logits, -1e30)
    sink_l = sink.astype(jnp.float32).reshape(N_KV_HEADS, Q_PER_KV)[None, None, :, :, None, None]
    m = jnp.maximum(jnp.max(logits, -1, keepdims=True), sink_l)
    e = jnp.exp(logits - m)
    probs = e / (jnp.sum(e, -1, keepdims=True) + jnp.exp(sink_l - m))
    out = jnp.einsum('bnhgqk,bnkhd->bnqhgd', probs.astype(v.dtype), vw)
    return out.reshape(b, s, ATTN_WIDTH)

def centred_token_shift(p, mu_prev, mu_next):
    zero = jnp.zeros_like(p[:, :1])
    p_prev = jnp.concatenate([zero, p[:, :-1]], 1)
    p_next = jnp.concatenate([p[:, 1:], zero], 1)
    return p + mu_prev * (p_prev - p) + mu_next * (p_next - p)

def wkv7_step(state, inp):
    r, w, k, v, kk, a = inp
    sa = jnp.einsum('bhvk,bhk->bhv', state, -kk)
    state = (state * w[:, :, None, :]
             + sa[..., :, None] * (kk * a)[:, :, None, :]
             + v[..., :, None] * k[:, :, None, :])
    y = jnp.einsum('bhvk,bhk->bhv', state, r)
    return state, y

def wkv7_scan(r, w, k, v, kk, a, reverse):
    def tm(t):
        return jnp.moveaxis(t, 1, 0)
    s0 = jnp.zeros((r.shape[0], N_RWKV_HEADS, HEAD_DIM, HEAD_DIM), jnp.float32)
    _, y = lax.scan(wkv7_step, s0, (tm(r), tm(w), tm(k), tm(v), tm(kk), tm(a)), reverse=reverse)
    return jnp.moveaxis(y, 0, 1)

def rwkv7_bidirectional(p, mu_prev, mu_next, w0, w2, a0, a2, g2, k_k, k_a, r_k, lnx_g, lnx_b):
    f32 = jnp.float32
    b, s, _ = p.shape
    p = centred_token_shift(p.astype(f32), mu_prev.astype(f32), mu_next.astype(f32))
    cuts = np.cumsum([RWKV_WIDTH, RWKV_WIDTH, RWKV_WIDTH, 2 * DECAY_RANK, 2 * ICLR_RANK]).tolist()
    r, k, v, wd, ad, gd = jnp.split(p, cuts, -1)
    wd = wd.reshape(b, s, 2, DECAY_RANK)
    ad = ad.reshape(b, s, 2, ICLR_RANK)
    w_log = -jax.nn.softplus(-(w0.astype(f32) + jnp.einsum('bsdr,drc->bsdc', jnp.tanh(wd), w2.astype(f32)))) - 0.5
    decay = jnp.exp(-jnp.exp(w_log))
    a = jax.nn.sigmoid(a0.astype(f32) + jnp.einsum('bsdr,drc->bsdc', ad, a2.astype(f32)))
    g = jax.nn.sigmoid(gd) @ g2.astype(f32)

    def heads(t):
        return t.reshape(t.shape[:-1] + (N_RWKV_HEADS, HEAD_DIM))

    kk = heads(k * k_k.astype(f32))
    kk = kk * lax.rsqrt(jnp.maximum(jnp.sum(jnp.square(kk), -1, keepdims=True), 1e-24))
    k_dir = k[:, :, None, :] * (1.0 + (a - 1.0) * k_a.astype(f32))
    rh = heads(r)
    vh = heads(v)
    y = (wkv7_scan(rh, heads(decay[:, :, 0]), heads(k_dir[:, :, 0]), vh, kk, heads(a[:, :, 0]), False)
         + wkv7_scan(rh, heads(decay[:, :, 1]), heads(k_dir[:, :, 1]), vh, kk, heads(a[:, :, 1]), True))
    mu = jnp.mean(y, -1, keepdims=True)
    var = jnp.mean(jnp.square(y - mu), -1, keepdims=True)
    y = ((y - mu) * lax.rsqrt(var + RWKV_GN_EPS)).reshape(b, s, RWKV_WIDTH)
    y = y * lnx_g.astype(f32) + lnx_b.astype(f32)
    k_mean = heads(0.5 * (k_dir[:, :, 0] + k_dir[:, :, 1]))
    bonus = jnp.sum(rh * k_mean * r_k.astype(f32), -1, keepdims=True) * vh
    return (y + bonus.reshape(b, s, RWKV_WIDTH)) * g

def peer_ffn(h, wq, keys, u, v):
    b, s, d = h.shape
    t = b * s
    ht = h.reshape(t, d)
    q = (ht @ wq).reshape(t, PEER_HEADS, 2, PEER_HALF).astype(jnp.float32)
    sc = jnp.einsum('thpc,hpnc->thpn', q, keys.astype(jnp.float32))
    s1, i1 = lax.top_k(sc[:, :, 0], PEER_TOPK)
    s2, i2 = lax.top_k(sc[:, :, 1], PEER_TOPK)
    cand = (s1[..., :, None] + s2[..., None, :]).reshape(t, PEER_HEADS, PEER_TOPK * PEER_TOPK)
    cs, ci = lax.top_k(cand, PEER_TOPK)
    idx = (jnp.take_along_axis(i1, ci // PEER_TOPK, -1) * PEER_NKEYS
           + jnp.take_along_axis(i2, ci % PEER_TOPK, -1))
    gate = jax.nn.softmax(cs, -1).astype(h.dtype)
    n_chunks = t // PEER_CHUNK
    n_sel = PEER_HEADS * PEER_TOPK

    def chunk(args):
        hc, ic, gc = args
        z = jnp.einsum('cd,ced->ce', hc, u[ic])
        return jnp.einsum('ce,ced->cd', gc * jax.nn.gelu(z, approximate=False), v[ic])

    y = lax.map(chunk, (ht.reshape(n_chunks, PEER_CHUNK, d),
                        idx.reshape(n_chunks, PEER_CHUNK, n_sel),
                        gate.reshape(n_chunks, PEER_CHUNK, n_sel)))
    return y.reshape(b, s, d)

def setup_inputs(seed: int = 0) -> dict:
    key = jax.random.key(seed)
    ks = jax.random.split(key, 26)
    f32 = jnp.float32
    L = DEPTH

    def nrm(k, shape, scale):
        return jax.random.normal(k, shape, f32) * scale

    x = nrm(ks[0], (BATCH, SEQ, D_MODEL), 1.0)
    col_scale = jnp.ones((IN_COLS,), f32)
    col_scale = col_scale.at[ATTN_WIDTH + ATTN_KV_WIDTH:ATTN_COLS].set(DEEPNORM_BETA)
    col_scale = col_scale.at[ATTN_COLS + 2 * RWKV_WIDTH:ATTN_COLS + 3 * RWKV_WIDTH].set(DEEPNORM_BETA)
    w_in = nrm(ks[1], (L, D_MODEL, IN_COLS), D_MODEL ** -0.5) * col_scale
    mu_prev = jax.random.uniform(ks[2], (L, RWKV_COLS), f32, 0.0, 0.4)
    mu_next = jax.random.uniform(ks[3], (L, RWKV_COLS), f32, 0.0, 0.4)
    w0 = jax.random.uniform(ks[4], (L, 2, RWKV_WIDTH), f32, -4.0, 1.0)
    w2 = nrm(ks[5], (L, 2, DECAY_RANK, RWKV_WIDTH), 0.3 * DECAY_RANK ** -0.5)
    a0 = nrm(ks[6], (L, 2, RWKV_WIDTH), 0.5)
    a2 = nrm(ks[7], (L, 2, ICLR_RANK, RWKV_WIDTH), ICLR_RANK ** -0.5)
    g2 = nrm(ks[8], (L, GATE_RANK, RWKV_WIDTH), GATE_RANK ** -0.5)
    k_k = 0.85 + nrm(ks[9], (L, RWKV_WIDTH), 0.05)
    k_a = 1.0 + nrm(ks[10], (L, RWKV_WIDTH), 0.05)
    r_k = nrm(ks[11], (L, N_RWKV_HEADS, HEAD_DIM), 0.1)
    lnx_g = 1.0 + nrm(ks[12], (L, RWKV_WIDTH), 0.05)
    lnx_b = nrm(ks[13], (L, RWKV_WIDTH), 0.02)
    sink = nrm(ks[14], (L, N_Q_HEADS), 0.5)
    w_out = nrm(ks[15], (L, MIX_WIDTH, D_MODEL), DEEPNORM_BETA * MIX_WIDTH ** -0.5)
    ln1_g = 1.0 + nrm(ks[16], (L, D_MODEL), 0.05)
    ln1_b = nrm(ks[17], (L, D_MODEL), 0.02)
    peer_wq = nrm(ks[18], (L, D_MODEL, PEER_HEADS * PEER_QDIM), D_MODEL ** -0.5)
    peer_keys = nrm(ks[19], (L, PEER_HEADS, 2, PEER_NKEYS, PEER_HALF), PEER_HALF ** -0.5)
    peer_u = nrm(ks[20], (L, PEER_EXPERTS, D_MODEL), DEEPNORM_BETA * D_MODEL ** -0.5)
    peer_v = nrm(ks[21], (L, PEER_EXPERTS, D_MODEL), DEEPNORM_BETA)
    ln2_g = 1.0 + nrm(ks[22], (L, D_MODEL), 0.05)
    ln2_b = nrm(ks[23], (L, D_MODEL), 0.02)
    return {'x': x, 'w_in': w_in, 'mu_prev': mu_prev, 'mu_next': mu_next,
            'w0': w0, 'w2': w2, 'a0': a0, 'a2': a2, 'g2': g2,
            'k_k': k_k, 'k_a': k_a, 'r_k': r_k, 'lnx_g': lnx_g, 'lnx_b': lnx_b,
            'sink': sink, 'w_out': w_out, 'ln1_g': ln1_g, 'ln1_b': ln1_b,
            'peer_wq': peer_wq, 'peer_keys': peer_keys, 'peer_u': peer_u, 'peer_v': peer_v,
            'ln2_g': ln2_g, 'ln2_b': ln2_b}

def reference(x, w_in, mu_prev, mu_next, w0, w2, a0, a2, g2, k_k, k_a, r_k, lnx_g, lnx_b,
              sink, w_out, ln1_g, ln1_b, peer_wq, peer_keys, peer_u, peer_v, ln2_g, ln2_b):
    b, s, _ = x.shape
    h = x
    for l in range(DEPTH):
        proj = h @ w_in[l]
        q, k, v, pr = jnp.split(proj, [ATTN_WIDTH, ATTN_WIDTH + ATTN_KV_WIDTH, ATTN_COLS], -1)
        q = rotary(q.reshape(b, s, N_Q_HEADS, HEAD_DIM))
        k = rotary(k.reshape(b, s, N_KV_HEADS, HEAD_DIM))
        v = v.reshape(b, s, N_KV_HEADS, HEAD_DIM)
        y_attn = banded_window_attention(q, k, v, sink[l])
        y_rwkv = rwkv7_bidirectional(pr, mu_prev[l], mu_next[l], w0[l], w2[l], a0[l], a2[l], g2[l],
                                     k_k[l], k_a[l], r_k[l], lnx_g[l], lnx_b[l]).astype(h.dtype)
        mix = jnp.concatenate([y_attn, y_rwkv], -1) @ w_out[l]
        h = layer_norm(DEEPNORM_ALPHA * h + mix, ln1_g[l], ln1_b[l])
        f = peer_ffn(h, peer_wq[l], peer_keys[l], peer_u[l], peer_v[l])
        h = layer_norm(DEEPNORM_ALPHA * h + f, ln2_g[l], ln2_b[l])
    return h


_drawn_inputs = setup_inputs


def setup_inputs(seed=0):
    import zlib

    import numpy as np

    out = dict(_drawn_inputs(seed))
    spreads = {}
    factors = {'w2': 5.252,
     'k_k': 4.673,
     'k_a': 2.955,
     'lnx_g': 3.531,
     'lnx_b': 5.66,
     'sink': 8.0,
     'ln2_b': 2.913}
    for name, (base, spread) in spreads.items():
        noise = np.random.default_rng([zlib.crc32(name.encode()), seed]).standard_normal(out[name].shape)
        drawn = base * np.exp(spread * noise) if base else spread * noise
        out[name] = jnp.asarray(drawn.astype(out[name].dtype))
    for name, factor in factors.items():
        out[name] = (out[name] * factor).astype(out[name].dtype)
    return out
```

```python
from contextlib import ExitStack

import numpy as np
import concourse.bass as bass
from concourse import mybir

F32 = mybir.dt.float32
U32 = mybir.dt.uint32
ALU = mybir.AluOpType
ACT = mybir.ActivationFunctionType
AX = mybir.AxisListType
ds = bass.ds

P = 128
SEQ = 1024
D = 1024
KT = D // P
TT = SEQ // P
HD = 64
NH = 8
HP = NH // 2
CH = 64
NC = SEQ // CH
XS = 5
NFT = 14
NAT = 6
WIN = 3 * P
PADDED = SEQ + 2 * P
ALPHA = 2.0 ** 0.25
DECAY = float(np.exp(-0.5))
GN_EPS = 64e-5
LN_EPS = 1e-5
NEG = -1e30
PH = 8
NK = 128
TOPK = 16
NSEL = PH * TOPK
GRP = 8
NG = NSEL // GRP
HALF = 512

W0F, W0B, A0F, A0B, KKS, KA, RK, LNG, LNB, KAC = range(10)
NPAR = 9


def allocator(nc, ctx, prefix=""):
    def sb(name, shape, dtype=F32):
        return ctx.enter_context(nc.sbuf_tensor(prefix + name, list(shape), dtype))
    return sb


def semaphores(nc, ctx, prefix):
    used = []

    def clear():
        with nc.Block() as block:
            @block.gpsimd
            def _(pool):
                for s in used:
                    pool.sem_clear(s)

    def sem(name):
        used.append(ctx.enter_context(nc.semaphore(prefix + name)))
        return used[-1]
    ctx.callback(clear)
    return sem


def project(nc, banks, x_t, w_tiles, xT, groups, tag):
    total = sum(n for _, n in groups)
    with ExitStack() as ctx:
        sb, sem = allocator(nc, ctx, tag), semaphores(nc, ctx, tag)
        w = [sb(f"w{b}", [P, KT, P]) for b in range(2)]
        x_in = [sem(f"x_in{k}") for k in range(2)]
        w_in = [sem(f"w_in{b}") for b in range(2)]
        product = [sem(f"product{h}") for h in range(2)]
        copied = [[sem(f"copied{b}{h}") for h in range(2)] for b in range(2)]
        block = ctx.enter_context(nc.Block())

        @block.sync
        def _(sp):
            for k in range(2):
                sp.dma_start(xT[:, k * 4:k * 4 + 4, :], x_t[:, k * 4:k * 4 + 4, :]).then_inc(x_in[k], 16)
            for b in range(2):
                sp.dma_start(w[b][:], w_tiles[b]).then_inc(w_in[b], 16)
            with sp.Fori(1, total // 2) as j:
                for b in range(2):
                    sp.wait_ge(product[1], 2 * j - 1 + b)
                    sp.dma_start(w[b][:], w_tiles[ds(2 * j + b, 1)].rearrange("o p k c -> p (o k) c")
                                 ).then_inc(w_in[b], 16)

        @block.tensor
        def _(pe):
            for k in range(2):
                pe.wait_ge(x_in[k], 16)
            with pe.Fori(0, total // 2) as j:
                for b in range(2):
                    pe.wait_ge(w_in[b], 16 * j + 16)
                    for h in range(2):
                        pe.wait_ge(copied[b][h], j)
                        bank = banks[2 * b + h]
                        for k in range(KT):
                            last = pe.matmul(bank[:], w[b][:, k, :], xT[:, k, h * HALF:(h + 1) * HALF],
                                             start=(k == 0), stop=(k == KT - 1))
                        last.then_inc(product[h], 1)

        def copies(eng, h, copy):
            done = 0
            for dest, n in groups:
                with eng.Fori(0, n // 2) as j:
                    for b in range(2):
                        eng.wait_ge(product[h], done + 2 * j + b + 1)
                        copy(dest[:, ds((2 * j + b) * SEQ + h * HALF, HALF)],
                             banks[2 * b + h][:]).then_inc(copied[b][h], 1)
                done += n

        @block.scalar
        def _(act):
            copies(act, 0, act.copy)

        @block.vector
        def _(dve):
            copies(dve, 1, dve.tensor_copy)


def attend(nc, banks, at, mixT, consts, rope, masks, sink, perm):
    ident = consts["ident"]
    with ExitStack() as ctx:
        sb, sem = allocator(nc, ctx, "at_"), semaphores(nc, ctx, "at_")
        cosT = sb("cosT", [P, SEQ])
        sinT = sb("sinT", [P, SEQ])
        swap = sb("swap", [P, P])
        mask = sb("mask", [P, TT, WIN])
        snk = sb("snk", [P, NH])
        turned = sb("turned", [P, 2, HALF])
        kP = sb("kP", [P, PADDED])
        vP = sb("vP", [P, TT + 2, P])
        qs = sb("qs", [P, 4, P])
        ks = sb("ks", [P, WIN])
        vs = sb("vs", [P, WIN])
        lg = sb("lg", [P, NH, WIN])
        st = sb("st", [P, 6, NH])
        pT = sb("pT", [P, 2, WIN])
        tables, cleared, apart = sem("tables"), sem("cleared"), sem("apart")
        swapped, dve_step, act_step = sem("swapped"), sem("dve_step"), sem("act_step")
        v_turned, v_copied = sem("v_turned"), sem("v_copied")
        staged, logits, masked = sem("staged"), sem("logits"), sem("masked")
        chain, maxed, expd, probs = sem("chain"), sem("maxed"), sem("expd"), sem("probs")
        turnd, pcopied, out_done, stored = sem("turnd"), sem("pcopied"), sem("out_done"), sem("stored")
        loads = ((cosT, rope[0]), (sinT, rope[1]), (swap, perm), (mask, masks),
                 (snk, sink.partition_broadcast(P)))

        with nc.Block() as block:
            @block.sync
            def _(sp):
                for to, of in loads:
                    sp.dma_start(to[:], of).then_inc(tables, 16)
                sp.wait_ge(tables, 16 * len(loads))

            @block.gpsimd
            def _(pool):
                pool.memset(kP[:], 0.0).then_inc(cleared, 1)
                pool.memset(vP[:], 0.0).then_inc(cleared, 1)

            @block.tensor
            def _(pe):
                pe.wait_ge(tables, 16 * len(loads))
                with pe.Fori(0, 5) as f:
                    for h in range(2):
                        pe.wait_ge(dve_step, 2 * f + h)
                        pe.matmul(banks[h][:], swap[:], at[:, ds(f * SEQ + h * HALF, HALF)],
                                  start=True, stop=True).then_inc(swapped, 1)
                for n in range(TT):
                    if n >= 4:
                        pe.wait_ge(v_copied, n - 3)
                    pe.transpose(banks[4 + n % 4][:, 0:P], at[:, 5 * SEQ + n * P:5 * SEQ + n * P + P],
                                 ident[:]).then_inc(v_turned, 1)

            @block.scalar
            def _(act):
                act.wait_ge(cleared, 2)
                for n in range(TT):
                    act.wait_ge(v_turned, n + 1)
                    act.copy(vP[:, n + 1, :], banks[4 + n % 4][:, 0:P]).then_inc(v_copied, 1)

            @block.vector
            def _(dve):
                dve.wait_ge(tables, 16 * len(loads))
                with dve.Fori(0, 5) as f:
                    for h in range(2):
                        cols = ds(f * SEQ + h * HALF, HALF)
                        dve.wait_ge(swapped, 2 * f + h + 1)
                        dve.tensor_tensor(turned[:, h, :], banks[h][:], sinT[:, h * HALF:(h + 1) * HALF],
                                          ALU.mult).then_inc(dve_step, 1)
                        dve.tensor_tensor(at[:, cols], at[:, cols], cosT[:, h * HALF:(h + 1) * HALF],
                                          ALU.mult).then_inc(chain, 1)
                        dve.wait_ge(chain, 4 * f + 2 * h + 1)
                        dve.wait_ge(dve_step, 2 * f + h + 1)
                        dve.tensor_tensor(at[:, cols], at[:, cols], turned[:, h, :], ALU.add
                                          ).then_inc(chain, 1)
                dve.wait_ge(chain, 20)
                dve.wait_ge(cleared, 2)
                dve.tensor_copy(kP[:, P:P + SEQ], at[:, 4 * SEQ:5 * SEQ]).then_inc(chain, 1)

        dve_n = 4

        with nc.Block() as block:
            @block.gpsimd
            def _(pool):
                with pool.Fori(0, TT) as n:
                    pool.wait_ge(out_done, 4 * n)
                    pool.sem_inc(apart, 1)
                    pool.tensor_copy(qs[:], at[:].rearrange("p (f t) -> p f t", t=SEQ)[:, 0:4, ds(n * P, P)]
                                     ).then_inc(staged, 1)
                    pool.tensor_copy(ks[:], kP[:, ds(n * P, WIN)]).then_inc(staged, 1)
                    pool.tensor_copy(vs[:], vP[:].rearrange("p b c -> p (b c)")[:, ds(n * P, WIN)]
                                     ).then_inc(staged, 1)

            @block.tensor
            def _(pe):
                with pe.Fori(0, TT) as n:
                    pe.wait_ge(staged, 3 * n + 3)
                    for p in range(4):
                        for s in range(2):
                            pe.wait_ge(masked, 8 * n + 2 * p + s - 3 if p >= 2 else 8 * n)
                            pe.matmul(banks[2 * (p % 2) + s][:, 0:WIN], qs[s * HD:(s + 1) * HD, p, :],
                                      ks[s * HD:(s + 1) * HD, :], start=True, stop=True
                                      ).then_inc(logits, 1)
                    for p in range(4):
                        for s in range(2):
                            i = 2 * p + s
                            pe.wait_ge(probs, 8 * n + i + 1)
                            pe.wait_ge(pcopied, 8 * n + i - 1 if i >= 2 else 8 * n)
                            for c in range(3):
                                last = pe.transpose(banks[4 + s][:, c * P:(c + 1) * P],
                                                    lg[:, i, c * P:(c + 1) * P], ident[:])
                            last.then_inc(turnd, 1)
                        for s in range(2):
                            i = 2 * p + s
                            pe.wait_ge(pcopied, 8 * n + i + 1)
                            if s == 0:
                                pe.wait_ge(stored, 4 * n + p - 1 if p >= 2 else 4 * n)
                            for c in range(3):
                                last = pe.matmul(banks[6 + p % 2][s * HD:(s + 1) * HD, 0:P],
                                                 vs[:, c * P + s * HD:c * P + (s + 1) * HD],
                                                 pT[:, s, c * P:(c + 1) * P], start=(c == 0), stop=(c == 2))
                        last.then_inc(out_done, 1)

            @block.vector
            def _(dve):
                with dve.Fori(0, TT) as n:
                    for i in range(NH):
                        p, s = i // 2, i % 2
                        dve.wait_ge(logits, 8 * n + i + 1)
                        dve.wait_ge(turnd, 8 * n)
                        dve.scalar_tensor_tensor(lg[:, i, :], banks[2 * (p % 2) + s][:, 0:WIN],
                                                 HD ** -0.5, mask[:, ds(n, 1), :].rearrange("p a k -> p (a k)"),
                                                 ALU.mult, ALU.add).then_inc(masked, 1)
                    dve.wait_ge(masked, 8 * n + 8)
                    dve.tensor_reduce(st[:, 0, :], lg[:], AX.X, ALU.max).then_inc(chain, 1)
                    dve.wait_ge(chain, 21 + 1 + dve_n * n)
                    dve.tensor_tensor(st[:, 1, :], st[:, 0, :], snk[:], ALU.max).then_inc(chain, 1)
                    dve.wait_ge(chain, 21 + 2 + dve_n * n)
                    dve.tensor_scalar(st[:, 2, :], st[:, 1, :], -1.0, None, ALU.mult).then_inc(maxed, 1)
                    dve.tensor_tensor(st[:, 3, :], snk[:], st[:, 1, :], ALU.subtract).then_inc(maxed, 1)
                    dve.wait_ge(expd, 9 * n + 9)
                    dve.tensor_tensor(st[:, 5, :], st[:, 5, :], st[:, 4, :], ALU.add).then_inc(chain, 1)
                    dve.wait_ge(chain, 21 + 3 + dve_n * n)
                    dve.reciprocal(st[:, 0, :], st[:, 5, :]).then_inc(chain, 1)
                    dve.wait_ge(chain, 21 + 4 + dve_n * n)
                    for i in range(NH):
                        dve.tensor_scalar(lg[:, i, :], lg[:, i, :], st[:, 0, i:i + 1], None, ALU.mult
                                          ).then_inc(probs, 1)
                    for p in range(4):
                        dve.wait_ge(out_done, 4 * n + p + 1)
                        dve.tensor_copy(mixT[:, p, :][:, ds(n * P, P)], banks[6 + p % 2][:, 0:P]
                                        ).then_inc(stored, 1)

            @block.scalar
            def _(act):
                with act.Fori(0, TT) as n:
                    act.wait_ge(maxed, 2 * n + 2)
                    act.activation(st[:, 4, :], st[:, 3, :], ACT.Exp).then_inc(expd, 1)
                    for i in range(NH):
                        act.activation(lg[:, i, :], lg[:, i, :], ACT.Exp, bias=st[:, 2, i:i + 1],
                                       accum_out=st[:, 5, i:i + 1]).then_inc(expd, 1)
                    for i in range(NH):
                        act.wait_ge(turnd, 8 * n + i + 1)
                        act.wait_ge(out_done, 4 * n + i // 2)
                        act.copy(pT[:, i % 2, :], banks[4 + i % 2][:, 0:WIN]).then_inc(pcopied, 1)


def shift_tokens(nc, feat, mu):
    with ExitStack() as ctx:
        sb, sem = allocator(nc, ctx, "sh_"), semaphores(nc, ctx, "sh_")
        part = sb("part", [P, 3, NFT])
        mu_in, links, shifted, bent = sem("mu_in"), sem("links"), sem("shifted"), sem("bent")
        block = ctx.enter_context(nc.Block())
        mp, mn, m0 = (part[:, i, :] for i in range(3))

        @block.sync
        def _(sp):
            for i in range(2):
                sp.dma_start(part[:, i, :], mu[i]).then_inc(mu_in, 16)
            sp.wait_ge(mu_in, 32)

        @block.vector
        def _(dve):
            dve.wait_ge(mu_in, 32)
            dve.tensor_tensor(m0, mp, mn, ALU.add).then_inc(links, 1)
            dve.wait_ge(links, 1)
            dve.tensor_scalar(m0, m0, -1.0, 1.0, ALU.mult, ALU.add).then_inc(links, 1)
            dve.wait_ge(links, 2)
            with dve.Fori(0, NFT) as f:
                def new(a, n):
                    return feat[:, ds(f * SEQ + a, n)]

                def old(a, n):
                    return feat[:, ds(f * SEQ + SEQ + a, n)]
                dve.tensor_scalar(new(0, SEQ), old(0, SEQ), m0[:, ds(f, 1)], None, ALU.mult).then_inc(links, 1)
                dve.wait_ge(links, 2 * f + 3)
                dve.scalar_tensor_tensor(new(1, SEQ - 1), old(0, SEQ - 1), mp[:, ds(f, 1)],
                                         new(1, SEQ - 1), ALU.mult, ALU.add).then_inc(links, 1)
                dve.wait_ge(links, 2 * f + 4)
                dve.scalar_tensor_tensor(new(0, SEQ - 1), old(1, SEQ - 1), mn[:, ds(f, 1)],
                                         new(0, SEQ - 1), ALU.mult, ALU.add).then_inc(shifted, 1)
                dve.wait_ge(shifted, f + 1)

        @block.scalar
        def _(act):
            act.wait_ge(shifted, NFT)
            wd = feat[0:2 * 32, 12 * SEQ:13 * SEQ]
            gd = feat[:, 13 * SEQ:14 * SEQ]
            act.activation(wd, wd, ACT.Tanh).then_inc(bent, 1)
            act.activation(gd, gd, ACT.Sigmoid).then_inc(bent, 1)


def prepare_chunks(nc, ps, feat, consts, low_rank, params, chunks, gates):
    ones = consts["ones"]
    with ExitStack() as ctx:
        sb, sem = allocator(nc, ctx, "pc_"), semaphores(nc, ctx, "pc_")
        lr = sb("lr", [P, 5, P])
        par_all = sb("par_all", [P, HP, NPAR])
        par = sb("par", [P, NPAR + 1])
        reset = sb("reset", [P, SEQ])
        sg = [sb(f"sg{d}", [P, SEQ]) for d in range(2)]
        a = [sb(f"a{d}", [P, SEQ]) for d in range(2)]
        kd = [sb(f"kd{d}", [P, SEQ]) for d in range(2)]
        kk = sb("kk", [P, SEQ])
        nrm = sb("nrm", [P, SEQ])
        cs = sb("cs", [P, SEQ])
        X = sb("X", [P, SEQ])
        Y = sb("Y", [P, SEQ])
        E = sb("E", [P, SEQ])
        half = sb("half", [P, NC])
        nxt = sb("nxt", [P, 2, NC])
        st = [sb(f"st{d}", [P, NC, XS, CH]) for d in range(2)]
        names = ("par_in lr_in scans_ready ranks keyed squared summed rooted links xy exps gate_in "
                 "gated staged_v written sigs floored bonus_in bonus_sum bonus_out g_prod g_out")
        (par_in, lr_in, scans_ready, ranks, keyed, squared, summed, rooted, links, xy, exps, gate_in,
         gated, staged_v, written, sigs, floored, bonus_in, bonus_sum, bonus_out, g_prod,
         g_out) = (sem(n) for n in names.split())
        apart = sem("apart")
        staged = [sem(f"staged{d}") for d in range(2)]
        stored = [sem(f"stored{d}") for d in range(2)]
        block = ctx.enter_context(nc.Block())
        slots = feat[:].rearrange("p (f t) -> p f t", t=SEQ)

        def slot(f, hp):
            return feat[:, ds((f + hp) * SEQ, SEQ)]

        def by_chunk(t):
            return t[:].rearrange("p (c t) -> p c t", t=CH)

        @block.sync
        def _(sp):
            sp.dma_start(par_all[:], params).then_inc(par_in, 16)
            with sp.Fori(0, HP) as hp:
                sp.wait_ge(g_prod, hp)
                sp.sem_inc(apart, 1)
                sp.dma_start(lr[:], low_rank[ds(hp, 1)].rearrange("o p x c -> p (o x) c")).then_inc(lr_in, 16)
                for d in range(2):
                    sp.wait_ge(staged[d], 4 * hp + 4)
                    sp.sem_inc(apart, 1)
                    sp.wait_ge(staged_v, 2 * hp + d + 1)
                    sp.sem_inc(apart, 1)
                    for c in range(0, NC, 8):
                        sp.dma_start(chunks[d, c:c + 8, :, ds(hp * XS * CH, XS * CH)].rearrange("c p n -> p c n"),
                                     st[d][:, c:c + 8].rearrange("p c x t -> p c (x t)")).then_inc(stored[d], 16)
            for d in range(2):
                sp.wait_ge(stored[d], 2 * 16 * HP)

        @block.tensor
        def _(pe):
            with pe.Fori(0, HP) as hp:
                pe.wait_ge(lr_in, 16 * hp + 16)
                pe.wait_ge(g_out, hp)
                pe.wait_ge(bonus_out, hp)
                pe.wait_ge(floored, hp)
                for x in range(4):
                    for h in range(2):
                        last = pe.matmul(ps[:, (2 * x + h) * HALF:(2 * x + h + 1) * HALF], lr[:, x, :],
                                         feat[:, 12 * SEQ + h * HALF:12 * SEQ + (h + 1) * HALF],
                                         start=True, stop=True)
                    last.then_inc(ranks, 1)
                pe.wait_ge(squared, hp + 1)
                pe.wait_ge(sigs, 4 * hp + 4)
                for h in range(2):
                    last = pe.matmul(ps[:, h * HALF:(h + 1) * HALF], ones[:], nrm[:, h * HALF:(h + 1) * HALF],
                                     start=True, stop=True)
                last.then_inc(summed, 1)
                for h in range(2):
                    last = pe.matmul(ps[:, (4 + h) * HALF:(5 + h) * HALF], lr[:, 4, :],
                                     feat[:, 13 * SEQ + h * HALF:13 * SEQ + (h + 1) * HALF],
                                     start=True, stop=True)
                last.then_inc(g_prod, 1)
                pe.wait_ge(bonus_in, hp + 1)
                for h in range(2):
                    last = pe.matmul(ps[:, (2 + h) * HALF:(3 + h) * HALF], ones[:], X[:, h * HALF:(h + 1) * HALF],
                                     start=True, stop=True)
                last.then_inc(bonus_sum, 1)

        @block.gpsimd
        def _(pool):
            pool.memset(reset[:], 1.0).then_inc(scans_ready, 1)
            pool.wait_ge(scans_ready, 1)
            pool.memset(by_chunk(reset)[:, :, 0:1], 0.0).then_inc(scans_ready, 1)
            with pool.Fori(0, HP) as hp:
                for d in range(2):
                    pool.wait_ge(stored[d], 32 * hp)
                    pool.sem_inc(apart, 1)
                    pool.tensor_copy(st[d][:, :, 4, :],
                                     slot(8, hp).rearrange("p (c t) -> p c t", t=CH)).then_inc(staged_v, 1)

        @block.scalar
        def _(act):
            with act.Fori(0, HP) as hp:
                act.wait_ge(written, hp + 1)
                for x, (to, col) in enumerate(((sg[0], W0F), (sg[1], W0B), (a[0], A0F), (a[1], A0B))):
                    act.wait_ge(ranks, 4 * hp + x + 1)
                    act.activation(to[:], ps[:, 2 * x * HALF:(2 * x + 2) * HALF], ACT.Sigmoid,
                                   bias=par[:, col:col + 1]).then_inc(sigs, 1)
                act.wait_ge(keyed, hp + 1)
                act.activation(nrm[:], kk[:], ACT.Square).then_inc(squared, 1)
                act.wait_ge(floored, hp + 1)
                act.activation(nrm[:], nrm[:], ACT.Sqrt).then_inc(rooted, 1)
                for d in range(2):
                    act.wait_ge(gate_in, 2 * hp + d + 1)
                    act.activation(gates[:, d, ds(hp, 1), :].rearrange("p a c -> p (a c)"), nxt[:, d, :],
                                   ACT.Exp, scale=-DECAY).then_inc(gated, 1)
                    act.wait_ge(xy, 2 * hp + d + 1)
                    if d == 0:
                        act.activation(E[:], X[:], ACT.Exp, scale=DECAY).then_inc(exps, 1)
                        act.wait_ge(exps, 6 * hp + 1)
                        act.activation(X[:], X[:], ACT.Exp, scale=-DECAY).then_inc(exps, 1)
                        act.activation(Y[:], Y[:], ACT.Exp, scale=-DECAY).then_inc(exps, 1)
                    else:
                        act.activation(E[:], Y[:], ACT.Exp, scale=-DECAY).then_inc(exps, 1)
                        act.wait_ge(exps, 6 * hp + 4)
                        act.activation(Y[:], Y[:], ACT.Exp, scale=DECAY).then_inc(exps, 1)
                        act.activation(X[:], X[:], ACT.Exp, scale=DECAY).then_inc(exps, 1)
                act.wait_ge(g_prod, hp + 1)
                act.wait_ge(bonus_in, hp + 1)
                act.copy(slot(0, hp), ps[:, 4 * HALF:6 * HALF]).then_inc(g_out, 1)

        @block.vector
        def _(dve):
            per_pair = 16
            n = [0]
            dve.wait_ge(par_in, 16)
            dve.wait_ge(scans_ready, 2)
            with dve.Fori(0, HP) as hp:
                def link(ins):
                    n[0] += 1
                    ins.then_inc(links, 1)
                    dve.wait_ge(links, hp * per_pair + n[0])

                k, r, v = slot(4, hp), slot(0, hp), slot(8, hp)
                dve.wait_ge(bonus_out, hp)
                link(dve.tensor_copy(par[:, 0:NPAR], par_all[:, ds(hp, 1), :].rearrange("p a c -> p (a c)")))
                dve.tensor_scalar(par[:, KAC:KAC + 1], par[:, KA:KA + 1], -1.0, 1.0, ALU.mult, ALU.add
                                  ).then_inc(written, 1)
                dve.wait_ge(written, hp + 1)
                dve.tensor_scalar(kk[:], k, par[:, KKS:KKS + 1], None, ALU.mult).then_inc(keyed, 1)
                dve.wait_ge(summed, hp + 1)
                dve.tensor_scalar(nrm[:], ps[:, 0:2 * HALF], 1e-24, None, ALU.max).then_inc(floored, 1)
                dve.wait_ge(rooted, hp + 1)
                link(dve.reciprocal(nrm[:], nrm[:]))
                link(dve.tensor_tensor(kk[:], kk[:], nrm[:], ALU.mult))
                for d in range(2):
                    dve.wait_ge(sigs, 4 * hp + 4)
                    link(dve.tensor_tensor_scan(cs[:], reset[:], sg[d][:], 0.0, ALU.mult, ALU.add))
                    link(dve.tensor_scalar(half[:], by_chunk(cs)[:, :, CH - 1], 0.5, None, ALU.mult))
                    dve.wait_ge(gated, 2 * hp + d)
                    a0, b0 = (0, 1) if d == 0 else (1, 0)
                    dve.tensor_tensor(nxt[:, d, a0:a0 + NC - 1], half[:, 0:NC - 1], half[:, 1:NC], ALU.add)
                    edge = NC - 1 if d == 0 else 0
                    dve.tensor_copy(nxt[:, d, edge:edge + 1], half[:, edge:edge + 1]).then_inc(gate_in, 1)
                    link(dve.tensor_tensor(by_chunk(X), by_chunk(cs),
                                           half[:].unsqueeze(2).broadcast_to([P, NC, CH]), ALU.subtract))
                    dve.tensor_tensor(Y[:], X[:], sg[d][:], ALU.subtract).then_inc(xy, 1)
                    link(dve.tensor_scalar(kd[d][:], a[d][:], par[:, KA:KA + 1], par[:, KAC:KAC + 1],
                                           ALU.mult, ALU.add))
                    link(dve.tensor_tensor(kd[d][:], kd[d][:], k, ALU.mult))
                    link(dve.tensor_tensor(a[d][:], a[d][:], kk[:], ALU.mult))
                    eA, eR = (Y, X) if d == 0 else (X, Y)
                    dve.wait_ge(exps, 6 * hp + 3 * d + 3)
                    dve.wait_ge(stored[d], 32 * hp)
                    dve.scalar_tensor_tensor(st[d][:, :, 1, :], by_chunk(kk), -1.0, by_chunk(eA),
                                             ALU.mult, ALU.mult).then_inc(staged[d], 1)
                    dve.tensor_tensor(st[d][:, :, 0, :], r.rearrange("p (c t) -> p c t", t=CH), by_chunk(eR),
                                      ALU.mult).then_inc(staged[d], 1)
                    dve.tensor_tensor(st[d][:, :, 2, :], by_chunk(a[d]), by_chunk(E), ALU.mult
                                      ).then_inc(staged[d], 1)
                    dve.tensor_tensor(st[d][:, :, 3, :], by_chunk(kd[d]), by_chunk(E), ALU.mult
                                      ).then_inc(staged[d], 1)
                    dve.wait_ge(staged[d], 4 * hp + 4)
                link(dve.tensor_tensor(kd[0][:], kd[0][:], kd[1][:], ALU.add))
                dve.scalar_tensor_tensor(X[:], kd[0][:], par[:, RK:RK + 1], r, ALU.mult, ALU.mult
                                         ).then_inc(bonus_in, 1)
                dve.wait_ge(bonus_sum, hp + 1)
                dve.wait_ge(staged_v, 2 * hp + 2)
                dve.scalar_tensor_tensor(v, ps[:, 2 * HALF:4 * HALF], 0.5, v, ALU.mult, ALU.mult
                                         ).then_inc(bonus_out, 1)
            assert n[0] == per_pair


def run_chunks(nc, ps, feat, consts, chunks, gates, tri, tri_l):
    ident = consts["ident"]
    G = 2 * HP
    W = G * CH
    LEVELS = 5
    with ExitStack() as ctx:
        sb, sem = allocator(nc, ctx, "rc_"), semaphores(nc, ctx, "rc_")
        stk = [sb(f"stk{b}", [P, G, 3, CH]) for b in range(2)]
        dia = [sb(f"dia{b}", [P, G, 4, P]) for b in range(2)]
        tri_s = sb("tri_s", [P, 2, 2, CH])
        tril_s = sb("tril_s", [P, 2, CH])
        eye = sb("eye", [P, CH])

        def stacked(name):
            return sb(name, [P, G, CH])

        def diagonal(name):
            return sb(name, [P, G, P])
        nt_s, l_s, x_s, rb_s, rk_s, v_s, z_s, u_s, s_s = (
            stacked(n) for n in ("nt_s", "l_s", "x_s", "rb_s", "rk_s", "v_s", "z_s", "u_s", "s_s"))
        nt_d, l_d, mt_d, b_d, k_d, v_d, u_d, s_d = (
            diagonal(n) for n in ("nt_d", "l_d", "mt_d", "b_d", "k_d", "v_d", "u_d", "s_d"))
        x_d = nt_d
        gs = sb("gs", [P, G])
        names = ("consts_in cleared made seeded masked v_ready turned natural squares l_dia nt_ready "
                 "l_stk xprod xadded z_made z_copied u_made u_copied u_dia y_made y_copied "
                 "gs_ready scaled state x_ready")
        (consts_in, cleared, made, seeded, masked, v_ready, turned, natural, squares, l_dia, nt_ready,
         l_stk, xprod, xadded, z_made, z_copied, u_made, u_copied, u_dia, y_made, y_copied,
         gs_ready, scaled, state, x_ready) = (sem(n) for n in names.split())
        loaded = [sem(f"loaded{b}") for b in range(2)]
        s_made = [sem(f"s_made{b}") for b in range(2)]
        block = ctx.enter_context(nc.Block())

        def bank(n, k=1):
            return ps[:, n * HALF:(n + k) * HALF]

        def pairs(ap, w=CH):
            return ap.rearrange("p (g c) -> p g c", c=w)

        def blocks(ap, s):
            rows = ap[s * HD:(s + 1) * HD]
            return rows if ap.shape[2] == CH else rows[:, :, s * CH:(s + 1) * CH]

        @block.sync
        def _(sp):
            for to, of in ((tri_s, tri), (tril_s, tri_l), (eye, consts["eye"])):
                sp.dma_start(to[:], of).then_inc(consts_in, 16)
            sp.wait_ge(cleared, 1)
            with sp.Fori(0, NC // 2) as j:
                for b in range(2):
                    sp.wait_ge(s_made[b], j)
                    for d in range(2):
                        c = 2 * j + b if d == 0 else NC - 1 - b - 2 * j
                        of = chunks[d, ds(c, 1)].rearrange("o p (h x t) -> p (o h) x t", x=XS, t=CH)
                        pr = slice(d * HP, (d + 1) * HP)
                        sp.dma_start(stk[b][:, pr], of[:, :, 0:3]).then_inc(loaded[b], 16)
                        for s in range(2):
                            for h in range(HP):
                                sp.dma_start(dia[b][s * HD:(s + 1) * HD, d * HP + h, :, s * CH:(s + 1) * CH],
                                             of[s * HD:(s + 1) * HD, h, 1:5]).then_inc(loaded[b], 16)

        loads = 16 * 2 * (1 + 2 * HP)

        @block.gpsimd
        def _(pool):
            for t in (nt_d, l_d, mt_d, u_d, s_d):
                pool.memset(t[:], 0.0)
            pool.memset(s_s[:], 0.0)
            for b in range(2):
                last = pool.memset(dia[b][:], 0.0)
            last.then_inc(cleared, 1)

        @block.tensor
        def _(pe):
            pe.wait_ge(cleared, 1)
            with pe.Fori(0, NC // 2) as j:
                for b in range(2):
                    i = 2 * j + b
                    S, Dg = stk[b], dia[b]
                    pe.wait_ge(loaded[b], loads * j + loads)
                    pe.wait_ge(y_copied, i)
                    pe.wait_ge(state, i)
                    for g in range(G):
                        last = pe.matmul(ps[:, g * P:(g + 1) * P], Dg[:, g, 1, :], S[:, g, 0:2, :],
                                         start=True, stop=True)
                    last.then_inc(made, 1)
                    for g in range(G):
                        last = pe.matmul(ps[:, 4 * HALF + g * CH:4 * HALF + (g + 1) * CH], Dg[:, g, 0, :],
                                         S[:, g, 2, :], start=True, stop=True)
                    last.then_inc(made, 1)
                    for g in range(G):
                        last = pe.matmul(ps[:, 2 * HALF + g * P:2 * HALF + (g + 1) * P], Dg[:, g, 2, :],
                                         S[:, g, 0:2, :], start=True, stop=True)
                    last.then_inc(made, 1)
                    for g in range(G):
                        last = pe.transpose(ps[:, 5 * HALF + g * P:5 * HALF + (g + 1) * P], Dg[:, g, 3, :], ident[:])
                    last.then_inc(made, 1)
                    pe.wait_ge(masked, i + 1)
                    for g in range(G):
                        last = pe.transpose(ps[:, 2 * HALF + g * P:2 * HALF + (g + 1) * P], Dg[:, g, 1, :], ident[:])
                    last.then_inc(turned, 1)
                    pe.wait_ge(v_ready, i + 1)
                    for g in range(G):
                        last = pe.transpose(ps[:, 5 * HALF + g * P:5 * HALF + (g + 1) * P], Dg[:, g, 2, :], ident[:])
                    last.then_inc(turned, 1)
                    for k in range(LEVELS + 1):
                        if k == 0:
                            pe.wait_ge(seeded, i + 1)
                        else:
                            pe.wait_ge(l_dia, LEVELS * i + k)
                            pe.wait_ge(xadded, LEVELS * i + k)
                            for g in range(G):
                                last = pe.matmul(ps[:, 4 * HALF + g * CH:4 * HALF + (g + 1) * CH], l_d[:, g, :],
                                                 x_s[:, g, :], start=True, stop=True)
                            last.then_inc(xprod, 1)
                        if k == LEVELS:
                            continue
                        if k:
                            pe.wait_ge(nt_ready, 4 * i + k)
                            pe.wait_ge(l_stk, 4 * i + k)
                        for g in range(G):
                            last = pe.matmul(ps[:, HALF + g * CH:HALF + (g + 1) * CH], nt_d[:, g, :],
                                             l_s[:, g, :], start=True, stop=True)
                        if k < LEVELS - 1:
                            for g in range(G):
                                last = pe.matmul(ps[:, g * CH:(g + 1) * CH], l_d[:, g, :],
                                                 nt_s[:, g, :], start=True, stop=True)
                        last.then_inc(squares, 1)
                    for g in range(G):
                        o = ps[:, g * CH:(g + 1) * CH]
                        pe.matmul(o, mt_d[:, g, :], v_s[:, g, :], start=True, stop=False)
                        last = pe.matmul(o, Dg[:, g, 0, :], s_s[:, g, :], start=False, stop=True)
                    last.then_inc(z_made, 1)
                    pe.wait_ge(z_copied, i + 1)
                    pe.wait_ge(x_ready, i + 1)
                    for g in range(G):
                        last = pe.matmul(ps[:, HALF + g * CH:HALF + (g + 1) * CH], x_d[:, g, :], z_s[:, g, :],
                                         start=True, stop=True)
                    last.then_inc(u_made, 1)
                    pe.wait_ge(natural, 2 * i + 2)
                    pe.wait_ge(u_dia, i + 1)
                    for g in range(G):
                        o = ps[:, 2 * HALF + g * CH:2 * HALF + (g + 1) * CH]
                        pe.matmul(o, s_d[:, g, :], S[:, g, 0, :], start=True, stop=False)
                        pe.matmul(o, v_d[:, g, :], rk_s[:, g, :], start=False, stop=False)
                        last = pe.matmul(o, u_d[:, g, :], rb_s[:, g, :], start=False, stop=True)
                    last.then_inc(y_made, 1)
                    pe.wait_ge(u_copied, i + 1)
                    for g in range(G):
                        o = ps[:, 3 * HALF + g * CH:3 * HALF + (g + 1) * CH]
                        pe.matmul(o, ident[:], s_s[:, g, :], start=True, stop=False)
                        pe.matmul(o, k_d[:, g, :], v_s[:, g, :], start=False, stop=False)
                        last = pe.matmul(o, b_d[:, g, :], u_s[:, g, :], start=False, stop=True)
                    last.then_inc(s_made[b], 1)

        @block.vector
        def _(dve):
            dve.wait_ge(consts_in, 48)
            dve.wait_ge(cleared, 1)
            with dve.Fori(0, NC // 2) as j:
                for b in range(2):
                    i = 2 * j + b

                    def tri_of(rows, x):
                        return tri_s[rows, :, x, :].unsqueeze(2).broadcast_to([rows.stop - rows.start, 2, HP, CH])

                    def by_dir(ap):
                        return ap.rearrange("p (d h) c -> p d h c", d=2)

                    def part(base, x):
                        return bank(base, 2).rearrange("p (d h x c) -> p d h x c", d=2, x=2, c=CH)[:, :, :, x, :]
                    every = slice(0, P)
                    dve.wait_ge(made, 4 * i + 1)
                    dve.tensor_tensor(by_dir(nt_s[:]), part(0, 1), tri_of(every, 1), ALU.mult).then_inc(scaled, 1)
                    dve.tensor_tensor(by_dir(rb_s[:]), part(0, 0), tri_of(every, 0), ALU.mult)
                    dve.wait_ge(made, 4 * i + 2)
                    for s in range(2):
                        rows = slice(s * HD, (s + 1) * HD)
                        lm = tril_s[rows].unsqueeze(2).broadcast_to([HD, 2, HP, CH])
                        dve.tensor_tensor(by_dir(blocks(l_d, s)), by_dir(pairs(bank(4)))[rows], lm, ALU.mult)
                    dve.tensor_tensor(by_dir(l_s[:]), by_dir(pairs(bank(4))),
                                      tril_s[:].unsqueeze(2).broadcast_to([P, 2, HP, CH]), ALU.mult)
                    dve.wait_ge(scaled, 2 * i + 1)
                    for s in range(2):
                        last = dve.tensor_copy(blocks(nt_d, s), blocks(nt_s, s))
                    last.then_inc(seeded, 1)
                    dve.tensor_tensor(x_s[:], nt_s[:], eye[:].unsqueeze(1).broadcast_to([P, G, CH]), ALU.add
                                      ).then_inc(xadded, 1)
                    dve.wait_ge(made, 4 * i + 3)
                    for s in range(2):
                        rows = slice(s * HD, (s + 1) * HD)
                        dve.tensor_tensor(by_dir(blocks(mt_d, s)), part(2, 1)[rows], tri_of(rows, 1), ALU.mult)
                    dve.tensor_tensor(by_dir(rk_s[:]), part(2, 0), tri_of(every, 0), ALU.mult).then_inc(masked, 1)
                    for k in range(1, LEVELS + 1):
                        if k < LEVELS:
                            dve.wait_ge(squares, LEVELS * i + k)
                            if k < LEVELS - 1:
                                dve.tensor_copy(nt_s[:], pairs(bank(0)))
                            for s in range(2):
                                last = dve.tensor_copy(blocks(nt_d, s), pairs(bank(0))[s * HD:(s + 1) * HD])
                            last.then_inc(nt_ready, 1)
                        dve.wait_ge(xprod, LEVELS * i + k)
                        dve.wait_ge(xadded, LEVELS * i + k)
                        if k < LEVELS:
                            dve.tensor_tensor(x_s[:], x_s[:], pairs(bank(4)), ALU.add).then_inc(xadded, 1)
                        else:
                            for s in range(2):
                                last = dve.tensor_tensor(blocks(x_d, s), blocks(x_s, s),
                                                         pairs(bank(4))[s * HD:(s + 1) * HD], ALU.add)
                            last.then_inc(x_ready, 1)
                    dve.wait_ge(z_made, i + 1)
                    dve.tensor_copy(z_s[:], pairs(bank(0))).then_inc(z_copied, 1)
                    dve.tensor_copy(gs[:, 0:HP].unsqueeze(2), gates[:, 0, :, ds(i, 1)]).then_inc(gs_ready, 1)
                    dve.tensor_copy(gs[:, HP:G].unsqueeze(2), gates[:, 1, :, ds(NC - 1 - b - 2 * j, 1)]
                                    ).then_inc(gs_ready, 1)
                    dve.wait_ge(s_made[b], j + 1)
                    dve.wait_ge(gs_ready, 2 * i + 2)
                    dve.tensor_tensor(s_s[:], pairs(bank(3)), gs[:].unsqueeze(2).broadcast_to([P, G, CH]),
                                      ALU.mult).then_inc(scaled, 1)
                    dve.wait_ge(scaled, 2 * i + 2)
                    for s in range(2):
                        last = dve.tensor_copy(blocks(s_d, s), blocks(s_s, s))
                    last.then_inc(state, 1)

        @block.scalar
        def _(act):
            with act.Fori(0, NC // 2) as j:
                for b in range(2):
                    i = 2 * j + b
                    act.wait_ge(made, 4 * i + 4)
                    act.copy(v_d[:], pairs(bank(5, 2), P))
                    for s in range(2):
                        last = act.copy(blocks(v_s, s), pairs(bank(5, 2), P)[s * HD:(s + 1) * HD, :, s * CH:(s + 1) * CH])
                    last.then_inc(v_ready, 1)
                    act.wait_ge(turned, 2 * i + 1)
                    act.copy(b_d[:], pairs(bank(2, 2), P)).then_inc(natural, 1)
                    act.wait_ge(turned, 2 * i + 2)
                    act.copy(k_d[:], pairs(bank(5, 2), P)).then_inc(natural, 1)
                    for k in range(1, LEVELS + 1):
                        act.wait_ge(squares, LEVELS * i + k)
                        if k > 1:
                            act.wait_ge(xprod, LEVELS * i + k - 1)
                        for s in range(2):
                            last = act.copy(blocks(l_d, s), pairs(bank(1))[s * HD:(s + 1) * HD])
                        last.then_inc(l_dia, 1)
                        if k < LEVELS:
                            act.copy(l_s[:], pairs(bank(1))).then_inc(l_stk, 1)
                    act.wait_ge(u_made, i + 1)
                    for s in range(2):
                        last = act.copy(blocks(u_d, s), pairs(bank(1))[s * HD:(s + 1) * HD])
                    last.then_inc(u_dia, 1)
                    act.copy(u_s[:], pairs(bank(1))).then_inc(u_copied, 1)
                    act.wait_ge(y_made, i + 1)
                    slots = feat[:].rearrange("p (f t) -> p f t", t=SEQ)
                    act.copy(slots[:, 4:8, ds(i * CH, CH)], pairs(bank(2))[:, 0:HP])
                    act.copy(slots[:, 12:16, ds((NC - 1 - b - 2 * j) * CH, CH)], pairs(bank(2))[:, HP:G]
                             ).then_inc(y_copied, 1)


def finish_rwkv(nc, ps, feat, mixT, consts, params):
    ones = consts["ones"]
    with ExitStack() as ctx:
        sb, sem = allocator(nc, ctx, "fr_"), semaphores(nc, ctx, "fr_")
        par_all = sb("par_all", [P, HP, NPAR])
        par = sb("par", [P, NPAR])
        y = sb("y", [P, SEQ])
        sq = sb("sq", [P, SEQ])
        names = "par_in links added mean_made centred squared var_made floored rooted"
        (par_in, links, added, mean_made, centred, squared, var_made, floored,
         rooted) = (sem(n) for n in names.split())
        block = ctx.enter_context(nc.Block())

        def slot(f, hp):
            return feat[:, ds((f + hp) * SEQ, SEQ)]

        @block.sync
        def _(sp):
            sp.dma_start(par_all[:], params).then_inc(par_in, 16)
            sp.wait_ge(par_in, 16)

        def head_sums(pe, base, of, done):
            for h in range(2):
                last = pe.matmul(ps[:, (base + h) * HALF:(base + h + 1) * HALF], ones[:],
                                 of[:, h * HALF:(h + 1) * HALF], start=True, stop=True)
            last.then_inc(done, 1)

        @block.tensor
        def _(pe):
            with pe.Fori(0, HP) as hp:
                pe.wait_ge(added, hp + 1)
                head_sums(pe, 0, y, mean_made)
                pe.wait_ge(squared, hp + 1)
                head_sums(pe, 2, sq, var_made)

        @block.scalar
        def _(act):
            with act.Fori(0, HP) as hp:
                act.wait_ge(centred, hp + 1)
                act.activation(sq[:], y[:], ACT.Square).then_inc(squared, 1)
                act.wait_ge(floored, hp + 1)
                act.activation(sq[:], sq[:], ACT.Sqrt).then_inc(rooted, 1)

        @block.vector
        def _(dve):
            per_pair = 6
            dve.wait_ge(par_in, 16)
            with dve.Fori(0, HP) as hp:
                n = [0]

                def link(ins):
                    n[0] += 1
                    ins.then_inc(links, 1)
                    dve.wait_ge(links, hp * per_pair + n[0])

                link(dve.tensor_copy(par[:], par_all[:, ds(hp, 1), :].rearrange("p a c -> p (a c)")))
                dve.tensor_tensor(y[:], slot(4, hp), slot(12, hp), ALU.add).then_inc(added, 1)
                dve.wait_ge(mean_made, hp + 1)
                dve.wait_ge(added, hp + 1)
                dve.scalar_tensor_tensor(y[:], ps[:, 0:2 * HALF], -1.0 / HD, y[:], ALU.mult, ALU.add
                                         ).then_inc(centred, 1)
                dve.wait_ge(var_made, hp + 1)
                dve.tensor_scalar(sq[:], ps[:, 2 * HALF:4 * HALF], 1.0 / HD, GN_EPS, ALU.mult, ALU.add
                                  ).then_inc(floored, 1)
                dve.wait_ge(rooted, hp + 1)
                link(dve.reciprocal(sq[:], sq[:]))
                link(dve.tensor_tensor(y[:], y[:], sq[:], ALU.mult))
                link(dve.tensor_scalar(y[:], y[:], par[:, LNG:LNG + 1], par[:, LNB:LNB + 1], ALU.mult, ALU.add))
                link(dve.tensor_tensor(y[:], y[:], slot(8, hp), ALU.add))
                link(dve.tensor_tensor(mixT[:].rearrange("p k t -> p (k t)")[:, ds((4 + hp) * SEQ, SEQ)],
                                       y[:], slot(0, hp), ALU.mult))
                assert n[0] == per_pair


class Norm:

    def __init__(self, sb, sem, name, apart):
        self.parts = sb(name + "_parts", [P, 2, 6])
        self.stat = sb(name + "_stat", [P, 4])
        self.summed, self.rooted = sem(name + "_summed"), sem(name + "_rooted")
        self.apart = apart

    def on_vector(self, dve, link, t, g, b, count):
        for h in range(2):
            last = dve.bn_stats(self.parts[:, h, :], t[:, h * HALF:(h + 1) * HALF])
        link(last)
        dve.sem_inc(self.apart, 1)
        link(dve.bn_aggr(self.stat[:, 0:2], self.parts[:]))
        dve.tensor_scalar(self.stat[:, 2:3], self.stat[:, 1:2], LN_EPS, None, ALU.add).then_inc(self.summed, 1)
        dve.wait_ge(self.rooted, count + 1)
        link(dve.reciprocal(self.stat[:, 2:3], self.stat[:, 3:4]))
        link(dve.tensor_scalar(t[:], t[:], self.stat[:, 0:1], self.stat[:, 2:3], ALU.subtract, ALU.mult))
        link(dve.tensor_tensor(t[:], t[:], g[:], ALU.mult))
        return dve.tensor_tensor(t[:], t[:], b[:], ALU.add)

    LINKS = 5

    def on_scalar(self, act, count):
        act.wait_ge(self.summed, count + 1)
        act.activation(self.stat[:, 3:4], self.stat[:, 2:3], ACT.Sqrt).then_inc(self.rooted, 1)


def mix_and_norm(nc, ps, mixT, h, consts, x, w_out, ln):
    ident = consts["ident"]
    with ExitStack() as ctx:
        sb, sem = allocator(nc, ctx, "mx_"), semaphores(nc, ctx, "mx_")
        w = sb("w", [P, KT, D])
        lhs = sb("lhs", [P, KT, P])
        xt = [sb(f"xt{b}", [P, D]) for b in range(2)]
        t = sb("t", [P, D])
        g_b = [sb(n, [P, D]) for n in ("g", "b")]
        w_in, ln_in, staged, product, links = (sem(n) for n in ("w_in", "ln_in", "staged", "product", "links"))
        summed, normed, turned, kept = (sem(n) for n in ("summed", "normed", "turned", "kept"))
        x_in = [sem(f"x_in{b}") for b in range(2)]
        apart = sem("apart")
        norm = Norm(sb, sem, "ln", apart)
        block = ctx.enter_context(nc.Block())

        @block.sync
        def _(sp):
            sp.dma_start(w[:], w_out).then_inc(w_in, 16)
            for i in range(2):
                sp.dma_start(g_b[i][:], ln[i].partition_broadcast(P)).then_inc(ln_in, 16)
            with sp.Fori(0, TT // 2) as j:
                for b in range(2):
                    sp.wait_ge(summed, 2 * j)
                    sp.dma_start(xt[b][:], x[ds((2 * j + b) * P, P), :]).then_inc(x_in[b], 16)

        @block.gpsimd
        def _(pool):
            with pool.Fori(0, TT) as i:
                pool.wait_ge(product, i)
                pool.sem_inc(apart, 1)
                pool.tensor_copy(lhs[:], mixT[:, :, ds(i * P, P)]).then_inc(staged, 1)

        @block.tensor
        def _(pe):
            pe.wait_ge(w_in, 16)
            with pe.Fori(0, TT) as i:
                pe.wait_ge(staged, i + 1)
                pe.wait_ge(summed, i)
                for n in range(2):
                    for k in range(KT):
                        last = pe.matmul(ps[:, n * HALF:(n + 1) * HALF], lhs[:, k, :],
                                         w[:, k, n * HALF:(n + 1) * HALF], start=(k == 0), stop=(k == KT - 1))
                last.then_inc(product, 1)
                pe.wait_ge(normed, i + 1)
                pe.wait_ge(kept, i)
                for k in range(KT):
                    last = pe.transpose(ps[:, 2 * HALF + k * P:2 * HALF + (k + 1) * P],
                                        t[:, k * P:(k + 1) * P], ident[:])
                last.then_inc(turned, 1)

        @block.scalar
        def _(act):
            with act.Fori(0, TT) as i:
                norm.on_scalar(act, i)
                act.wait_ge(normed, i + 1)
                act.copy(h[:, ds(i * D, D)], t[:])
                act.wait_ge(turned, i + 1)
                act.copy(mixT[:, :, ds(i * P, P)],
                         ps[:, 2 * HALF:4 * HALF].rearrange("p (k t) -> p k t", t=P)).then_inc(kept, 1)

        @block.vector
        def _(dve):
            dve.wait_ge(ln_in, 32)
            with dve.Fori(0, TT // 2) as j:
                n = [0]

                def link(ins):
                    n[0] += 1
                    ins.then_inc(links, 1)
                    dve.wait_ge(links, j * 2 * Norm.LINKS + n[0])

                for b in range(2):
                    i = 2 * j + b
                    dve.wait_ge(x_in[b], 16 * j + 16)
                    dve.wait_ge(product, i + 1)
                    dve.wait_ge(kept, i)
                    dve.scalar_tensor_tensor(t[:], xt[b][:], ALPHA, ps[:, 0:D], ALU.mult, ALU.add
                                             ).then_inc(summed, 1)
                    dve.wait_ge(summed, i + 1)
                    norm.on_vector(dve, link, t, *g_b, i).then_inc(normed, 1)
                assert n[0] == 2 * Norm.LINKS


def choose_experts(nc, ps, hT, idx, gate, consts, wq, keys):
    M = 2 * PH
    with ExitStack() as ctx:
        sb, sem = allocator(nc, ctx, "ex_"), semaphores(nc, ctx, "ex_")
        w = sb("w", [P, KT, M * P])
        ky = sb("ky", [P, M, NK])
        qT = sb("qT", [P, 4, P])
        sc = sb("sc", [P, M, NK])
        s16 = sb("s16", [P, PH, 2, TOPK])
        i16 = sb("i16", [P, PH, 2, TOPK], U32)
        f16 = sb("f16", [P, PH, 2, TOPK])
        cand = sb("cand", [P, PH, TOPK, TOPK])
        hot = sb("hot", [P, PH, TOPK, TOPK])
        best = sb("best", [P, PH, TOPK])
        at = sb("at", [P, PH, TOPK], U32)
        part = sb("part", [P, 2, PH, TOPK], U32)
        part_f = sb("part_f", [P, 2, PH, TOPK])
        row = sb("row", [P, 2, PH, TOPK])
        iota_i = sb("iota_i", [P, TOPK], U32)
        iota = sb("iota", [P, TOPK])
        total = sb("total", [P, 2, PH])
        names = "keys_in iota_made q_made q_copied sc_made sc_copied links centred expd chosen"
        (keys_in, iota_made, q_made, q_copied, sc_made, sc_copied, links, centred, expd,
         chosen) = (sem(n) for n in names.split())
        apart = sem("apart")
        w_in = [sem(f"w_in{k}") for k in range(4)]
        block = ctx.enter_context(nc.Block())

        @block.sync
        def _(sp):
            sp.dma_start(ky[:], keys).then_inc(keys_in, 16)
            for k in range(4):
                sp.dma_start(w[:, 2 * k:2 * k + 2, :], wq[:, 2 * k:2 * k + 2, :]).then_inc(w_in[k], 16)
            sp.wait_ge(keys_in, 16)

        @block.gpsimd
        def _(pool):
            pool.iota(iota_i[:], [[1, TOPK]], base=0, channel_multiplier=0).then_inc(iota_made, 1)
            pool.wait_ge(iota_made, 1)
            pool.tensor_copy(iota[:], iota_i[:]).then_inc(iota_made, 1)

        @block.tensor
        def _(pe):
            for k in range(4):
                pe.wait_ge(w_in[k], 16)
            pe.wait_ge(keys_in, 16)
            with pe.Fori(0, TT) as i:
                def query(m):
                    pe.wait_ge(q_copied, M * i + m - 3 if m >= 4 else M * i)
                    for k in range(KT):
                        last = pe.matmul(ps[:, (m % 4) * HALF:(m % 4) * HALF + P], w[:, k, m * P:(m + 1) * P],
                                         hT[:, k, ds(i * P, P)], start=(k == 0), stop=(k == KT - 1))
                    last.then_inc(q_made, 1)

                def score(m):
                    pe.wait_ge(q_copied, M * i + m + 1)
                    pe.wait_ge(sc_copied, M * i + m - 3 if m >= 4 else M * i)
                    pe.matmul(ps[:, (4 + m % 4) * HALF:(4 + m % 4) * HALF + NK], qT[:, m % 4, :], ky[:, m, :],
                              start=True, stop=True).then_inc(sc_made, 1)
                for m in range(M):
                    query(m)
                    if m:
                        score(m - 1)
                score(M - 1)

        def keep_score(act, i, m):
            if m == 0:
                act.wait_ge(centred, i)
            act.wait_ge(sc_made, M * i + m + 1)
            act.copy(sc[:, m, :], ps[:, (4 + m % 4) * HALF:(4 + m % 4) * HALF + NK]).then_inc(sc_copied, 1)

        @block.scalar
        def _(act):
            with act.Fori(0, TT) as i:
                for m in range(M):
                    act.wait_ge(q_made, M * i + m + 1)
                    act.wait_ge(sc_made, M * i + m - 3 if m >= 4 else M * i)
                    act.copy(qT[:, m % 4, :], ps[:, (m % 4) * HALF:(m % 4) * HALF + P]).then_inc(q_copied, 1)
                    if m:
                        keep_score(act, i, m - 1)
                keep_score(act, i, M - 1)
                act.wait_ge(centred, i + 1)
                act.activation(best[:], best[:], ACT.Exp).then_inc(expd, 1)

        @block.vector
        def _(dve):
            per_tile = 37
            dve.wait_ge(iota_made, 2)
            with dve.Fori(0, TT) as i:
                n = [0]

                def link(ins):
                    n[0] += 1
                    ins.then_inc(links, 1)
                    dve.wait_ge(links, i * per_tile + n[0])

                def top16(values, vals, idxs):
                    dve.sem_inc(apart, 1)
                    for v, o in zip(values, vals):
                        last = dve.max(o[:, 0:8], v)
                    link(last)
                    dve.sem_inc(apart, 1)
                    for v, o, p in zip(values, vals, idxs):
                        last = dve.max_index(p[:, 0:8], o[:, 0:8], v)
                    link(last)
                    dve.sem_inc(apart, 1)
                    for v, o in zip(values, vals):
                        last = dve.match_replace(v, o[:, 0:8], v, -3e38)
                    link(last)
                    dve.sem_inc(apart, 1)
                    for v, o in zip(values, vals):
                        last = dve.max(o[:, 8:16], v)
                    link(last)
                    dve.sem_inc(apart, 1)
                    for v, o, p in zip(values, vals, idxs):
                        last = dve.max_index(p[:, 8:16], o[:, 8:16], v)
                    link(last)

                for q in range(4):
                    ms = range(4 * q, 4 * q + 4)
                    dve.wait_ge(sc_copied, M * i + 4 * q + 4)
                    top16([sc[:, m, :] for m in ms], [s16[:, m // 2, m % 2, :] for m in ms],
                          [i16[:, m // 2, m % 2, :] for m in ms])
                dve.tensor_copy(f16[:], i16[:])
                link(dve.tensor_tensor(cand[:], s16[:, :, 0, :].unsqueeze(3).broadcast_to([P, PH, TOPK, TOPK]),
                                       s16[:, :, 1, :].unsqueeze(2).broadcast_to([P, PH, TOPK, TOPK]), ALU.add))
                top16([cand[:, e].rearrange("p a b -> p (a b)") for e in range(PH)],
                      [best[:, e, :] for e in range(PH)], [at[:, e, :] for e in range(PH)])
                dve.tensor_scalar(total[:, 0, :].unsqueeze(2), best[:, :, 0:1], 1.0, None, ALU.mult)
                dve.tensor_scalar(part[:, 0], at[:], 4, None, ALU.logical_shift_right)
                link(dve.tensor_scalar(part[:, 1], at[:], TOPK - 1, None, ALU.bitwise_and))
                dve.tensor_tensor(best[:], best[:], total[:, 0, :].unsqueeze(2).broadcast_to([P, PH, TOPK]),
                                  ALU.subtract).then_inc(centred, 1)
                link(dve.tensor_copy(part_f[:], part[:]))
                for x in range(2):
                    link(dve.tensor_tensor(hot[:], part_f[:, x].unsqueeze(3).broadcast_to([P, PH, TOPK, TOPK]),
                                           iota[:].unsqueeze(1).unsqueeze(1).broadcast_to([P, PH, TOPK, TOPK]),
                                           ALU.is_equal))
                    link(dve.tensor_tensor(hot[:], hot[:], f16[:, :, x, :].unsqueeze(2)
                                           .broadcast_to([P, PH, TOPK, TOPK]), ALU.mult))
                    link(dve.tensor_reduce(row[:, x], hot[:], AX.X, ALU.add))
                dve.scalar_tensor_tensor(idx[:, ds(i * NSEL, NSEL)], row[:, 0].rearrange("p h k -> p (h k)"),
                                         float(NK), row[:, 1].rearrange("p h k -> p (h k)"), ALU.mult, ALU.add)
                dve.wait_ge(expd, i + 1)
                link(dve.tensor_reduce(total[:, 0, :], best[:], AX.X, ALU.add))
                link(dve.reciprocal(total[:, 1, :], total[:, 0, :]))
                link(dve.tensor_tensor(gate[:, ds(i * NSEL, NSEL)].rearrange("p (h k) -> p h k", k=TOPK), best[:],
                                       total[:, 1, :].unsqueeze(2).broadcast_to([P, PH, TOPK]), ALU.mult))
                assert n[0] == per_tile, n[0]


def apply_experts(nc, ps, h, idx, gate, consts, u, v, ln, out):
    ident = consts["ident"]
    with ExitStack() as ctx:
        sb, sem = allocator(nc, ctx, "ap_"), semaphores(nc, ctx, "ap_")
        rows_u = sb("rows_u", [P, GRP, D])
        rows_v = sb("rows_v", [P, GRP, D])
        picks = [sb(f"picks{b}", [P, GRP], U32) for b in range(2)]
        z = sb("z", [P, 2, GRP])
        act_z = sb("act_z", [P, 2, GRP])
        wt = sb("wt", [P, 2, GRP])
        diag = sb("diag", [P, 2, GRP, P])
        zero = sb("zero", [P, P])
        keep = sb("keep", [P, P])
        hc = sb("hc", [P, D])
        t = sb("t", [P, D])
        g_b = [sb(n, [P, D]) for n in ("g", "b")]
        u_in = [sem(f"u_in{j}") for j in range(GRP)]
        v_in = [sem(f"v_in{j}") for j in range(GRP)]
        u_read = [sem(f"u_read{j}") for j in range(GRP)]
        v_read = [sem(f"v_read{j}") for j in range(GRP)]
        names = "ln_in ready picked h_copied bent weighted spread summed links normed stored copied"
        (ln_in, ready, picked, h_copied, bent, weighted, spread, summed, links, normed, stored,
         copied) = (sem(n) for n in names.split())
        apart = sem("apart")
        norm = Norm(sb, sem, "ln", apart)
        block = ctx.enter_context(nc.Block())
        HG = NG // 2

        @block.gpsimd
        def _(pool):
            pool.memset(zero[:], 0.0).then_inc(ready, 1)
            with pool.Fori(0, TT) as i:
                with pool.Fori(0, HG) as gg:
                    for b in range(2):
                        q = NG * i + 2 * gg + b
                        pool.wait_ge(v_in[GRP - 1], 16 * q)
                        pool.wait_ge(u_in[GRP - 1], 16 * q)
                        pool.sem_inc(apart, 1)
                        pool.tensor_copy(picks[b][:], idx[:, ds(i * NSEL + (2 * gg + b) * GRP, GRP)]
                                         ).then_inc(picked, 1)
                        pool.wait_ge(picked, q + 1)
                        pool.sem_inc(apart, 1)
                        for table, rows, landed, read in ((u, rows_u, u_in, u_read), (v, rows_v, v_in, v_read)):
                            for j in range(GRP):
                                pool.wait_ge(read[j], q)
                                pool.sem_inc(apart, 1)
                                pool.indirect_dma_start(
                                    out=rows[:, j, :], out_offset=None, in_=table,
                                    in_offset=bass.IndirectOffsetOnAxis(ap=picks[b][:, j:j + 1], axis=0),
                                ).then_inc(landed[j], 16)

        @block.sync
        def _(sp):
            for k in range(2):
                sp.dma_start(g_b[k][:], ln[k].partition_broadcast(P)).then_inc(ln_in, 16)
            with sp.Fori(0, TT) as i:
                sp.wait_ge(normed, i + 1)
                sp.dma_start(out[ds(i * P, P), :], t[:]).then_inc(stored, 16)
            sp.wait_ge(stored, 16 * TT)

        @block.vector
        def _(dve):
            dve.wait_ge(ln_in, 32)
            with dve.Fori(0, TT) as i:
                n = [0]

                def link(ins):
                    n[0] += 1
                    ins.then_inc(links, 1)
                    dve.wait_ge(links, i * Norm.LINKS + n[0])
                dve.tensor_copy(hc[:], h[:, ds(i * D, D)]).then_inc(h_copied, 1)
                dve.wait_ge(h_copied, i + 1)
                dve.sem_inc(apart, 1)
                with dve.Fori(0, HG) as gg:
                    for b in range(2):
                        q = NG * i + 2 * gg + b
                        for j in range(GRP):
                            dve.wait_ge(u_in[j], 16 * q + 16)
                            dve.tensor_tensor_reduce(rows_u[:, j, :], rows_u[:, j, :], hc[:], 1.0, 0.0,
                                                     ALU.mult, ALU.add, z[:, b, j:j + 1]).then_inc(u_read[j], 1)
                        dve.wait_ge(bent, q + 1)
                        dve.tensor_tensor(wt[:, b, :], act_z[:, b, :],
                                          gate[:, ds(i * NSEL + (2 * gg + b) * GRP, GRP)], ALU.mult
                                          ).then_inc(weighted, 1)
                dve.wait_ge(summed, i + 1)
                dve.wait_ge(stored, 16 * i)
                dve.tensor_copy(t[:], ps[:, 0:D]).then_inc(copied, 1)
                dve.wait_ge(copied, i + 1)
                norm.on_vector(dve, link, t, *g_b, i).then_inc(normed, 1)
                assert n[0] == Norm.LINKS

        @block.scalar
        def _(act):
            act.wait_ge(ready, 1)
            act.mul(keep[:], ident[:], ALPHA).then_inc(ready, 1)
            with act.Fori(0, TT) as i:
                with act.Fori(0, HG) as gg:
                    for b in range(2):
                        q = NG * i + 2 * gg + b
                        act.wait_ge(u_read[GRP - 1], q + 1)
                        act.activation(act_z[:, b, :], z[:, b, :], ACT.Gelu).then_inc(bent, 1)
                        act.wait_ge(weighted, q + 1)
                        for j in range(GRP):
                            act.activation(diag[:, b, j, :], ident[:], ACT.Copy, scale=wt[:, b, j:j + 1]
                                           ).then_inc(spread, 1)
                norm.on_scalar(act, i)

        @block.tensor
        def _(pe):
            pe.wait_ge(ready, 2)
            with pe.Fori(0, TT) as i:
                pe.wait_ge(copied, i)
                for n in range(2):
                    pe.matmul(ps[:, n * HALF:(n + 1) * HALF], zero[:], h[:, ds(i * D + n * HALF, HALF)],
                              start=True, stop=False)
                with pe.Fori(0, HG) as gg:
                    for b in range(2):
                        q = NG * i + 2 * gg + b
                        for j in range(GRP):
                            pe.wait_ge(v_in[j], 16 * q + 16)
                            pe.wait_ge(spread, GRP * q + j + 1)
                            for n in range(2):
                                last = pe.matmul(ps[:, n * HALF:(n + 1) * HALF], diag[:, b, j, :],
                                                 rows_v[:, j, n * HALF:(n + 1) * HALF], start=False, stop=False)
                            last.then_inc(v_read[j], 1)
                for n in range(2):
                    last = pe.matmul(ps[:, n * HALF:(n + 1) * HALF], keep[:], h[:, ds(i * D + n * HALF, HALF)],
                                     start=False, stop=True)
                last.then_inc(summed, 1)


def program(nc, x, x_t, w_tiles, rope, masks, sink, perm, mu, low_rank, params, tri, tri_l, eye, ident_in,
            ones_in, w_out, ln1, wq, keys, u, v, ln2, out):
    with ExitStack() as ctx:
        sb = allocator(nc, ctx)
        ps = ctx.enter_context(nc.psum_tensor("ps", [P, 8 * HALF], F32))
        banks = [ps[:, n * HALF:(n + 1) * HALF] for n in range(8)]
        mixT = sb("mixT", [P, KT, SEQ])
        ident = sb("ident", [P, P])
        ones = sb("ones", [P, P])
        chunks = nc.dram_tensor("chunks", [2, NC, P, HP * XS * CH], F32, kind="Internal").ap()
        consts = {"ident": ident, "ones": ones, "eye": eye}
        consts_in = ctx.enter_context(nc.semaphore("consts_in"))
        with nc.Block() as block:
            @block.sync
            def _(sp):
                sp.dma_start(ident[:], ident_in).then_inc(consts_in, 16)
                sp.dma_start(ones[:], ones_in).then_inc(consts_in, 16)
                sp.wait_ge(consts_in, 32)
        with ExitStack() as mixer:
            msb = allocator(nc, mixer)
            feat = msb("feat", [P, 16 * SEQ])
            with ExitStack() as attention:
                asb = allocator(nc, attention)
                at = asb("at", [P, NAT * SEQ])
                with ExitStack() as projection:
                    xT = allocator(nc, projection)("xT", [P, KT, SEQ])
                    project(nc, banks, x_t, w_tiles, xT, ((feat[:, SEQ:], NFT), (at, NAT)), "pr_")
                attend(nc, banks, at, mixT, consts, rope, masks, sink, perm)
            gates = msb("gates", [P, 2, HP, NC])
            shift_tokens(nc, feat, mu)
            prepare_chunks(nc, ps, feat, consts, low_rank, params, chunks, gates)
            run_chunks(nc, ps, feat, consts, chunks, gates, tri, tri_l)
            finish_rwkv(nc, ps, feat, mixT, consts, params)
        h = sb("h", [P, TT * D])
        idx = sb("idx", [P, TT * NSEL], U32)
        gate = sb("gate", [P, TT * NSEL])
        mix_and_norm(nc, ps, mixT, h, consts, x, w_out, ln1)
        choose_experts(nc, ps, mixT, idx, gate, consts, wq, keys)
        apply_experts(nc, ps, h, idx, gate, consts, u, v, ln2, out)


def constants():
    f = np.float32
    pos = np.arange(SEQ, dtype=f)
    inv = f(10000.0) ** (-np.arange(0, HD, 2, dtype=f) / f(HD))
    ang = np.concatenate([pos[:, None] * inv[None, :]] * 2, -1).astype(f)
    cos, sin = np.cos(ang).T, np.sin(ang).T.copy()
    sin[:HD // 2] *= -1
    rope = np.stack([np.tile(cos, (2, 1)), np.tile(sin, (2, 1))]).astype(f)
    perm = np.zeros((P, P), f)
    for m in range(P):
        perm[m // HD * HD + (m % HD + HD // 2) % HD, m] = 1
    q, k = np.arange(P)[:, None], np.arange(WIN)[None] - P
    masks = np.zeros((P, TT, WIN), f)
    for n in range(TT):
        at = k + n * P
        masks[:, n] = np.where((abs(q - k) <= P) & (at >= 0) & (at < SEQ), 0, NEG)
    j, t = np.meshgrid(np.arange(CH), np.arange(CH), indexing="ij")
    tri = np.stack([np.stack([j <= t, j < t], 1), np.stack([j >= t, j > t], 1)], 1).astype(f)
    tri_l = np.stack([j > t, j < t], 1).astype(f)
    pair = np.kron(np.eye(2, dtype=f), np.ones((HD, HD), f))
    return {"rope": rope, "masks": masks, "perm": perm, "tri": np.tile(tri, (2, 1, 1, 1)),
            "tri_l": np.tile(tri_l, (2, 1, 1)), "eye": np.tile(np.eye(CH, dtype=f), (2, 1)),
            "ident_in": np.eye(P, dtype=f), "ones_in": pair}


def layouts(inp):
    f = np.float32
    o = {"x": inp["x"][0]}
    o["x_t"] = np.ascontiguousarray(inp["x"][0].T.reshape(KT, P, SEQ).transpose(1, 0, 2))
    attn = (NH + 2 * 2) * HD
    n_rwkv = inp["mu_prev"].shape[-1]
    pair_cols = [c for p in range(NH // 2) for s in range(2) for c in range((4 * s + p) * HD, (4 * s + p + 1) * HD)]
    order = list(range(attn, attn + n_rwkv)) + [-1] * (NFT * P - n_rwkv) + pair_cols + list(range(NH * HD, attn))
    w = np.concatenate([inp["w_in"][0], np.zeros((D, 1), f)], 1)[:, order]
    o["w_tiles"] = np.ascontiguousarray(w.reshape(KT, P, NFT + NAT, P).transpose(2, 1, 0, 3))
    mu = np.zeros((2, NFT * P), f)
    mu[0, :n_rwkv], mu[1, :n_rwkv] = inp["mu_prev"][0], inp["mu_next"][0]
    o["mu"] = np.ascontiguousarray(mu.reshape(2, NFT, P).transpose(0, 2, 1))
    lr = np.zeros((HP, P, 5, P), f)
    for hp in range(HP):
        c = slice(hp * P, hp * P + P)
        for n, part in enumerate((inp["w2"][0, 0], inp["w2"][0, 1], inp["a2"][0, 0], inp["a2"][0, 1])):
            lr[hp, 32 * n:32 * n + 32, n] = part[:, c]
        lr[hp, :inp["g2"].shape[1], 4] = inp["g2"][0][:, c]
    o["low_rank"] = lr
    cols = [inp["w0"][0, 0], inp["w0"][0, 1], inp["a0"][0, 0], inp["a0"][0, 1], inp["k_k"][0], inp["k_a"][0],
            inp["r_k"][0].reshape(-1), inp["lnx_g"][0], inp["lnx_b"][0]]
    o["params"] = np.stack([c.reshape(HP, P).T for c in cols], -1)
    o["sink"] = inp["sink"][0].reshape(2, NH // 2).T.reshape(-1)
    rows = pair_cols + list(range(NH * HD, 2 * NH * HD))
    o["w_out"] = np.ascontiguousarray(inp["w_out"][0][rows].reshape(KT, P, D).transpose(1, 0, 2))
    o["ln1"] = np.stack([inp["ln1_g"][0], inp["ln1_b"][0]])
    o["ln2"] = np.stack([inp["ln2_g"][0], inp["ln2_b"][0]])
    o["wq"] = np.ascontiguousarray(inp["peer_wq"][0].reshape(KT, P, 2 * PH * P).transpose(1, 0, 2))
    o["keys"] = np.ascontiguousarray(inp["peer_keys"][0].reshape(2 * PH, NK, P).transpose(2, 0, 1))
    o["u"], o["v"] = inp["peer_u"][0], inp["peer_v"][0]
    return o


_ORDER = ["x", "x_t", "w_tiles", "rope", "masks", "sink", "perm", "mu", "low_rank", "params", "tri", "tri_l",
          "eye", "ident_in", "ones_in", "w_out", "ln1", "wq", "keys", "u", "v", "ln2"]


def kernel(**inputs):
    from concourse import bacc
    from concourse.bass_utils import run_bass_kernel_spmd

    arrays = layouts({k: np.asarray(a) for k, a in inputs.items()})
    arrays.update(constants())
    nc = bacc.Bacc("TRN2", target_bir_lowering=False, num_devices=1)
    args = []
    for name in _ORDER:
        a = arrays[name] = np.ascontiguousarray(arrays[name])
        args.append(nc.dram_tensor("in_" + name, a.shape, mybir.dt.from_np(a.dtype), kind="ExternalInput").ap())
    args.append(nc.dram_tensor("out_y", (SEQ, D), F32, kind="ExternalOutput").ap())
    program(nc, *args)
    r = run_bass_kernel_spmd(nc, [{"in_" + n: arrays[n] for n in _ORDER}], core_ids=[0])
    return r.results[0]["out_y"].reshape(1, SEQ, D)
```

```python
from contextlib import ExitStack

import numpy as np
import concourse.bass as bass
from concourse import mybir

F32 = mybir.dt.float32
U32 = mybir.dt.uint32
ALU = mybir.AluOpType
ACT = mybir.ActivationFunctionType
AX = mybir.AxisListType
ds = bass.ds

P = 128
SEQ = 1024
D = 1024
KT = D // P
TT = SEQ // P
HD = 64
NH = 8
HP = NH // 2
CH = 64
NC = SEQ // CH
XS = 5
NFT = 14
NAT = 6
WIN = 3 * P
PADDED = SEQ + 2 * P
ALPHA = 2.0 ** 0.25
DECAY = float(np.exp(-0.5))
GN_EPS = 64e-5
LN_EPS = 1e-5
NEG = -1e30
PH = 8
NK = 128
TOPK = 16
NSEL = PH * TOPK
GRP = 8
NG = NSEL // GRP
HALF = 512

W0F, W0B, A0F, A0B, KKS, KA, RK, LNG, LNB, KAC = range(10)
NPAR = 9


def allocator(nc, ctx, prefix=""):
    def sb(name, shape, dtype=F32):
        return ctx.enter_context(nc.sbuf_tensor(prefix + name, list(shape), dtype))
    return sb


def semaphores(nc, ctx, prefix):
    used = []

    def clear():
        with nc.Block() as block:
            @block.gpsimd
            def _(pool):
                for s in used:
                    pool.sem_clear(s)

    def sem(name):
        used.append(ctx.enter_context(nc.semaphore(prefix + name)))
        return used[-1]
    ctx.callback(clear)
    return sem


def project(nc, banks, x_t, w_tiles, xT, groups, tag):
    total = sum(n for _, n in groups)
    with ExitStack() as ctx:
        sb, sem = allocator(nc, ctx, tag), semaphores(nc, ctx, tag)
        w = [sb(f"w{b}", [P, KT, P]) for b in range(2)]
        x_in = [sem(f"x_in{k}") for k in range(2)]
        w_in = [sem(f"w_in{b}") for b in range(2)]
        product = [sem(f"product{h}") for h in range(2)]
        copied = [[sem(f"copied{b}{h}") for h in range(2)] for b in range(2)]
        block = ctx.enter_context(nc.Block())

        @block.sync
        def _(sp):
            for k in range(2):
                sp.dma_start(xT[:, k * 4:k * 4 + 4, :], x_t[:, k * 4:k * 4 + 4, :]).then_inc(x_in[k], 16)
            for b in range(2):
                sp.dma_start(w[b][:], w_tiles[b]).then_inc(w_in[b], 16)
            with sp.Fori(1, total // 2) as j:
                for b in range(2):
                    sp.wait_ge(product[1], 2 * j - 1 + b)
                    sp.dma_start(w[b][:], w_tiles[ds(2 * j + b, 1)].rearrange("o p k c -> p (o k) c")
                                 ).then_inc(w_in[b], 16)

        @block.tensor
        def _(pe):
            for k in range(2):
                pe.wait_ge(x_in[k], 16)
            with pe.Fori(0, total // 2) as j:
                for b in range(2):
                    pe.wait_ge(w_in[b], 16 * j + 16)
                    for h in range(2):
                        pe.wait_ge(copied[b][h], j)
                        bank = banks[2 * b + h]
                        for k in range(KT):
                            last = pe.matmul(bank[:], w[b][:, k, :], xT[:, k, h * HALF:(h + 1) * HALF],
                                             start=(k == 0), stop=(k == KT - 1))
                        last.then_inc(product[h], 1)

        def copies(eng, h, copy):
            done = 0
            for dest, n in groups:
                with eng.Fori(0, n // 2) as j:
                    for b in range(2):
                        eng.wait_ge(product[h], done + 2 * j + b + 1)
                        copy(dest[:, ds((2 * j + b) * SEQ + h * HALF, HALF)],
                             banks[2 * b + h][:]).then_inc(copied[b][h], 1)
                done += n

        @block.scalar
        def _(act):
            copies(act, 0, act.copy)

        @block.vector
        def _(dve):
            copies(dve, 1, dve.tensor_copy)


def attend(nc, banks, at, mixT, consts, rope, masks, sink, perm, attended):
    ident = consts["ident"]
    with ExitStack() as ctx:
        sb, sem = allocator(nc, ctx, "at_"), semaphores(nc, ctx, "at_")
        cosT = sb("cosT", [P, SEQ])
        sinT = sb("sinT", [P, SEQ])
        swap = sb("swap", [P, P])
        mask = sb("mask", [P, TT, WIN])
        snk = sb("snk", [P, NH])
        turned = sb("turned", [P, 2, HALF])
        kP = sb("kP", [P, PADDED])
        vP = sb("vP", [P, TT + 2, P])
        qs = sb("qs", [P, 4, P])
        ks = sb("ks", [P, WIN])
        vs = sb("vs", [P, WIN])
        lg = sb("lg", [P, NH, WIN])
        st = sb("st", [P, 6, NH])
        pT = sb("pT", [P, 2, WIN])
        tables, cleared, apart = sem("tables"), sem("cleared"), sem("apart")
        swapped, dve_step, act_step = sem("swapped"), sem("dve_step"), sem("act_step")
        v_turned, v_copied = sem("v_turned"), sem("v_copied")
        staged, logits, masked = sem("staged"), sem("logits"), sem("masked")
        chain, maxed, expd, probs = sem("chain"), sem("maxed"), sem("expd"), sem("probs")
        turnd, pcopied, out_done, stored = sem("turnd"), sem("pcopied"), sem("out_done"), sem("stored")
        set_aside = sem("set_aside")
        loads = ((cosT, rope[0]), (sinT, rope[1]), (swap, perm), (mask, masks),
                 (snk, sink.partition_broadcast(P)))

        with nc.Block() as block:
            @block.sync
            def _(sp):
                for to, of in loads:
                    sp.dma_start(to[:], of).then_inc(tables, 16)
                sp.wait_ge(tables, 16 * len(loads))

            @block.gpsimd
            def _(pool):
                pool.memset(kP[:], 0.0).then_inc(cleared, 1)
                pool.memset(vP[:], 0.0).then_inc(cleared, 1)

            @block.tensor
            def _(pe):
                pe.wait_ge(tables, 16 * len(loads))
                with pe.Fori(0, 5) as f:
                    for h in range(2):
                        pe.wait_ge(dve_step, 2 * f + h)
                        pe.matmul(banks[h][:], swap[:], at[:, ds(f * SEQ + h * HALF, HALF)],
                                  start=True, stop=True).then_inc(swapped, 1)
                for n in range(TT):
                    if n >= 4:
                        pe.wait_ge(v_copied, n - 3)
                    pe.transpose(banks[4 + n % 4][:, 0:P], at[:, 5 * SEQ + n * P:5 * SEQ + n * P + P],
                                 ident[:]).then_inc(v_turned, 1)

            @block.scalar
            def _(act):
                act.wait_ge(cleared, 2)
                for n in range(TT):
                    act.wait_ge(v_turned, n + 1)
                    act.copy(vP[:, n + 1, :], banks[4 + n % 4][:, 0:P]).then_inc(v_copied, 1)

            @block.vector
            def _(dve):
                dve.wait_ge(tables, 16 * len(loads))
                with dve.Fori(0, 5) as f:
                    for h in range(2):
                        cols = ds(f * SEQ + h * HALF, HALF)
                        dve.wait_ge(swapped, 2 * f + h + 1)
                        dve.tensor_tensor(turned[:, h, :], banks[h][:], sinT[:, h * HALF:(h + 1) * HALF],
                                          ALU.mult).then_inc(dve_step, 1)
                        dve.tensor_tensor(at[:, cols], at[:, cols], cosT[:, h * HALF:(h + 1) * HALF],
                                          ALU.mult).then_inc(chain, 1)
                        dve.wait_ge(chain, 4 * f + 2 * h + 1)
                        dve.wait_ge(dve_step, 2 * f + h + 1)
                        dve.tensor_tensor(at[:, cols], at[:, cols], turned[:, h, :], ALU.add
                                          ).then_inc(chain, 1)
                dve.wait_ge(chain, 20)
                dve.wait_ge(cleared, 2)
                dve.tensor_copy(kP[:, P:P + SEQ], at[:, 4 * SEQ:5 * SEQ]).then_inc(chain, 1)

        dve_n = 4

        with nc.Block() as block:
            @block.sync
            def _(sp):
                with sp.Fori(0, TT) as n:
                    sp.wait_ge(stored, 4 * n + 4)
                    sp.dma_start(attended[:, :, ds(n * P, P)], mixT[:, 0:4, ds(n * P, P)]).then_inc(set_aside, 16)
                sp.wait_ge(set_aside, 16 * TT)

            @block.gpsimd
            def _(pool):
                with pool.Fori(0, TT) as n:
                    pool.wait_ge(out_done, 4 * n)
                    pool.sem_inc(apart, 1)
                    pool.tensor_copy(qs[:], at[:].rearrange("p (f t) -> p f t", t=SEQ)[:, 0:4, ds(n * P, P)]
                                     ).then_inc(staged, 1)
                    pool.tensor_copy(ks[:], kP[:, ds(n * P, WIN)]).then_inc(staged, 1)
                    pool.tensor_copy(vs[:], vP[:].rearrange("p b c -> p (b c)")[:, ds(n * P, WIN)]
                                     ).then_inc(staged, 1)

            @block.tensor
            def _(pe):
                with pe.Fori(0, TT) as n:
                    pe.wait_ge(staged, 3 * n + 3)
                    for p in range(4):
                        for s in range(2):
                            pe.wait_ge(masked, 8 * n + 2 * p + s - 3 if p >= 2 else 8 * n)
                            pe.matmul(banks[2 * (p % 2) + s][:, 0:WIN], qs[s * HD:(s + 1) * HD, p, :],
                                      ks[s * HD:(s + 1) * HD, :], start=True, stop=True
                                      ).then_inc(logits, 1)
                    for p in range(4):
                        for s in range(2):
                            i = 2 * p + s
                            pe.wait_ge(probs, 8 * n + i + 1)
                            pe.wait_ge(pcopied, 8 * n + i - 1 if i >= 2 else 8 * n)
                            for c in range(3):
                                last = pe.transpose(banks[4 + s][:, c * P:(c + 1) * P],
                                                    lg[:, i, c * P:(c + 1) * P], ident[:])
                            last.then_inc(turnd, 1)
                        for s in range(2):
                            i = 2 * p + s
                            pe.wait_ge(pcopied, 8 * n + i + 1)
                            if s == 0:
                                pe.wait_ge(stored, 4 * n + p - 1 if p >= 2 else 4 * n)
                            for c in range(3):
                                last = pe.matmul(banks[6 + p % 2][s * HD:(s + 1) * HD, 0:P],
                                                 vs[:, c * P + s * HD:c * P + (s + 1) * HD],
                                                 pT[:, s, c * P:(c + 1) * P], start=(c == 0), stop=(c == 2))
                        last.then_inc(out_done, 1)

            @block.vector
            def _(dve):
                with dve.Fori(0, TT) as n:
                    for i in range(NH):
                        p, s = i // 2, i % 2
                        dve.wait_ge(logits, 8 * n + i + 1)
                        dve.wait_ge(turnd, 8 * n)
                        dve.scalar_tensor_tensor(lg[:, i, :], banks[2 * (p % 2) + s][:, 0:WIN],
                                                 HD ** -0.5, mask[:, ds(n, 1), :].rearrange("p a k -> p (a k)"),
                                                 ALU.mult, ALU.add).then_inc(masked, 1)
                    dve.wait_ge(masked, 8 * n + 8)
                    dve.tensor_reduce(st[:, 0, :], lg[:], AX.X, ALU.max).then_inc(chain, 1)
                    dve.wait_ge(chain, 21 + 1 + dve_n * n)
                    dve.tensor_tensor(st[:, 1, :], st[:, 0, :], snk[:], ALU.max).then_inc(chain, 1)
                    dve.wait_ge(chain, 21 + 2 + dve_n * n)
                    dve.tensor_scalar(st[:, 2, :], st[:, 1, :], -1.0, None, ALU.mult).then_inc(maxed, 1)
                    dve.tensor_tensor(st[:, 3, :], snk[:], st[:, 1, :], ALU.subtract).then_inc(maxed, 1)
                    dve.wait_ge(expd, 9 * n + 9)
                    dve.tensor_tensor(st[:, 5, :], st[:, 5, :], st[:, 4, :], ALU.add).then_inc(chain, 1)
                    dve.wait_ge(chain, 21 + 3 + dve_n * n)
                    dve.reciprocal(st[:, 0, :], st[:, 5, :]).then_inc(chain, 1)
                    dve.wait_ge(chain, 21 + 4 + dve_n * n)
                    for i in range(NH):
                        dve.tensor_scalar(lg[:, i, :], lg[:, i, :], st[:, 0, i:i + 1], None, ALU.mult
                                          ).then_inc(probs, 1)
                    for p in range(4):
                        dve.wait_ge(out_done, 4 * n + p + 1)
                        dve.tensor_copy(mixT[:, p, :][:, ds(n * P, P)], banks[6 + p % 2][:, 0:P]
                                        ).then_inc(stored, 1)

            @block.scalar
            def _(act):
                with act.Fori(0, TT) as n:
                    act.wait_ge(maxed, 2 * n + 2)
                    act.activation(st[:, 4, :], st[:, 3, :], ACT.Exp).then_inc(expd, 1)
                    for i in range(NH):
                        act.activation(lg[:, i, :], lg[:, i, :], ACT.Exp, bias=st[:, 2, i:i + 1],
                                       accum_out=st[:, 5, i:i + 1]).then_inc(expd, 1)
                    for i in range(NH):
                        act.wait_ge(turnd, 8 * n + i + 1)
                        act.wait_ge(out_done, 4 * n + i // 2)
                        act.copy(pT[:, i % 2, :], banks[4 + i % 2][:, 0:WIN]).then_inc(pcopied, 1)


def shift_tokens(nc, feat, mu):
    with ExitStack() as ctx:
        sb, sem = allocator(nc, ctx, "sh_"), semaphores(nc, ctx, "sh_")
        part = sb("part", [P, 3, NFT])
        mu_in, links, shifted, bent = sem("mu_in"), sem("links"), sem("shifted"), sem("bent")
        block = ctx.enter_context(nc.Block())
        mp, mn, m0 = (part[:, i, :] for i in range(3))

        @block.sync
        def _(sp):
            for i in range(2):
                sp.dma_start(part[:, i, :], mu[i]).then_inc(mu_in, 16)
            sp.wait_ge(mu_in, 32)

        @block.vector
        def _(dve):
            dve.wait_ge(mu_in, 32)
            dve.tensor_tensor(m0, mp, mn, ALU.add).then_inc(links, 1)
            dve.wait_ge(links, 1)
            dve.tensor_scalar(m0, m0, -1.0, 1.0, ALU.mult, ALU.add).then_inc(links, 1)
            dve.wait_ge(links, 2)
            with dve.Fori(0, NFT) as f:
                def new(a, n):
                    return feat[:, ds(f * SEQ + a, n)]

                def old(a, n):
                    return feat[:, ds(f * SEQ + SEQ + a, n)]
                dve.tensor_scalar(new(0, SEQ), old(0, SEQ), m0[:, ds(f, 1)], None, ALU.mult).then_inc(links, 1)
                dve.wait_ge(links, 2 * f + 3)
                dve.scalar_tensor_tensor(new(1, SEQ - 1), old(0, SEQ - 1), mp[:, ds(f, 1)],
                                         new(1, SEQ - 1), ALU.mult, ALU.add).then_inc(links, 1)
                dve.wait_ge(links, 2 * f + 4)
                dve.scalar_tensor_tensor(new(0, SEQ - 1), old(1, SEQ - 1), mn[:, ds(f, 1)],
                                         new(0, SEQ - 1), ALU.mult, ALU.add).then_inc(shifted, 1)
                dve.wait_ge(shifted, f + 1)

        @block.scalar
        def _(act):
            act.wait_ge(shifted, NFT)
            wd = feat[0:2 * 32, 12 * SEQ:13 * SEQ]
            gd = feat[:, 13 * SEQ:14 * SEQ]
            act.activation(wd, wd, ACT.Tanh).then_inc(bent, 1)
            act.activation(gd, gd, ACT.Sigmoid).then_inc(bent, 1)


def prepare_chunks(nc, ps, feat, consts, low_rank, params, chunks, gates):
    ones = consts["ones"]
    with ExitStack() as ctx:
        sb, sem = allocator(nc, ctx, "pc_"), semaphores(nc, ctx, "pc_")
        lr = sb("lr", [P, 5, P])
        par_all = sb("par_all", [P, HP, NPAR])
        par = sb("par", [P, NPAR + 1])
        reset = sb("reset", [P, SEQ])
        sg = [sb(f"sg{d}", [P, SEQ]) for d in range(2)]
        a = [sb(f"a{d}", [P, SEQ]) for d in range(2)]
        kd = [sb(f"kd{d}", [P, SEQ]) for d in range(2)]
        kk = sb("kk", [P, SEQ])
        nrm = sb("nrm", [P, SEQ])
        cs = sb("cs", [P, SEQ])
        X = sb("X", [P, SEQ])
        Y = sb("Y", [P, SEQ])
        E = sb("E", [P, SEQ])
        half = sb("half", [P, NC])
        nxt = sb("nxt", [P, 2, NC])
        st = [sb(f"st{d}", [P, NC, XS, CH]) for d in range(2)]
        names = ("par_in lr_in scans_ready ranks keyed squared summed rooted links xy exps gate_in "
                 "gated staged_v written sigs floored bonus_in bonus_sum bonus_out g_prod g_out")
        (par_in, lr_in, scans_ready, ranks, keyed, squared, summed, rooted, links, xy, exps, gate_in,
         gated, staged_v, written, sigs, floored, bonus_in, bonus_sum, bonus_out, g_prod,
         g_out) = (sem(n) for n in names.split())
        apart = sem("apart")
        staged = [sem(f"staged{d}") for d in range(2)]
        stored = [sem(f"stored{d}") for d in range(2)]
        block = ctx.enter_context(nc.Block())
        slots = feat[:].rearrange("p (f t) -> p f t", t=SEQ)

        def slot(f, hp):
            return feat[:, ds((f + hp) * SEQ, SEQ)]

        def by_chunk(t):
            return t[:].rearrange("p (c t) -> p c t", t=CH)

        @block.sync
        def _(sp):
            sp.dma_start(par_all[:], params).then_inc(par_in, 16)
            with sp.Fori(0, HP) as hp:
                sp.wait_ge(g_prod, hp)
                sp.sem_inc(apart, 1)
                sp.dma_start(lr[:], low_rank[ds(hp, 1)].rearrange("o p x c -> p (o x) c")).then_inc(lr_in, 16)
                for d in range(2):
                    sp.wait_ge(staged[d], 4 * hp + 4)
                    sp.sem_inc(apart, 1)
                    sp.wait_ge(staged_v, 2 * hp + d + 1)
                    sp.sem_inc(apart, 1)
                    for c in range(0, NC, 8):
                        sp.dma_start(chunks[d, c:c + 8, :, ds(hp * XS * CH, XS * CH)].rearrange("c p n -> p c n"),
                                     st[d][:, c:c + 8].rearrange("p c x t -> p c (x t)")).then_inc(stored[d], 16)
            for d in range(2):
                sp.wait_ge(stored[d], 2 * 16 * HP)

        @block.tensor
        def _(pe):
            with pe.Fori(0, HP) as hp:
                pe.wait_ge(lr_in, 16 * hp + 16)
                pe.wait_ge(g_out, hp)
                pe.wait_ge(bonus_out, hp)
                pe.wait_ge(floored, hp)
                for x in range(4):
                    for h in range(2):
                        last = pe.matmul(ps[:, (2 * x + h) * HALF:(2 * x + h + 1) * HALF], lr[:, x, :],
                                         feat[:, 12 * SEQ + h * HALF:12 * SEQ + (h + 1) * HALF],
                                         start=True, stop=True)
                    last.then_inc(ranks, 1)
                pe.wait_ge(squared, hp + 1)
                pe.wait_ge(sigs, 4 * hp + 4)
                for h in range(2):
                    last = pe.matmul(ps[:, h * HALF:(h + 1) * HALF], ones[:], nrm[:, h * HALF:(h + 1) * HALF],
                                     start=True, stop=True)
                last.then_inc(summed, 1)
                for h in range(2):
                    last = pe.matmul(ps[:, (4 + h) * HALF:(5 + h) * HALF], lr[:, 4, :],
                                     feat[:, 13 * SEQ + h * HALF:13 * SEQ + (h + 1) * HALF],
                                     start=True, stop=True)
                last.then_inc(g_prod, 1)
                pe.wait_ge(bonus_in, hp + 1)
                for h in range(2):
                    last = pe.matmul(ps[:, (2 + h) * HALF:(3 + h) * HALF], ones[:], X[:, h * HALF:(h + 1) * HALF],
                                     start=True, stop=True)
                last.then_inc(bonus_sum, 1)

        @block.gpsimd
        def _(pool):
            pool.memset(reset[:], 1.0).then_inc(scans_ready, 1)
            pool.wait_ge(scans_ready, 1)
            pool.memset(by_chunk(reset)[:, :, 0:1], 0.0).then_inc(scans_ready, 1)
            with pool.Fori(0, HP) as hp:
                for d in range(2):
                    pool.wait_ge(stored[d], 32 * hp)
                    pool.sem_inc(apart, 1)
                    pool.tensor_copy(st[d][:, :, 4, :],
                                     slot(8, hp).rearrange("p (c t) -> p c t", t=CH)).then_inc(staged_v, 1)

        @block.scalar
        def _(act):
            with act.Fori(0, HP) as hp:
                act.wait_ge(written, hp + 1)
                for x, (to, col) in enumerate(((sg[0], W0F), (sg[1], W0B), (a[0], A0F), (a[1], A0B))):
                    act.wait_ge(ranks, 4 * hp + x + 1)
                    act.activation(to[:], ps[:, 2 * x * HALF:(2 * x + 2) * HALF], ACT.Sigmoid,
                                   bias=par[:, col:col + 1]).then_inc(sigs, 1)
                act.wait_ge(keyed, hp + 1)
                act.activation(nrm[:], kk[:], ACT.Square).then_inc(squared, 1)
                act.wait_ge(floored, hp + 1)
                act.activation(nrm[:], nrm[:], ACT.Sqrt).then_inc(rooted, 1)
                for d in range(2):
                    act.wait_ge(gate_in, 2 * hp + d + 1)
                    act.activation(gates[:, d, ds(hp, 1), :].rearrange("p a c -> p (a c)"), nxt[:, d, :],
                                   ACT.Exp, scale=-DECAY).then_inc(gated, 1)
                    act.wait_ge(xy, 2 * hp + d + 1)
                    if d == 0:
                        act.activation(E[:], X[:], ACT.Exp, scale=DECAY).then_inc(exps, 1)
                        act.wait_ge(exps, 6 * hp + 1)
                        act.activation(X[:], X[:], ACT.Exp, scale=-DECAY).then_inc(exps, 1)
                        act.activation(Y[:], Y[:], ACT.Exp, scale=-DECAY).then_inc(exps, 1)
                    else:
                        act.activation(E[:], Y[:], ACT.Exp, scale=-DECAY).then_inc(exps, 1)
                        act.wait_ge(exps, 6 * hp + 4)
                        act.activation(Y[:], Y[:], ACT.Exp, scale=DECAY).then_inc(exps, 1)
                        act.activation(X[:], X[:], ACT.Exp, scale=DECAY).then_inc(exps, 1)
                act.wait_ge(g_prod, hp + 1)
                act.wait_ge(bonus_in, hp + 1)
                act.copy(slot(0, hp), ps[:, 4 * HALF:6 * HALF]).then_inc(g_out, 1)

        @block.vector
        def _(dve):
            per_pair = 16
            n = [0]
            dve.wait_ge(par_in, 16)
            dve.wait_ge(scans_ready, 2)
            with dve.Fori(0, HP) as hp:
                def link(ins):
                    n[0] += 1
                    ins.then_inc(links, 1)
                    dve.wait_ge(links, hp * per_pair + n[0])

                k, r, v = slot(4, hp), slot(0, hp), slot(8, hp)
                dve.wait_ge(bonus_out, hp)
                link(dve.tensor_copy(par[:, 0:NPAR], par_all[:, ds(hp, 1), :].rearrange("p a c -> p (a c)")))
                dve.tensor_scalar(par[:, KAC:KAC + 1], par[:, KA:KA + 1], -1.0, 1.0, ALU.mult, ALU.add
                                  ).then_inc(written, 1)
                dve.wait_ge(written, hp + 1)
                dve.tensor_scalar(kk[:], k, par[:, KKS:KKS + 1], None, ALU.mult).then_inc(keyed, 1)
                dve.wait_ge(summed, hp + 1)
                dve.tensor_scalar(nrm[:], ps[:, 0:2 * HALF], 1e-24, None, ALU.max).then_inc(floored, 1)
                dve.wait_ge(rooted, hp + 1)
                link(dve.reciprocal(nrm[:], nrm[:]))
                link(dve.tensor_tensor(kk[:], kk[:], nrm[:], ALU.mult))
                for d in range(2):
                    dve.wait_ge(sigs, 4 * hp + 4)
                    link(dve.tensor_tensor_scan(cs[:], reset[:], sg[d][:], 0.0, ALU.mult, ALU.add))
                    link(dve.tensor_scalar(half[:], by_chunk(cs)[:, :, CH - 1], 0.5, None, ALU.mult))
                    dve.wait_ge(gated, 2 * hp + d)
                    a0, b0 = (0, 1) if d == 0 else (1, 0)
                    dve.tensor_tensor(nxt[:, d, a0:a0 + NC - 1], half[:, 0:NC - 1], half[:, 1:NC], ALU.add)
                    edge = NC - 1 if d == 0 else 0
                    dve.tensor_copy(nxt[:, d, edge:edge + 1], half[:, edge:edge + 1]).then_inc(gate_in, 1)
                    link(dve.tensor_tensor(by_chunk(X), by_chunk(cs),
                                           half[:].unsqueeze(2).broadcast_to([P, NC, CH]), ALU.subtract))
                    dve.tensor_tensor(Y[:], X[:], sg[d][:], ALU.subtract).then_inc(xy, 1)
                    link(dve.tensor_scalar(kd[d][:], a[d][:], par[:, KA:KA + 1], par[:, KAC:KAC + 1],
                                           ALU.mult, ALU.add))
                    link(dve.tensor_tensor(kd[d][:], kd[d][:], k, ALU.mult))
                    link(dve.tensor_tensor(a[d][:], a[d][:], kk[:], ALU.mult))
                    eA, eR = (Y, X) if d == 0 else (X, Y)
                    dve.wait_ge(exps, 6 * hp + 3 * d + 3)
                    dve.wait_ge(stored[d], 32 * hp)
                    dve.scalar_tensor_tensor(st[d][:, :, 1, :], by_chunk(kk), -1.0, by_chunk(eA),
                                             ALU.mult, ALU.mult).then_inc(staged[d], 1)
                    dve.tensor_tensor(st[d][:, :, 0, :], r.rearrange("p (c t) -> p c t", t=CH), by_chunk(eR),
                                      ALU.mult).then_inc(staged[d], 1)
                    dve.tensor_tensor(st[d][:, :, 2, :], by_chunk(a[d]), by_chunk(E), ALU.mult
                                      ).then_inc(staged[d], 1)
                    dve.tensor_tensor(st[d][:, :, 3, :], by_chunk(kd[d]), by_chunk(E), ALU.mult
                                      ).then_inc(staged[d], 1)
                    dve.wait_ge(staged[d], 4 * hp + 4)
                link(dve.tensor_tensor(kd[0][:], kd[0][:], kd[1][:], ALU.add))
                dve.scalar_tensor_tensor(X[:], kd[0][:], par[:, RK:RK + 1], r, ALU.mult, ALU.mult
                                         ).then_inc(bonus_in, 1)
                dve.wait_ge(bonus_sum, hp + 1)
                dve.wait_ge(staged_v, 2 * hp + 2)
                dve.scalar_tensor_tensor(v, ps[:, 2 * HALF:4 * HALF], 0.5, v, ALU.mult, ALU.mult
                                         ).then_inc(bonus_out, 1)
            assert n[0] == per_pair


def run_chunks(nc, ps, feat, mixT, consts, chunks, gates, tri, tri_l):
    ident = consts["ident"]
    G = 2 * HP
    LEVELS = 5
    with ExitStack() as ctx:
        sb, sem = allocator(nc, ctx, "rc_"), semaphores(nc, ctx, "rc_")
        stk = [sb(f"stk{b}", [P, G, 3, CH]) for b in range(2)]
        dia = [sb(f"dia{b}", [P, G, 4, P]) for b in range(2)]
        tri_s = sb("tri_s", [P, 2, 2, CH])
        tril_s = sb("tril_s", [P, 2, CH])
        eye = sb("eye", [P, CH])

        def stacked(name):
            return sb(name, [P, G, CH])

        def diagonal(name):
            return sb(name, [P, G, P])

        def in_slot(of, f):
            return of[:, f * SEQ:(f + 1) * SEQ].rearrange("p (g c) -> p g c", c=P)
        flat = mixT[:].rearrange("p k t -> p (k t)")
        nt_s, l_s, x_s, z_s, u_s, s_s = (stacked(n) for n in ("nt_s", "l_s", "x_s", "z_s", "u_s", "s_s"))
        nt_d, l_d, x_d, u_d, s_d = (diagonal(n) for n in ("nt_d", "l_d", "x_d", "u_d", "s_d"))
        rb_s, rk_s, v_s, r_s = ([stacked(f"{n}{b}") for b in range(2)] for n in ("rb_s", "rk_s", "v_s", "r_s"))
        mt_d = [diagonal(f"mt_d{b}") for b in range(2)]
        v_d, b_d = ([in_slot(flat, f + b) for b in range(2)] for f in (0, 2))
        k_d, a_d = ([in_slot(feat, f + b) for b in range(2)] for f in (12, 14))
        gs = sb("gs", [P, G])
        names = ("consts_in cleared made nt_masked seeded masked v_ready turned natural kept squares l_dia "
                 "nt_ready l_stk xprod xadded x_ready z_made z_copied u_made u_copied u_dia y_made "
                 "y_copied s_made gs_ready updated state apart")
        (consts_in, cleared, made, nt_masked, seeded, masked, v_ready, turned, natural, kept, squares, l_dia,
         nt_ready, l_stk, xprod, xadded, x_ready, z_made, z_copied, u_made, u_copied, u_dia, y_made,
         y_copied, s_made, gs_ready, updated, state, apart) = (sem(n) for n in names.split())
        loaded = [sem(f"loaded{b}") for b in range(2)]
        block = ctx.enter_context(nc.Block())
        loads = 16 * 2 * (1 + 2 * HP)

        def bank(n, k=1):
            return ps[:, n * HALF:(n + k) * HALF]

        def pairs(ap, w=CH):
            return ap.rearrange("p (g c) -> p g c", c=w)

        def blocks(ap, s):
            rows = ap[s * HD:(s + 1) * HD]
            return rows if ap.shape[2] == CH else rows[:, :, s * CH:(s + 1) * CH]

        def atleast(eng, sem, value):
            if not isinstance(value, int) or value > 0:
                eng.wait_ge(sem, value)

        def steps(eng, step):
            step(0, 0, True, False)
            with eng.Fori(0, (NC - 2) // 2) as j:
                for b in (1, 0):
                    step(2 * j + 2 - b, b, True, True)
            step(NC - 1, 1, True, True)
            step(NC, 0, False, True)

        def by_two(t, b):
            if isinstance(t, int):
                return loads * (t // 2 + 1)
            return (t + 2 - b) * (loads // 2)

        @block.sync
        def _(sp):
            for to, of in ((tri_s, tri), (tril_s, tri_l), (eye, consts["eye"])):
                sp.dma_start(to[:], of).then_inc(consts_in, 16)
            sp.wait_ge(cleared, 1)

            def load(t, back, b):
                for d in range(2):
                    of = chunks[d, ds(back if d else t, 1)].rearrange("o p (h x t) -> p (o h) x t", x=XS, t=CH)
                    sp.dma_start(stk[b][:, d * HP:(d + 1) * HP], of[:, :, 0:3]).then_inc(loaded[b], 16)
                    for s in range(2):
                        for h in range(HP):
                            sp.dma_start(dia[b][s * HD:(s + 1) * HD, d * HP + h, :, s * CH:(s + 1) * CH],
                                         of[s * HD:(s + 1) * HD, h, 1:5]).then_inc(loaded[b], 16)
            for b in range(2):
                load(b, NC - 1 - b, b)
            with sp.Fori(1, NC // 2) as j:
                for b in range(2):
                    sp.wait_ge(turned, 4 * j + 2 * b - 2)
                    sp.wait_ge(kept, 4 * j + 2 * b - 2)
                    load(2 * j + b, NC - 1 - b - 2 * j, b)

        @block.gpsimd
        def _(pool):
            for t in (nt_d, l_d, x_d, *mt_d, u_d, s_d):
                pool.memset(t[:], 0.0)
            pool.memset(s_s[:], 0.0)
            for b in range(2):
                last = pool.memset(dia[b][:], 0.0)
            last.then_inc(cleared, 1)

            def step(t, b, prepares, advances):
                if prepares:
                    atleast(pool, y_made, t - 1)
                    pool.wait_ge(loaded[b], by_two(t, b))
                    pool.sem_inc(apart, 1)
                    pool.tensor_copy(r_s[b][:], stk[b][:, :, 0, :]).then_inc(kept, 1)
                    pool.tensor_copy(a_d[b], dia[b][:, :, 0, :]).then_inc(kept, 1)
            steps(pool, step)

        @block.tensor
        def _(pe):
            pe.wait_ge(cleared, 1)

            def each_pair(n, w, lhs, rhs):
                for g in range(G):
                    last = pe.matmul(ps[:, n * HALF + g * w:n * HALF + (g + 1) * w], lhs(g), rhs(g),
                                     start=True, stop=True)
                return last

            def turn(n, lhs):
                for g in range(G):
                    last = pe.transpose(ps[:, n * HALF + g * P:n * HALF + (g + 1) * P], lhs(g), ident[:])
                return last

            def products(t, b):
                S, Dg = stk[b], dia[b]
                pe.wait_ge(loaded[b], by_two(t, b))
                atleast(pe, y_copied, t - 1)
                atleast(pe, state, t - 1)
                atleast(pe, x_ready, t)
                each_pair(0, P, lambda g: Dg[:, g, 1, :], lambda g: S[:, g, 0:2, :]).then_inc(made, 1)
                each_pair(4, CH, lambda g: Dg[:, g, 0, :], lambda g: S[:, g, 2, :]).then_inc(made, 1)
                each_pair(2, P, lambda g: Dg[:, g, 2, :], lambda g: S[:, g, 0:2, :]).then_inc(made, 1)
                turn(5, lambda g: Dg[:, g, 3, :]).then_inc(made, 1)

            def naturals(t, b):
                Dg = dia[b]
                pe.wait_ge(masked, t + 1)
                turn(2, lambda g: Dg[:, g, 1, :]).then_inc(turned, 1)
                pe.wait_ge(v_ready, t + 1)
                turn(5, lambda g: Dg[:, g, 2, :]).then_inc(turned, 1)

            def level(t, k):
                if k == 0:
                    pe.wait_ge(seeded, t + 1)
                else:
                    pe.wait_ge(l_dia, LEVELS * t + k)
                    pe.wait_ge(xadded, LEVELS * t + k)
                    each_pair(4, CH, lambda g: l_d[:, g, :], lambda g: x_s[:, g, :]).then_inc(xprod, 1)
                if k == LEVELS:
                    return
                if k:
                    pe.wait_ge(nt_ready, 4 * t + k)
                    pe.wait_ge(l_stk, 4 * t + k)
                last = each_pair(1, CH, lambda g: nt_d[:, g, :], lambda g: l_s[:, g, :])
                if k < LEVELS - 1:
                    last = each_pair(0, CH, lambda g: l_d[:, g, :], lambda g: nt_s[:, g, :])
                last.then_inc(squares, 1)

            def sums(n, *terms):
                for g in range(G):
                    for i, (lhs, rhs) in enumerate(terms):
                        last = pe.matmul(ps[:, n * HALF + g * CH:n * HALF + (g + 1) * CH],
                                         lhs if lhs is ident_all else lhs[:, g, :], rhs[:, g, :],
                                         start=(i == 0), stop=(i == len(terms) - 1))
                return last
            ident_all = ident[:]

            def step(t, b, prepares, advances):
                p, o = t - 1, 1 - b
                if prepares:
                    products(t, b)
                    naturals(t, b)
                    level(t, 0)
                if advances:
                    if prepares:
                        pe.wait_ge(natural, 2 * t + 2)
                    pe.wait_ge(kept, 2 * t)
                    atleast(pe, state, p)
                    sums(2, (mt_d[o], v_s[o]), (a_d[o], s_s)).then_inc(z_made, 1)
                if prepares:
                    level(t, 1)
                if advances:
                    pe.wait_ge(z_copied, p + 1)
                    pe.wait_ge(x_ready, p + 1)
                    sums(3, (x_d, z_s)).then_inc(u_made, 1)
                if prepares:
                    level(t, 2)
                if advances:
                    pe.wait_ge(u_dia, p + 1)
                    sums(5, (s_d, r_s[o]), (v_d[o], rk_s[o]), (u_d, rb_s[o])).then_inc(y_made, 1)
                if prepares:
                    level(t, 3)
                if advances:
                    pe.wait_ge(u_copied, p + 1)
                    sums(6, (ident_all, s_s), (k_d[o], v_s[o]), (b_d[o], u_s)).then_inc(s_made, 1)
                if prepares:
                    level(t, 4)
                    level(t, 5)
            steps(pe, step)

        @block.vector
        def _(dve):
            dve.wait_ge(consts_in, 48)
            dve.wait_ge(cleared, 1)

            def tri_of(rows, x):
                return tri_s[rows, :, x, :].unsqueeze(2).broadcast_to([rows.stop - rows.start, 2, HP, CH])

            def tril_of(rows):
                return tril_s[rows].unsqueeze(2).broadcast_to([rows.stop - rows.start, 2, HP, CH])

            def by_dir(ap):
                return ap.rearrange("p (d h) c -> p d h c", d=2)

            def part(base, x):
                return bank(base, 2).rearrange("p (d h x c) -> p d h x c", d=2, x=2, c=CH)[:, :, :, x, :]
            every = slice(0, P)
            halves = [slice(s * HD, (s + 1) * HD) for s in range(2)]

            def mask_products(t, b):
                dve.wait_ge(made, 4 * t + 1)
                dve.tensor_tensor(by_dir(nt_s[:]), part(0, 1), tri_of(every, 1), ALU.mult).then_inc(nt_masked, 1)
                dve.tensor_tensor(by_dir(rb_s[b][:]), part(0, 0), tri_of(every, 0), ALU.mult)
                dve.wait_ge(made, 4 * t + 2)
                for s, rows in enumerate(halves):
                    dve.tensor_tensor(by_dir(blocks(l_d, s)), by_dir(pairs(bank(4)))[rows], tril_of(rows), ALU.mult)
                dve.tensor_tensor(by_dir(l_s[:]), by_dir(pairs(bank(4))), tril_of(every), ALU.mult)
                dve.wait_ge(nt_masked, t + 1)
                for s in range(2):
                    last = dve.tensor_copy(blocks(nt_d, s), blocks(nt_s, s))
                last.then_inc(seeded, 1)
                dve.tensor_tensor(x_s[:], nt_s[:], eye[:].unsqueeze(1).broadcast_to([P, G, CH]), ALU.add
                                  ).then_inc(xadded, 1)
                dve.wait_ge(made, 4 * t + 3)
                for s, rows in enumerate(halves):
                    dve.tensor_tensor(by_dir(blocks(mt_d[b], s)), part(2, 1)[rows], tri_of(rows, 1), ALU.mult)
                dve.tensor_tensor(by_dir(rk_s[b][:]), part(2, 0), tri_of(every, 0), ALU.mult).then_inc(masked, 1)

            def keep_squares(t, k):
                dve.wait_ge(squares, LEVELS * t + k)
                if k < LEVELS - 1:
                    dve.tensor_copy(nt_s[:], pairs(bank(0)))
                for s in range(2):
                    last = dve.tensor_copy(blocks(nt_d, s), pairs(bank(0))[halves[s]])
                last.then_inc(nt_ready, 1)

            def add_level(t, k):
                dve.wait_ge(xprod, LEVELS * t + k)
                dve.wait_ge(xadded, LEVELS * t + k)
                if k < LEVELS:
                    dve.tensor_tensor(x_s[:], x_s[:], pairs(bank(4)), ALU.add).then_inc(xadded, 1)
                    return
                for s in range(2):
                    last = dve.tensor_tensor(blocks(x_d, s), blocks(x_s, s), pairs(bank(4))[halves[s]], ALU.add)
                last.then_inc(x_ready, 1)

            def step(t, b, prepares, advances):
                p = t - 1
                if prepares:
                    mask_products(t, b)
                    keep_squares(t, 1)
                if advances:
                    dve.wait_ge(z_made, p + 1)
                    dve.tensor_copy(z_s[:], pairs(bank(2))).then_inc(z_copied, 1)
                if prepares:
                    add_level(t, 1)
                    keep_squares(t, 2)
                    add_level(t, 2)
                    keep_squares(t, 3)
                    add_level(t, 3)
                    keep_squares(t, 4)
                if advances:
                    dve.tensor_copy(gs[:, 0:HP].unsqueeze(2), gates[:, 0, :, ds(p, 1)]).then_inc(gs_ready, 1)
                    dve.tensor_copy(gs[:, HP:G].unsqueeze(2), gates[:, 1, :, ds(NC - 1 - p, 1)]
                                    ).then_inc(gs_ready, 1)
                    dve.wait_ge(s_made, p + 1)
                    dve.wait_ge(gs_ready, 2 * p + 2)
                    dve.tensor_tensor(s_s[:], pairs(bank(6)), gs[:].unsqueeze(2).broadcast_to([P, G, CH]),
                                      ALU.mult).then_inc(updated, 1)
                    dve.wait_ge(updated, p + 1)
                    for s in range(2):
                        last = dve.tensor_copy(blocks(s_d, s), blocks(s_s, s))
                    last.then_inc(state, 1)
                if prepares:
                    add_level(t, 4)
                    add_level(t, 5)
            steps(dve, step)

        @block.scalar
        def _(act):
            halves = [slice(s * HD, (s + 1) * HD) for s in range(2)]

            def keep_squares(t, k):
                act.wait_ge(squares, LEVELS * t + k)
                for s in range(2):
                    last = act.copy(blocks(l_d, s), pairs(bank(1))[halves[s]])
                last.then_inc(l_dia, 1)
                if k < LEVELS:
                    act.copy(l_s[:], pairs(bank(1))).then_inc(l_stk, 1)

            def step(t, b, prepares, advances):
                p = t - 1
                if prepares:
                    act.wait_ge(made, 4 * t + 4)
                    act.copy(v_d[b], pairs(bank(5, 2), P))
                    for s in range(2):
                        last = act.copy(blocks(v_s[b], s), pairs(bank(5, 2), P)[halves[s], :, s * CH:(s + 1) * CH])
                    last.then_inc(v_ready, 1)
                    act.wait_ge(turned, 2 * t + 1)
                    act.copy(b_d[b], pairs(bank(2, 2), P)).then_inc(natural, 1)
                    act.wait_ge(turned, 2 * t + 2)
                    act.copy(k_d[b], pairs(bank(5, 2), P)).then_inc(natural, 1)
                    keep_squares(t, 1)
                    keep_squares(t, 2)
                if advances:
                    act.wait_ge(u_made, p + 1)
                    for s in range(2):
                        last = act.copy(blocks(u_d, s), pairs(bank(3))[halves[s]])
                    last.then_inc(u_dia, 1)
                    act.copy(u_s[:], pairs(bank(3))).then_inc(u_copied, 1)
                if prepares:
                    keep_squares(t, 3)
                if advances:
                    act.wait_ge(y_made, p + 1)
                    act.copy(feat[:].rearrange("p (f t) -> p f t", t=SEQ)[:, 4:8, ds(p * CH, CH)],
                             pairs(bank(5))[:, 0:HP])
                    act.copy(mixT[:, 4:8, ds((NC - 1) * CH - p * CH, CH)], pairs(bank(5))[:, HP:G]
                             ).then_inc(y_copied, 1)
                if prepares:
                    keep_squares(t, 4)
                    keep_squares(t, 5)
            steps(act, step)


def finish_rwkv(nc, ps, feat, mixT, consts, params):
    ones = consts["ones"]
    with ExitStack() as ctx:
        sb, sem = allocator(nc, ctx, "fr_"), semaphores(nc, ctx, "fr_")
        par_all = sb("par_all", [P, HP, NPAR])
        par = sb("par", [P, NPAR])
        y = sb("y", [P, SEQ])
        sq = sb("sq", [P, SEQ])
        names = "par_in links added mean_made centred squared var_made floored rooted"
        (par_in, links, added, mean_made, centred, squared, var_made, floored,
         rooted) = (sem(n) for n in names.split())
        block = ctx.enter_context(nc.Block())

        def slot(f, hp):
            return feat[:, ds((f + hp) * SEQ, SEQ)]

        def mixed(hp):
            return mixT[:].rearrange("p k t -> p (k t)")[:, ds((4 + hp) * SEQ, SEQ)]

        @block.sync
        def _(sp):
            sp.dma_start(par_all[:], params).then_inc(par_in, 16)
            sp.wait_ge(par_in, 16)

        def head_sums(pe, base, of, done):
            for h in range(2):
                last = pe.matmul(ps[:, (base + h) * HALF:(base + h + 1) * HALF], ones[:],
                                 of[:, h * HALF:(h + 1) * HALF], start=True, stop=True)
            last.then_inc(done, 1)

        @block.tensor
        def _(pe):
            with pe.Fori(0, HP) as hp:
                pe.wait_ge(added, hp + 1)
                head_sums(pe, 0, y, mean_made)
                pe.wait_ge(squared, hp + 1)
                head_sums(pe, 2, sq, var_made)

        @block.scalar
        def _(act):
            with act.Fori(0, HP) as hp:
                act.wait_ge(centred, hp + 1)
                act.activation(sq[:], y[:], ACT.Square).then_inc(squared, 1)
                act.wait_ge(floored, hp + 1)
                act.activation(sq[:], sq[:], ACT.Sqrt).then_inc(rooted, 1)

        @block.vector
        def _(dve):
            per_pair = 6
            dve.wait_ge(par_in, 16)
            with dve.Fori(0, HP) as hp:
                n = [0]

                def link(ins):
                    n[0] += 1
                    ins.then_inc(links, 1)
                    dve.wait_ge(links, hp * per_pair + n[0])

                link(dve.tensor_copy(par[:], par_all[:, ds(hp, 1), :].rearrange("p a c -> p (a c)")))
                dve.tensor_tensor(y[:], slot(4, hp), mixed(hp), ALU.add).then_inc(added, 1)
                dve.wait_ge(mean_made, hp + 1)
                dve.wait_ge(added, hp + 1)
                dve.scalar_tensor_tensor(y[:], ps[:, 0:2 * HALF], -1.0 / HD, y[:], ALU.mult, ALU.add
                                         ).then_inc(centred, 1)
                dve.wait_ge(var_made, hp + 1)
                dve.tensor_scalar(sq[:], ps[:, 2 * HALF:4 * HALF], 1.0 / HD, GN_EPS, ALU.mult, ALU.add
                                  ).then_inc(floored, 1)
                dve.wait_ge(rooted, hp + 1)
                link(dve.reciprocal(sq[:], sq[:]))
                link(dve.tensor_tensor(y[:], y[:], sq[:], ALU.mult))
                link(dve.tensor_scalar(y[:], y[:], par[:, LNG:LNG + 1], par[:, LNB:LNB + 1], ALU.mult, ALU.add))
                link(dve.tensor_tensor(y[:], y[:], slot(8, hp), ALU.add))
                link(dve.tensor_tensor(mixed(hp), y[:], slot(0, hp), ALU.mult))
                assert n[0] == per_pair


class Norm:

    def __init__(self, sb, sem, name, apart):
        self.parts = sb(name + "_parts", [P, 2, 6])
        self.stat = sb(name + "_stat", [P, 4])
        self.summed, self.rooted = sem(name + "_summed"), sem(name + "_rooted")
        self.apart = apart

    def on_vector(self, dve, link, t, g, b, count):
        for h in range(2):
            last = dve.bn_stats(self.parts[:, h, :], t[:, h * HALF:(h + 1) * HALF])
        link(last)
        dve.sem_inc(self.apart, 1)
        link(dve.bn_aggr(self.stat[:, 0:2], self.parts[:]))
        dve.tensor_scalar(self.stat[:, 2:3], self.stat[:, 1:2], LN_EPS, None, ALU.add).then_inc(self.summed, 1)
        dve.wait_ge(self.rooted, count + 1)
        link(dve.reciprocal(self.stat[:, 2:3], self.stat[:, 3:4]))
        link(dve.tensor_scalar(t[:], t[:], self.stat[:, 0:1], self.stat[:, 2:3], ALU.subtract, ALU.mult))
        link(dve.tensor_tensor(t[:], t[:], g[:], ALU.mult))
        return dve.tensor_tensor(t[:], t[:], b[:], ALU.add)

    LINKS = 5

    def on_scalar(self, act, count):
        act.wait_ge(self.summed, count + 1)
        act.activation(self.stat[:, 3:4], self.stat[:, 2:3], ACT.Sqrt).then_inc(self.rooted, 1)


def mix_and_norm(nc, ps, mixT, h, consts, x, w_out, ln, attended):
    ident = consts["ident"]
    with ExitStack() as ctx:
        sb, sem = allocator(nc, ctx, "mx_"), semaphores(nc, ctx, "mx_")
        w = sb("w", [P, KT, D])
        lhs = sb("lhs", [P, KT, P])
        xt = [sb(f"xt{b}", [P, D]) for b in range(2)]
        t = sb("t", [P, D])
        g_b = [sb(n, [P, D]) for n in ("g", "b")]
        w_in, ln_in, staged, product, links = (sem(n) for n in ("w_in", "ln_in", "staged", "product", "links"))
        summed, normed, turned, kept, mix_in = (sem(n) for n in ("summed", "normed", "turned", "kept", "mix_in"))
        x_in = [sem(f"x_in{b}") for b in range(2)]
        apart = sem("apart")
        norm = Norm(sb, sem, "ln", apart)
        block = ctx.enter_context(nc.Block())

        @block.sync
        def _(sp):
            sp.dma_start(mixT[:, 0:4, :], attended).then_inc(mix_in, 16)
            sp.dma_start(w[:], w_out).then_inc(w_in, 16)
            for i in range(2):
                sp.dma_start(g_b[i][:], ln[i].partition_broadcast(P)).then_inc(ln_in, 16)
            with sp.Fori(0, TT // 2) as j:
                for b in range(2):
                    sp.wait_ge(summed, 2 * j)
                    sp.dma_start(xt[b][:], x[ds((2 * j + b) * P, P), :]).then_inc(x_in[b], 16)

        @block.gpsimd
        def _(pool):
            pool.wait_ge(mix_in, 16)
            with pool.Fori(0, TT) as i:
                pool.wait_ge(product, i)
                pool.sem_inc(apart, 1)
                pool.tensor_copy(lhs[:], mixT[:, :, ds(i * P, P)]).then_inc(staged, 1)

        @block.tensor
        def _(pe):
            pe.wait_ge(w_in, 16)
            with pe.Fori(0, TT) as i:
                pe.wait_ge(staged, i + 1)
                pe.wait_ge(summed, i)
                for n in range(2):
                    for k in range(KT):
                        last = pe.matmul(ps[:, n * HALF:(n + 1) * HALF], lhs[:, k, :],
                                         w[:, k, n * HALF:(n + 1) * HALF], start=(k == 0), stop=(k == KT - 1))
                last.then_inc(product, 1)
                pe.wait_ge(normed, i + 1)
                pe.wait_ge(kept, i)
                for k in range(KT):
                    last = pe.transpose(ps[:, 2 * HALF + k * P:2 * HALF + (k + 1) * P],
                                        t[:, k * P:(k + 1) * P], ident[:])
                last.then_inc(turned, 1)

        @block.scalar
        def _(act):
            with act.Fori(0, TT) as i:
                norm.on_scalar(act, i)
                act.wait_ge(normed, i + 1)
                act.copy(h[:, ds(i * D, D)], t[:])
                act.wait_ge(turned, i + 1)
                act.copy(mixT[:, :, ds(i * P, P)],
                         ps[:, 2 * HALF:4 * HALF].rearrange("p (k t) -> p k t", t=P)).then_inc(kept, 1)

        @block.vector
        def _(dve):
            dve.wait_ge(ln_in, 32)
            with dve.Fori(0, TT // 2) as j:
                n = [0]

                def link(ins):
                    n[0] += 1
                    ins.then_inc(links, 1)
                    dve.wait_ge(links, j * 2 * Norm.LINKS + n[0])

                for b in range(2):
                    i = 2 * j + b
                    dve.wait_ge(x_in[b], 16 * j + 16)
                    dve.wait_ge(product, i + 1)
                    dve.wait_ge(kept, i)
                    dve.scalar_tensor_tensor(t[:], xt[b][:], ALPHA, ps[:, 0:D], ALU.mult, ALU.add
                                             ).then_inc(summed, 1)
                    dve.wait_ge(summed, i + 1)
                    norm.on_vector(dve, link, t, *g_b, i).then_inc(normed, 1)
                assert n[0] == 2 * Norm.LINKS


def choose_experts(nc, ps, hT, idx, gate, consts, wq, keys):
    M = 2 * PH
    with ExitStack() as ctx:
        sb, sem = allocator(nc, ctx, "ex_"), semaphores(nc, ctx, "ex_")
        w = sb("w", [P, KT, M * P])
        ky = sb("ky", [P, M, NK])
        qT = sb("qT", [P, 4, P])
        sc = sb("sc", [P, M, NK])
        s16 = sb("s16", [P, PH, 2, TOPK])
        i16 = sb("i16", [P, PH, 2, TOPK], U32)
        f16 = sb("f16", [P, PH, 2, TOPK])
        cand = sb("cand", [P, PH, TOPK, TOPK])
        hot = sb("hot", [P, PH, TOPK, TOPK])
        best = sb("best", [P, PH, TOPK])
        at = sb("at", [P, PH, TOPK], U32)
        part = sb("part", [P, 2, PH, TOPK], U32)
        part_f = sb("part_f", [P, 2, PH, TOPK])
        row = sb("row", [P, 2, PH, TOPK])
        iota_i = sb("iota_i", [P, TOPK], U32)
        iota = sb("iota", [P, TOPK])
        total = sb("total", [P, 2, PH])
        names = "keys_in iota_made q_made q_copied sc_made sc_copied links centred expd chosen"
        (keys_in, iota_made, q_made, q_copied, sc_made, sc_copied, links, centred, expd,
         chosen) = (sem(n) for n in names.split())
        apart = sem("apart")
        w_in = [sem(f"w_in{k}") for k in range(4)]
        block = ctx.enter_context(nc.Block())

        @block.sync
        def _(sp):
            sp.dma_start(ky[:], keys).then_inc(keys_in, 16)
            for k in range(4):
                sp.dma_start(w[:, 2 * k:2 * k + 2, :], wq[:, 2 * k:2 * k + 2, :]).then_inc(w_in[k], 16)
            sp.wait_ge(keys_in, 16)

        @block.gpsimd
        def _(pool):
            pool.iota(iota_i[:], [[1, TOPK]], base=0, channel_multiplier=0).then_inc(iota_made, 1)
            pool.wait_ge(iota_made, 1)
            pool.tensor_copy(iota[:], iota_i[:]).then_inc(iota_made, 1)

        @block.tensor
        def _(pe):
            for k in range(4):
                pe.wait_ge(w_in[k], 16)
            pe.wait_ge(keys_in, 16)
            with pe.Fori(0, TT) as i:
                def query(m):
                    pe.wait_ge(q_copied, M * i + m - 3 if m >= 4 else M * i)
                    for k in range(KT):
                        last = pe.matmul(ps[:, (m % 4) * HALF:(m % 4) * HALF + P], w[:, k, m * P:(m + 1) * P],
                                         hT[:, k, ds(i * P, P)], start=(k == 0), stop=(k == KT - 1))
                    last.then_inc(q_made, 1)

                def score(m):
                    pe.wait_ge(q_copied, M * i + m + 1)
                    pe.wait_ge(sc_copied, M * i + m - 3 if m >= 4 else M * i)
                    pe.matmul(ps[:, (4 + m % 4) * HALF:(4 + m % 4) * HALF + NK], qT[:, m % 4, :], ky[:, m, :],
                              start=True, stop=True).then_inc(sc_made, 1)
                for m in range(M):
                    query(m)
                    if m:
                        score(m - 1)
                score(M - 1)

        def keep_score(act, i, m):
            if m == 0:
                act.wait_ge(centred, i)
            act.wait_ge(sc_made, M * i + m + 1)
            act.copy(sc[:, m, :], ps[:, (4 + m % 4) * HALF:(4 + m % 4) * HALF + NK]).then_inc(sc_copied, 1)

        @block.scalar
        def _(act):
            with act.Fori(0, TT) as i:
                for m in range(M):
                    act.wait_ge(q_made, M * i + m + 1)
                    act.wait_ge(sc_made, M * i + m - 3 if m >= 4 else M * i)
                    act.copy(qT[:, m % 4, :], ps[:, (m % 4) * HALF:(m % 4) * HALF + P]).then_inc(q_copied, 1)
                    if m:
                        keep_score(act, i, m - 1)
                keep_score(act, i, M - 1)
                act.wait_ge(centred, i + 1)
                act.activation(best[:], best[:], ACT.Exp).then_inc(expd, 1)

        @block.vector
        def _(dve):
            per_tile = 37
            dve.wait_ge(iota_made, 2)
            with dve.Fori(0, TT) as i:
                n = [0]

                def link(ins):
                    n[0] += 1
                    ins.then_inc(links, 1)
                    dve.wait_ge(links, i * per_tile + n[0])

                def top16(values, vals, idxs):
                    dve.sem_inc(apart, 1)
                    for v, o in zip(values, vals):
                        last = dve.max(o[:, 0:8], v)
                    link(last)
                    dve.sem_inc(apart, 1)
                    for v, o, p in zip(values, vals, idxs):
                        last = dve.max_index(p[:, 0:8], o[:, 0:8], v)
                    link(last)
                    dve.sem_inc(apart, 1)
                    for v, o in zip(values, vals):
                        last = dve.match_replace(v, o[:, 0:8], v, -3e38)
                    link(last)
                    dve.sem_inc(apart, 1)
                    for v, o in zip(values, vals):
                        last = dve.max(o[:, 8:16], v)
                    link(last)
                    dve.sem_inc(apart, 1)
                    for v, o, p in zip(values, vals, idxs):
                        last = dve.max_index(p[:, 8:16], o[:, 8:16], v)
                    link(last)

                for q in range(4):
                    ms = range(4 * q, 4 * q + 4)
                    dve.wait_ge(sc_copied, M * i + 4 * q + 4)
                    top16([sc[:, m, :] for m in ms], [s16[:, m // 2, m % 2, :] for m in ms],
                          [i16[:, m // 2, m % 2, :] for m in ms])
                dve.tensor_copy(f16[:], i16[:])
                link(dve.tensor_tensor(cand[:], s16[:, :, 0, :].unsqueeze(3).broadcast_to([P, PH, TOPK, TOPK]),
                                       s16[:, :, 1, :].unsqueeze(2).broadcast_to([P, PH, TOPK, TOPK]), ALU.add))
                top16([cand[:, e].rearrange("p a b -> p (a b)") for e in range(PH)],
                      [best[:, e, :] for e in range(PH)], [at[:, e, :] for e in range(PH)])
                dve.tensor_scalar(total[:, 0, :].unsqueeze(2), best[:, :, 0:1], 1.0, None, ALU.mult)
                dve.tensor_scalar(part[:, 0], at[:], 4, None, ALU.logical_shift_right)
                link(dve.tensor_scalar(part[:, 1], at[:], TOPK - 1, None, ALU.bitwise_and))
                dve.tensor_tensor(best[:], best[:], total[:, 0, :].unsqueeze(2).broadcast_to([P, PH, TOPK]),
                                  ALU.subtract).then_inc(centred, 1)
                link(dve.tensor_copy(part_f[:], part[:]))
                for x in range(2):
                    link(dve.tensor_tensor(hot[:], part_f[:, x].unsqueeze(3).broadcast_to([P, PH, TOPK, TOPK]),
                                           iota[:].unsqueeze(1).unsqueeze(1).broadcast_to([P, PH, TOPK, TOPK]),
                                           ALU.is_equal))
                    link(dve.tensor_tensor(hot[:], hot[:], f16[:, :, x, :].unsqueeze(2)
                                           .broadcast_to([P, PH, TOPK, TOPK]), ALU.mult))
                    link(dve.tensor_reduce(row[:, x], hot[:], AX.X, ALU.add))
                dve.scalar_tensor_tensor(idx[:, ds(i * NSEL, NSEL)], row[:, 0].rearrange("p h k -> p (h k)"),
                                         float(NK), row[:, 1].rearrange("p h k -> p (h k)"), ALU.mult, ALU.add)
                dve.wait_ge(expd, i + 1)
                link(dve.tensor_reduce(total[:, 0, :], best[:], AX.X, ALU.add))
                link(dve.reciprocal(total[:, 1, :], total[:, 0, :]))
                link(dve.tensor_tensor(gate[:, ds(i * NSEL, NSEL)].rearrange("p (h k) -> p h k", k=TOPK), best[:],
                                       total[:, 1, :].unsqueeze(2).broadcast_to([P, PH, TOPK]), ALU.mult))
                assert n[0] == per_tile, n[0]


def apply_experts(nc, ps, h, idx, gate, consts, u, v, ln, out):
    ident = consts["ident"]
    with ExitStack() as ctx:
        sb, sem = allocator(nc, ctx, "ap_"), semaphores(nc, ctx, "ap_")
        rows_u = sb("rows_u", [P, GRP, D])
        rows_v = sb("rows_v", [P, GRP, D])
        picks = [sb(f"picks{b}", [P, GRP], U32) for b in range(2)]
        z = sb("z", [P, 2, GRP])
        act_z = sb("act_z", [P, 2, GRP])
        wt = sb("wt", [P, 2, GRP])
        diag = sb("diag", [P, 2, GRP, P])
        zero = sb("zero", [P, P])
        keep = sb("keep", [P, P])
        hc = sb("hc", [P, D])
        t = sb("t", [P, D])
        g_b = [sb(n, [P, D]) for n in ("g", "b")]
        u_in = [sem(f"u_in{j}") for j in range(GRP)]
        v_in = [sem(f"v_in{j}") for j in range(GRP)]
        u_read = [sem(f"u_read{j}") for j in range(GRP)]
        v_read = [sem(f"v_read{j}") for j in range(GRP)]
        names = "ln_in ready picked h_copied bent weighted spread summed links normed stored copied"
        (ln_in, ready, picked, h_copied, bent, weighted, spread, summed, links, normed, stored,
         copied) = (sem(n) for n in names.split())
        apart = sem("apart")
        norm = Norm(sb, sem, "ln", apart)
        block = ctx.enter_context(nc.Block())
        HG = NG // 2

        @block.gpsimd
        def _(pool):
            pool.memset(zero[:], 0.0).then_inc(ready, 1)
            with pool.Fori(0, TT) as i:
                with pool.Fori(0, HG) as gg:
                    for b in range(2):
                        q = NG * i + 2 * gg + b
                        pool.wait_ge(v_in[GRP - 1], 16 * q)
                        pool.wait_ge(u_in[GRP - 1], 16 * q)
                        pool.sem_inc(apart, 1)
                        pool.tensor_copy(picks[b][:], idx[:, ds(i * NSEL + (2 * gg + b) * GRP, GRP)]
                                         ).then_inc(picked, 1)
                        pool.wait_ge(picked, q + 1)
                        pool.sem_inc(apart, 1)
                        for table, rows, landed, read in ((u, rows_u, u_in, u_read), (v, rows_v, v_in, v_read)):
                            for j in range(GRP):
                                pool.wait_ge(read[j], q)
                                pool.sem_inc(apart, 1)
                                pool.indirect_dma_start(
                                    out=rows[:, j, :], out_offset=None, in_=table,
                                    in_offset=bass.IndirectOffsetOnAxis(ap=picks[b][:, j:j + 1], axis=0),
                                ).then_inc(landed[j], 16)

        @block.sync
        def _(sp):
            for k in range(2):
                sp.dma_start(g_b[k][:], ln[k].partition_broadcast(P)).then_inc(ln_in, 16)
            with sp.Fori(0, TT) as i:
                sp.wait_ge(normed, i + 1)
                sp.dma_start(out[ds(i * P, P), :], t[:]).then_inc(stored, 16)
            sp.wait_ge(stored, 16 * TT)

        @block.vector
        def _(dve):
            dve.wait_ge(ln_in, 32)
            with dve.Fori(0, TT) as i:
                n = [0]

                def link(ins):
                    n[0] += 1
                    ins.then_inc(links, 1)
                    dve.wait_ge(links, i * Norm.LINKS + n[0])
                dve.tensor_copy(hc[:], h[:, ds(i * D, D)]).then_inc(h_copied, 1)
                dve.wait_ge(h_copied, i + 1)
                dve.sem_inc(apart, 1)
                with dve.Fori(0, HG) as gg:
                    for b in range(2):
                        q = NG * i + 2 * gg + b
                        for j in range(GRP):
                            dve.wait_ge(u_in[j], 16 * q + 16)
                            dve.tensor_tensor_reduce(rows_u[:, j, :], rows_u[:, j, :], hc[:], 1.0, 0.0,
                                                     ALU.mult, ALU.add, z[:, b, j:j + 1]).then_inc(u_read[j], 1)
                        dve.wait_ge(bent, q + 1)
                        dve.tensor_tensor(wt[:, b, :], act_z[:, b, :],
                                          gate[:, ds(i * NSEL + (2 * gg + b) * GRP, GRP)], ALU.mult
                                          ).then_inc(weighted, 1)
                dve.wait_ge(summed, i + 1)
                dve.wait_ge(stored, 16 * i)
                dve.tensor_copy(t[:], ps[:, 0:D]).then_inc(copied, 1)
                dve.wait_ge(copied, i + 1)
                norm.on_vector(dve, link, t, *g_b, i).then_inc(normed, 1)
                assert n[0] == Norm.LINKS

        @block.scalar
        def _(act):
            act.wait_ge(ready, 1)
            act.mul(keep[:], ident[:], ALPHA).then_inc(ready, 1)
            with act.Fori(0, TT) as i:
                with act.Fori(0, HG) as gg:
                    for b in range(2):
                        q = NG * i + 2 * gg + b
                        act.wait_ge(u_read[GRP - 1], q + 1)
                        act.activation(act_z[:, b, :], z[:, b, :], ACT.Gelu).then_inc(bent, 1)
                        act.wait_ge(weighted, q + 1)
                        for j in range(GRP):
                            act.activation(diag[:, b, j, :], ident[:], ACT.Copy, scale=wt[:, b, j:j + 1]
                                           ).then_inc(spread, 1)
                norm.on_scalar(act, i)

        @block.tensor
        def _(pe):
            pe.wait_ge(ready, 2)
            with pe.Fori(0, TT) as i:
                pe.wait_ge(copied, i)
                for n in range(2):
                    pe.matmul(ps[:, n * HALF:(n + 1) * HALF], zero[:], h[:, ds(i * D + n * HALF, HALF)],
                              start=True, stop=False)
                with pe.Fori(0, HG) as gg:
                    for b in range(2):
                        q = NG * i + 2 * gg + b
                        for j in range(GRP):
                            pe.wait_ge(v_in[j], 16 * q + 16)
                            pe.wait_ge(spread, GRP * q + j + 1)
                            for n in range(2):
                                last = pe.matmul(ps[:, n * HALF:(n + 1) * HALF], diag[:, b, j, :],
                                                 rows_v[:, j, n * HALF:(n + 1) * HALF], start=False, stop=False)
                            last.then_inc(v_read[j], 1)
                for n in range(2):
                    last = pe.matmul(ps[:, n * HALF:(n + 1) * HALF], keep[:], h[:, ds(i * D + n * HALF, HALF)],
                                     start=False, stop=True)
                last.then_inc(summed, 1)


def program(nc, x, x_t, w_tiles, rope, masks, sink, perm, mu, low_rank, params, tri, tri_l, eye, ident_in,
            ones_in, w_out, ln1, wq, keys, u, v, ln2, out):
    with ExitStack() as ctx:
        sb = allocator(nc, ctx)
        ps = ctx.enter_context(nc.psum_tensor("ps", [P, 8 * HALF], F32))
        banks = [ps[:, n * HALF:(n + 1) * HALF] for n in range(8)]
        mixT = sb("mixT", [P, KT, SEQ])
        ident = sb("ident", [P, P])
        ones = sb("ones", [P, P])
        chunks = nc.dram_tensor("chunks", [2, NC, P, HP * XS * CH], F32, kind="Internal").ap()
        attended = nc.dram_tensor("attended", [P, 4, SEQ], F32, kind="Internal").ap()
        consts = {"ident": ident, "ones": ones, "eye": eye}
        consts_in = ctx.enter_context(nc.semaphore("consts_in"))
        with nc.Block() as block:
            @block.sync
            def _(sp):
                sp.dma_start(ident[:], ident_in).then_inc(consts_in, 16)
                sp.dma_start(ones[:], ones_in).then_inc(consts_in, 16)
                sp.wait_ge(consts_in, 32)
        with ExitStack() as mixer:
            msb = allocator(nc, mixer)
            feat = msb("feat", [P, 16 * SEQ])
            with ExitStack() as attention:
                asb = allocator(nc, attention)
                at = asb("at", [P, NAT * SEQ])
                with ExitStack() as projection:
                    xT = allocator(nc, projection)("xT", [P, KT, SEQ])
                    project(nc, banks, x_t, w_tiles, xT, ((feat[:, SEQ:], NFT), (at, NAT)), "pr_")
                attend(nc, banks, at, mixT, consts, rope, masks, sink, perm, attended)
            gates = msb("gates", [P, 2, HP, NC])
            shift_tokens(nc, feat, mu)
            prepare_chunks(nc, ps, feat, consts, low_rank, params, chunks, gates)
            run_chunks(nc, ps, feat, mixT, consts, chunks, gates, tri, tri_l)
            finish_rwkv(nc, ps, feat, mixT, consts, params)
        h = sb("h", [P, TT * D])
        idx = sb("idx", [P, TT * NSEL], U32)
        gate = sb("gate", [P, TT * NSEL])
        mix_and_norm(nc, ps, mixT, h, consts, x, w_out, ln1, attended)
        choose_experts(nc, ps, mixT, idx, gate, consts, wq, keys)
        apply_experts(nc, ps, h, idx, gate, consts, u, v, ln2, out)


def constants():
    f = np.float32
    pos = np.arange(SEQ, dtype=f)
    inv = f(10000.0) ** (-np.arange(0, HD, 2, dtype=f) / f(HD))
    ang = np.concatenate([pos[:, None] * inv[None, :]] * 2, -1).astype(f)
    cos, sin = np.cos(ang).T, np.sin(ang).T.copy()
    sin[:HD // 2] *= -1
    rope = np.stack([np.tile(cos, (2, 1)), np.tile(sin, (2, 1))]).astype(f)
    perm = np.zeros((P, P), f)
    for m in range(P):
        perm[m // HD * HD + (m % HD + HD // 2) % HD, m] = 1
    q, k = np.arange(P)[:, None], np.arange(WIN)[None] - P
    masks = np.zeros((P, TT, WIN), f)
    for n in range(TT):
        at = k + n * P
        masks[:, n] = np.where((abs(q - k) <= P) & (at >= 0) & (at < SEQ), 0, NEG)
    j, t = np.meshgrid(np.arange(CH), np.arange(CH), indexing="ij")
    tri = np.stack([np.stack([j <= t, j < t], 1), np.stack([j >= t, j > t], 1)], 1).astype(f)
    tri_l = np.stack([j > t, j < t], 1).astype(f)
    pair = np.kron(np.eye(2, dtype=f), np.ones((HD, HD), f))
    return {"rope": rope, "masks": masks, "perm": perm, "tri": np.tile(tri, (2, 1, 1, 1)),
            "tri_l": np.tile(tri_l, (2, 1, 1)), "eye": np.tile(np.eye(CH, dtype=f), (2, 1)),
            "ident_in": np.eye(P, dtype=f), "ones_in": pair}


def layouts(inp):
    f = np.float32
    o = {"x": inp["x"][0]}
    o["x_t"] = np.ascontiguousarray(inp["x"][0].T.reshape(KT, P, SEQ).transpose(1, 0, 2))
    attn = (NH + 2 * 2) * HD
    n_rwkv = inp["mu_prev"].shape[-1]
    pair_cols = [c for p in range(NH // 2) for s in range(2) for c in range((4 * s + p) * HD, (4 * s + p + 1) * HD)]
    order = list(range(attn, attn + n_rwkv)) + [-1] * (NFT * P - n_rwkv) + pair_cols + list(range(NH * HD, attn))
    w = np.concatenate([inp["w_in"][0], np.zeros((D, 1), f)], 1)[:, order]
    o["w_tiles"] = np.ascontiguousarray(w.reshape(KT, P, NFT + NAT, P).transpose(2, 1, 0, 3))
    mu = np.zeros((2, NFT * P), f)
    mu[0, :n_rwkv], mu[1, :n_rwkv] = inp["mu_prev"][0], inp["mu_next"][0]
    o["mu"] = np.ascontiguousarray(mu.reshape(2, NFT, P).transpose(0, 2, 1))
    lr = np.zeros((HP, P, 5, P), f)
    for hp in range(HP):
        c = slice(hp * P, hp * P + P)
        for n, part in enumerate((inp["w2"][0, 0], inp["w2"][0, 1], inp["a2"][0, 0], inp["a2"][0, 1])):
            lr[hp, 32 * n:32 * n + 32, n] = part[:, c]
        lr[hp, :inp["g2"].shape[1], 4] = inp["g2"][0][:, c]
    o["low_rank"] = lr
    cols = [inp["w0"][0, 0], inp["w0"][0, 1], inp["a0"][0, 0], inp["a0"][0, 1], inp["k_k"][0], inp["k_a"][0],
            inp["r_k"][0].reshape(-1), inp["lnx_g"][0], inp["lnx_b"][0]]
    o["params"] = np.stack([c.reshape(HP, P).T for c in cols], -1)
    o["sink"] = inp["sink"][0].reshape(2, NH // 2).T.reshape(-1)
    rows = pair_cols + list(range(NH * HD, 2 * NH * HD))
    o["w_out"] = np.ascontiguousarray(inp["w_out"][0][rows].reshape(KT, P, D).transpose(1, 0, 2))
    o["ln1"] = np.stack([inp["ln1_g"][0], inp["ln1_b"][0]])
    o["ln2"] = np.stack([inp["ln2_g"][0], inp["ln2_b"][0]])
    o["wq"] = np.ascontiguousarray(inp["peer_wq"][0].reshape(KT, P, 2 * PH * P).transpose(1, 0, 2))
    o["keys"] = np.ascontiguousarray(inp["peer_keys"][0].reshape(2 * PH, NK, P).transpose(2, 0, 1))
    o["u"], o["v"] = inp["peer_u"][0], inp["peer_v"][0]
    return o


_ORDER = ["x", "x_t", "w_tiles", "rope", "masks", "sink", "perm", "mu", "low_rank", "params", "tri", "tri_l",
          "eye", "ident_in", "ones_in", "w_out", "ln1", "wq", "keys", "u", "v", "ln2"]


def kernel(**inputs):
    from concourse import bacc
    from concourse.bass_utils import run_bass_kernel_spmd

    arrays = layouts({k: np.asarray(a) for k, a in inputs.items()})
    arrays.update(constants())
    nc = bacc.Bacc("TRN2", target_bir_lowering=False, num_devices=1)
    args = []
    for name in _ORDER:
        a = arrays[name] = np.ascontiguousarray(arrays[name])
        args.append(nc.dram_tensor("in_" + name, a.shape, mybir.dt.from_np(a.dtype), kind="ExternalInput").ap())
    args.append(nc.dram_tensor("out_y", (SEQ, D), F32, kind="ExternalOutput").ap())
    program(nc, *args)
    r = run_bass_kernel_spmd(nc, [{"in_" + n: arrays[n] for n in _ORDER}], core_ids=[0])
    return r.results[0]["out_y"].reshape(1, SEQ, D)
```

```python
from contextlib import ExitStack

import numpy as np
import concourse.bass as bass
from concourse import mybir

F32 = mybir.dt.float32
U32 = mybir.dt.uint32
ALU = mybir.AluOpType
ACT = mybir.ActivationFunctionType
AX = mybir.AxisListType
ds = bass.ds

P = 128
SEQ = 1024
D = 1024
KT = D // P
TT = SEQ // P
HD = 64
NH = 8
HP = NH // 2
CH = 64
NC = SEQ // CH
XS = 5
NFT = 14
NAT = 6
WIN = 3 * P
PADDED = SEQ + 2 * P
ALPHA = 2.0 ** 0.25
DECAY = float(np.exp(-0.5))
GN_EPS = 64e-5
LN_EPS = 1e-5
NEG = -1e30
PH = 8
NK = 128
TOPK = 16
NSEL = PH * TOPK
GRP = 8
NG = NSEL // GRP
WQ_LOADS = 1 + KT // 2
HALF = 512

W0F, W0B, A0F, A0B, KKS, KA, RK, LNG, LNB, KAC = range(10)
NPAR = 9


def allocator(nc, ctx, prefix=""):
    def sb(name, shape, dtype=F32):
        return ctx.enter_context(nc.sbuf_tensor(prefix + name, list(shape), dtype))
    return sb


class Semaphores:

    def __init__(self, nc, ctx, prefix):
        self.nc, self.ctx, self.prefix, self.used, self.from_zero = nc, ctx, prefix, [], []
        ctx.callback(self.clear)

    def __call__(self, name, from_zero=False):
        s = self.ctx.enter_context(self.nc.semaphore(self.prefix + name))
        (self.from_zero if from_zero else self.used).append(s)
        return s

    def start(self):
        with self.nc.Block() as block:
            @block.gpsimd
            def _(pool):
                for s in self.used:
                    pool.sem_inc(s, 1)

    def clear(self):
        with self.nc.Block() as block:
            @block.gpsimd
            def _(pool):
                for s in self.used + self.from_zero:
                    pool.sem_clear(s)


def seen(count):
    return count + 1


def project(nc, banks, x_t, w_tiles, xT, feat, at, mu):
    total = NFT + NAT
    with ExitStack() as ctx:
        sb, sem = allocator(nc, ctx, "pr_"), Semaphores(nc, ctx, "pr_")
        part = sb("part", [P, 3, NFT])
        mu_in, links, shifted, bent = sem("mu_in"), sem("links"), sem("shifted"), sem("bent")
        mp, mn, m0 = (part[:, i, :] for i in range(3))
        w = [sb(f"w{b}", [P, KT, P]) for b in range(2)]
        x_in = [sem(f"x_in{k}") for k in range(2)]
        w_in = [sem(f"w_in{b}") for b in range(2)]
        product = [sem(f"product{h}") for h in range(2)]
        copied = [[sem(f"copied{b}{h}") for h in range(2)] for b in range(2)]
        sem.start()
        block = ctx.enter_context(nc.Block())

        @block.sync
        def _(sp):
            for k in range(2):
                sp.dma_start(xT[:, k * 4:k * 4 + 4, :], x_t[:, k * 4:k * 4 + 4, :]).then_inc(x_in[k], 16)
            for b in range(2):
                sp.dma_start(w[b][:], w_tiles[b]).then_inc(w_in[b], 16)
            for i in range(2):
                sp.dma_start(part[:, i, :], mu[i]).then_inc(mu_in, 16)
            with sp.Fori(1, total // 2) as j:
                for b in range(2):
                    sp.wait_ge(product[1], seen(2 * j - 1 + b))
                    sp.dma_start(w[b][:], w_tiles[ds(2 * j + b, 1)].rearrange("o p k c -> p (o k) c")
                                 ).then_inc(w_in[b], 16)

        @block.tensor
        def _(pe):
            for k in range(2):
                pe.wait_ge(x_in[k], seen(16))
            with pe.Fori(0, total // 2) as j:
                for b in range(2):
                    pe.wait_ge(w_in[b], seen(16 * j + 16))
                    for h in range(2):
                        pe.wait_ge(copied[b][h], seen(j))
                        bank = banks[2 * b + h]
                        for k in range(KT):
                            last = pe.matmul(bank[:], w[b][:, k, :], xT[:, k, h * HALF:(h + 1) * HALF],
                                             start=(k == 0), stop=(k == KT - 1))
                        last.then_inc(product[h], 1)

        def copies(eng, h, copy, then):
            for dest, first, n in ((feat[:, SEQ:], 0, NFT), (at, NFT, NAT)):
                with eng.Fori(0, n // 2) as j:
                    for b in range(2):
                        eng.wait_ge(product[h], seen(first + 2 * j + b + 1))
                        copy(dest[:, ds((2 * j + b) * SEQ + h * HALF, HALF)],
                             banks[2 * b + h][:]).then_inc(copied[b][h], 1)
                        if first == 0 and then:
                            then(2 * j + b, j, b)

        @block.scalar
        def _(act):
            copies(act, 0, act.copy, None)
            act.wait_ge(shifted, seen(NFT))
            wd = feat[0:2 * 32, 12 * SEQ:13 * SEQ]
            gd = feat[:, 13 * SEQ:14 * SEQ]
            act.activation(wd, wd, ACT.Tanh).then_inc(bent, 1)
            act.activation(gd, gd, ACT.Sigmoid).then_inc(bent, 1)

        @block.vector
        def _(dve):
            dve.wait_ge(mu_in, seen(32))
            dve.tensor_tensor(m0, mp, mn, ALU.add).then_inc(links, 1)
            dve.wait_ge(links, seen(1))
            dve.tensor_scalar(m0, m0, -1.0, 1.0, ALU.mult, ALU.add).then_inc(links, 1)
            dve.wait_ge(links, seen(2))

            def shift(f, j, b):
                def new(a, n):
                    return feat[:, ds(f * SEQ + a, n)]

                def old(a, n):
                    return feat[:, ds(f * SEQ + SEQ + a, n)]
                for h in range(2):
                    dve.wait_ge(copied[b][h], seen(j + 1))
                dve.tensor_scalar(new(0, SEQ), old(0, SEQ), m0[:, ds(f, 1)], None, ALU.mult).then_inc(links, 1)
                dve.wait_ge(links, seen(2 * f + 3))
                dve.scalar_tensor_tensor(new(1, SEQ - 1), old(0, SEQ - 1), mp[:, ds(f, 1)],
                                         new(1, SEQ - 1), ALU.mult, ALU.add).then_inc(links, 1)
                dve.wait_ge(links, seen(2 * f + 4))
                dve.scalar_tensor_tensor(new(0, SEQ - 1), old(1, SEQ - 1), mn[:, ds(f, 1)],
                                         new(0, SEQ - 1), ALU.mult, ALU.add).then_inc(shifted, 1)
            copies(dve, 1, dve.tensor_copy, shift)


def attend(nc, banks, at, mixT, consts, rope, masks, sink, perm, attended):
    ident = consts["ident"]
    with ExitStack() as ctx:
        sb, sem = allocator(nc, ctx, "at_"), Semaphores(nc, ctx, "at_")
        cosT = sb("cosT", [P, SEQ])
        sinT = sb("sinT", [P, SEQ])
        swap = sb("swap", [P, P])
        mask = sb("mask", [P, TT, WIN])
        snk = sb("snk", [P, NH])
        turned = sb("turned", [P, 2, HALF])
        kP = sb("kP", [P, PADDED])
        vP = sb("vP", [P, TT + 2, P])
        qs = [sb(f"qs{b}", [P, 4, P]) for b in range(2)]
        ks = [sb(f"ks{b}", [P, WIN]) for b in range(2)]
        vs = [sb(f"vs{b}", [P, WIN]) for b in range(2)]
        lg = sb("lg", [P, NH, WIN])
        st = sb("st", [P, 6, NH])
        pT = sb("pT", [P, 2, WIN])
        tables, cleared, apart = sem("tables"), sem("cleared"), sem("apart")
        swapped, dve_step, act_step = sem("swapped"), sem("dve_step"), sem("act_step")
        v_turned, v_copied = sem("v_turned"), sem("v_copied")
        staged, logits, masked = sem("staged"), sem("logits"), sem("masked")
        chain, maxed, expd, probs = sem("chain"), sem("maxed"), sem("expd"), sem("probs")
        turnd, pcopied, out_done, stored = sem("turnd"), sem("pcopied"), sem("out_done"), sem("stored")
        set_aside = sem("set_aside")
        loads = ((cosT, rope[0]), (sinT, rope[1]), (swap, perm), (mask, masks),
                 (snk, sink.partition_broadcast(P)))

        sem.start()
        with nc.Block() as block:
            @block.sync
            def _(sp):
                for to, of in loads:
                    sp.dma_start(to[:], of).then_inc(tables, 16)
                sp.wait_ge(tables, seen(16 * len(loads)))

            @block.gpsimd
            def _(pool):
                pool.memset(kP[:], 0.0).then_inc(cleared, 1)
                pool.memset(vP[:], 0.0).then_inc(cleared, 1)

            @block.tensor
            def _(pe):
                pe.wait_ge(tables, seen(16 * len(loads)))
                with pe.Fori(0, 5) as f:
                    for h in range(2):
                        pe.wait_ge(dve_step, seen(2 * f + h))
                        pe.matmul(banks[h][:], swap[:], at[:, ds(f * SEQ + h * HALF, HALF)],
                                  start=True, stop=True).then_inc(swapped, 1)
                for n in range(TT):
                    if n >= 4:
                        pe.wait_ge(v_copied, seen(n - 3))
                    pe.transpose(banks[4 + n % 4][:, 0:P], at[:, 5 * SEQ + n * P:5 * SEQ + n * P + P],
                                 ident[:]).then_inc(v_turned, 1)

            @block.scalar
            def _(act):
                act.wait_ge(cleared, seen(2))
                for n in range(TT):
                    act.wait_ge(v_turned, seen(n + 1))
                    act.copy(vP[:, n + 1, :], banks[4 + n % 4][:, 0:P]).then_inc(v_copied, 1)

            @block.vector
            def _(dve):
                dve.wait_ge(tables, seen(16 * len(loads)))
                with dve.Fori(0, 5) as f:
                    for h in range(2):
                        cols = ds(f * SEQ + h * HALF, HALF)
                        dve.wait_ge(swapped, seen(2 * f + h + 1))
                        dve.tensor_tensor(turned[:, h, :], banks[h][:], sinT[:, h * HALF:(h + 1) * HALF],
                                          ALU.mult).then_inc(dve_step, 1)
                        dve.tensor_tensor(at[:, cols], at[:, cols], cosT[:, h * HALF:(h + 1) * HALF],
                                          ALU.mult).then_inc(chain, 1)
                        dve.wait_ge(chain, seen(4 * f + 2 * h + 1))
                        dve.wait_ge(dve_step, seen(2 * f + h + 1))
                        dve.tensor_tensor(at[:, cols], at[:, cols], turned[:, h, :], ALU.add
                                          ).then_inc(chain, 1)
                dve.wait_ge(chain, seen(20))
                dve.wait_ge(cleared, seen(2))
                dve.tensor_copy(kP[:, P:P + SEQ], at[:, 4 * SEQ:5 * SEQ]).then_inc(chain, 1)

        with nc.Block() as block:
            @block.sync
            def _(sp):
                with sp.Fori(0, TT) as n:
                    sp.wait_ge(stored, seen(4 * n + 4))
                    sp.dma_start(attended[:, :, ds(n * P, P)], mixT[:, 0:4, ds(n * P, P)]).then_inc(set_aside, 16)
                sp.wait_ge(set_aside, seen(16 * TT))

            @block.gpsimd
            def _(pool):
                def stage(n, b):
                    pool.sem_inc(apart, 1)
                    pool.tensor_copy(qs[b][:], at[:].rearrange("p (f t) -> p f t", t=SEQ)[:, 0:4, ds(n * P, P)]
                                     ).then_inc(staged, 1)
                    pool.tensor_copy(ks[b][:], kP[:, ds(n * P, WIN)]).then_inc(staged, 1)
                    pool.tensor_copy(vs[b][:], vP[:].rearrange("p b c -> p (b c)")[:, ds(n * P, WIN)]
                                     ).then_inc(staged, 1)
                for b in range(2):
                    stage(b, b)
                with pool.Fori(1, TT // 2) as j:
                    for b in range(2):
                        pool.wait_ge(out_done, seen(4 * (2 * j + b - 1)))
                        stage(2 * j + b, b)

            @block.tensor
            def _(pe):
                def block_of(n, qs, ks, vs):
                    pe.wait_ge(staged, seen(3 * n + 3))
                    for p in range(4):
                        for s in range(2):
                            pe.wait_ge(masked, seen(8 * n + 2 * p + s - 3 if p >= 2 else 8 * n))
                            pe.matmul(banks[2 * (p % 2) + s][:, 0:WIN], qs[s * HD:(s + 1) * HD, p, :],
                                      ks[s * HD:(s + 1) * HD, :], start=True, stop=True
                                      ).then_inc(logits, 1)
                    for p in range(4):
                        for s in range(2):
                            i = 2 * p + s
                            pe.wait_ge(probs, seen(8 * n + i + 1))
                            pe.wait_ge(pcopied, seen(8 * n + i - 1 if i >= 2 else 8 * n))
                            for c in range(3):
                                last = pe.transpose(banks[4 + s][:, c * P:(c + 1) * P],
                                                    lg[:, i, c * P:(c + 1) * P], ident[:])
                            last.then_inc(turnd, 1)
                        for s in range(2):
                            i = 2 * p + s
                            pe.wait_ge(pcopied, seen(8 * n + i + 1))
                            if s == 0:
                                pe.wait_ge(stored, seen(4 * n + p - 1 if p >= 2 else 4 * n))
                            for c in range(3):
                                last = pe.matmul(banks[6 + p % 2][s * HD:(s + 1) * HD, 0:P],
                                                 vs[:, c * P + s * HD:c * P + (s + 1) * HD],
                                                 pT[:, s, c * P:(c + 1) * P], start=(c == 0), stop=(c == 2))
                        last.then_inc(out_done, 1)
                with pe.Fori(0, TT // 2) as j:
                    for b in range(2):
                        block_of(2 * j + b, qs[b], ks[b], vs[b])

            @block.vector
            def _(dve):
                with dve.Fori(0, TT) as n:
                    for q in range(2):
                        hs = slice(4 * q, 4 * q + 4)
                        base = 21 + 8 * n + 2 * q
                        for i in range(4 * q, 4 * q + 4):
                            dve.wait_ge(logits, seen(8 * n + i + 1))
                            dve.wait_ge(turnd, seen(8 * n))
                            dve.scalar_tensor_tensor(lg[:, i, :], banks[i % 4][:, 0:WIN], HD ** -0.5,
                                                     mask[:, ds(n, 1), :].rearrange("p a k -> p (a k)"),
                                                     ALU.mult, ALU.add).then_inc(masked, 1)
                        dve.wait_ge(masked, seen(8 * n + 4 * q + 4))
                        dve.tensor_reduce(st[:, 0, hs], lg[:, hs], AX.X, ALU.max).then_inc(chain, 1)
                        dve.wait_ge(chain, seen(base + 1))
                        dve.tensor_tensor(st[:, 1, hs], st[:, 0, hs], snk[:, hs], ALU.max).then_inc(chain, 1)
                        dve.wait_ge(chain, seen(base + 2))
                        dve.tensor_scalar(st[:, 2, hs], st[:, 1, hs], -1.0, None, ALU.mult).then_inc(maxed, 1)
                        dve.tensor_tensor(st[:, 3, hs], snk[:, hs], st[:, 1, hs], ALU.subtract
                                          ).then_inc(maxed, 1)
                    for q in range(2):
                        hs = slice(4 * q, 4 * q + 4)
                        base = 21 + 8 * n + 4 + 2 * q
                        dve.wait_ge(expd, seen(10 * n + 5 * q + 5))
                        dve.tensor_tensor(st[:, 5, hs], st[:, 5, hs], st[:, 4, hs], ALU.add).then_inc(chain, 1)
                        dve.wait_ge(chain, seen(base + 1))
                        dve.reciprocal(st[:, 0, hs], st[:, 5, hs]).then_inc(chain, 1)
                        dve.wait_ge(chain, seen(base + 2))
                        for i in range(4 * q, 4 * q + 4):
                            dve.tensor_scalar(lg[:, i, :], lg[:, i, :], st[:, 0, i:i + 1], None, ALU.mult
                                              ).then_inc(probs, 1)
                    for p in range(4):
                        dve.wait_ge(out_done, seen(4 * n + p + 1))
                        dve.tensor_copy(mixT[:, p, :][:, ds(n * P, P)], banks[6 + p % 2][:, 0:P]
                                        ).then_inc(stored, 1)

            @block.scalar
            def _(act):
                with act.Fori(0, TT) as n:
                    for q in range(2):
                        hs = slice(4 * q, 4 * q + 4)
                        act.wait_ge(maxed, seen(4 * n + 2 * q + 2))
                        act.activation(st[:, 4, hs], st[:, 3, hs], ACT.Exp).then_inc(expd, 1)
                        for i in range(4 * q, 4 * q + 4):
                            act.activation(lg[:, i, :], lg[:, i, :], ACT.Exp, bias=st[:, 2, i:i + 1],
                                           accum_out=st[:, 5, i:i + 1]).then_inc(expd, 1)
                    for i in range(NH):
                        act.wait_ge(turnd, seen(8 * n + i + 1))
                        act.wait_ge(out_done, seen(4 * n + i // 2))
                        act.copy(pT[:, i % 2, :], banks[4 + i % 2][:, 0:WIN]).then_inc(pcopied, 1)


def prepare_chunks(nc, ps, feat, consts, low_rank, params, chunks, gates):
    ones = consts["ones"]
    with ExitStack() as ctx:
        sb, sem = allocator(nc, ctx, "pc_"), Semaphores(nc, ctx, "pc_")
        lr = sb("lr", [P, 5, P])
        par_all = sb("par_all", [P, HP, NPAR])
        par = sb("par", [P, NPAR + 1])
        reset = sb("reset", [P, SEQ])
        sg = [sb(f"sg{d}", [P, SEQ]) for d in range(2)]
        a = [sb(f"a{d}", [P, SEQ]) for d in range(2)]
        kd = [sb(f"kd{d}", [P, SEQ]) for d in range(2)]
        kk = sb("kk", [P, SEQ])
        nrm = sb("nrm", [P, SEQ])
        cs = sb("cs", [P, SEQ])
        X = sb("X", [P, SEQ])
        Y = sb("Y", [P, SEQ])
        E = sb("E", [P, SEQ])
        half = sb("half", [P, NC])
        nxt = sb("nxt", [P, 2, NC])
        st = [sb(f"st{d}", [P, NC, XS, CH]) for d in range(2)]
        names = ("par_in lr_in scans_ready ranks keyed squared summed rooted links xy exps gate_in "
                 "kd_made gated staged_v written sigs floored bonus_in bonus_sum bonus_out g_prod g_out")
        (par_in, lr_in, scans_ready, ranks, keyed, squared, summed, rooted, links, xy, exps, gate_in,
         kd_made, gated, staged_v, written, sigs, floored, bonus_in, bonus_sum, bonus_out, g_prod,
         g_out) = (sem(n) for n in names.split())
        apart = sem("apart")
        staged = [sem(f"staged{d}") for d in range(2)]
        stored = [sem(f"stored{d}") for d in range(2)]
        sem.start()
        block = ctx.enter_context(nc.Block())
        slots = feat[:].rearrange("p (f t) -> p f t", t=SEQ)

        def slot(f, hp):
            return feat[:, ds((f + hp) * SEQ, SEQ)]

        def by_chunk(t):
            return t[:].rearrange("p (c t) -> p c t", t=CH)

        @block.sync
        def _(sp):
            sp.dma_start(par_all[:], params).then_inc(par_in, 16)
            with sp.Fori(0, HP) as hp:
                sp.wait_ge(g_prod, seen(hp))
                sp.sem_inc(apart, 1)
                sp.dma_start(lr[:], low_rank[ds(hp, 1)].rearrange("o p x c -> p (o x) c")).then_inc(lr_in, 16)
                for d in range(2):
                    sp.wait_ge(staged[d], seen(4 * hp + 4))
                    sp.sem_inc(apart, 1)
                    sp.wait_ge(staged_v, seen(2 * hp + d + 1))
                    sp.sem_inc(apart, 1)
                    for c in range(0, NC, 8):
                        sp.dma_start(chunks[d, c:c + 8, :, ds(hp * XS * CH, XS * CH)].rearrange("c p n -> p c n"),
                                     st[d][:, c:c + 8].rearrange("p c x t -> p c (x t)")).then_inc(stored[d], 16)
            for d in range(2):
                sp.wait_ge(stored[d], seen(2 * 16 * HP))

        @block.tensor
        def _(pe):
            with pe.Fori(0, HP) as hp:
                pe.wait_ge(lr_in, seen(16 * hp + 16))
                pe.wait_ge(g_out, seen(hp))
                pe.wait_ge(bonus_out, seen(hp))
                pe.wait_ge(floored, seen(hp))
                for x in range(4):
                    for h in range(2):
                        last = pe.matmul(ps[:, (2 * x + h) * HALF:(2 * x + h + 1) * HALF], lr[:, x, :],
                                         feat[:, 12 * SEQ + h * HALF:12 * SEQ + (h + 1) * HALF],
                                         start=True, stop=True)
                    last.then_inc(ranks, 1)
                pe.wait_ge(squared, seen(hp + 1))
                pe.wait_ge(sigs, seen(4 * hp + 4))
                for h in range(2):
                    last = pe.matmul(ps[:, h * HALF:(h + 1) * HALF], ones[:], nrm[:, h * HALF:(h + 1) * HALF],
                                     start=True, stop=True)
                last.then_inc(summed, 1)
                for h in range(2):
                    last = pe.matmul(ps[:, (4 + h) * HALF:(5 + h) * HALF], lr[:, 4, :],
                                     feat[:, 13 * SEQ + h * HALF:13 * SEQ + (h + 1) * HALF],
                                     start=True, stop=True)
                last.then_inc(g_prod, 1)
                pe.wait_ge(bonus_in, seen(hp + 1))
                for h in range(2):
                    last = pe.matmul(ps[:, (2 + h) * HALF:(3 + h) * HALF], ones[:], X[:, h * HALF:(h + 1) * HALF],
                                     start=True, stop=True)
                last.then_inc(bonus_sum, 1)

        @block.gpsimd
        def _(pool):
            pool.memset(reset[:], 1.0).then_inc(scans_ready, 1)
            pool.wait_ge(scans_ready, seen(1))
            pool.memset(by_chunk(reset)[:, :, 0:1], 0.0).then_inc(scans_ready, 1)
            with pool.Fori(0, HP) as hp:
                for d in range(2):
                    pool.wait_ge(stored[d], seen(32 * hp))
                    pool.sem_inc(apart, 1)
                    pool.tensor_copy(st[d][:, :, 4, :],
                                     slot(8, hp).rearrange("p (c t) -> p c t", t=CH)).then_inc(staged_v, 1)

        @block.scalar
        def _(act):
            with act.Fori(0, HP) as hp:
                act.wait_ge(written, seen(hp + 1))
                act.activation(kk[:], slot(4, hp), ACT.Copy, scale=par[:, KKS:KKS + 1]).then_inc(keyed, 1)
                act.wait_ge(keyed, seen(hp + 1))
                act.activation(nrm[:], kk[:], ACT.Square).then_inc(squared, 1)
                for x, (to, col) in enumerate(((sg[0], W0F), (sg[1], W0B), (a[0], A0F), (a[1], A0B))):
                    act.wait_ge(ranks, seen(4 * hp + x + 1))
                    act.activation(to[:], ps[:, 2 * x * HALF:(2 * x + 2) * HALF], ACT.Sigmoid,
                                   bias=par[:, col:col + 1]).then_inc(sigs, 1)
                act.wait_ge(sigs, seen(4 * hp + 4))
                for d in range(2):
                    act.activation(kd[d][:], a[d][:], ACT.Identity, scale=par[:, KA:KA + 1],
                                   bias=par[:, KAC:KAC + 1]).then_inc(kd_made, 1)
                act.wait_ge(floored, seen(hp + 1))
                act.activation(nrm[:], nrm[:], ACT.Sqrt).then_inc(rooted, 1)
                for d in range(2):
                    act.wait_ge(gate_in, seen(2 * hp + d + 1))
                    act.activation(gates[:, d, ds(hp, 1), :].rearrange("p a c -> p (a c)"), nxt[:, d, :],
                                   ACT.Exp, scale=-DECAY).then_inc(gated, 1)
                    act.wait_ge(xy, seen(2 * hp + d + 1))
                    if d == 0:
                        act.activation(E[:], X[:], ACT.Exp, scale=DECAY).then_inc(exps, 1)
                        act.wait_ge(exps, seen(6 * hp + 1))
                        act.activation(X[:], X[:], ACT.Exp, scale=-DECAY).then_inc(exps, 1)
                        act.activation(Y[:], Y[:], ACT.Exp, scale=-DECAY).then_inc(exps, 1)
                    else:
                        act.activation(E[:], Y[:], ACT.Exp, scale=-DECAY).then_inc(exps, 1)
                        act.wait_ge(exps, seen(6 * hp + 4))
                        act.activation(Y[:], Y[:], ACT.Exp, scale=DECAY).then_inc(exps, 1)
                        act.activation(X[:], X[:], ACT.Exp, scale=DECAY).then_inc(exps, 1)
                act.wait_ge(g_prod, seen(hp + 1))
                act.wait_ge(bonus_in, seen(hp + 1))
                act.copy(slot(0, hp), ps[:, 4 * HALF:6 * HALF]).then_inc(g_out, 1)

        @block.vector
        def _(dve):
            per_pair = 14
            n = [0]
            dve.wait_ge(par_in, seen(16))
            dve.wait_ge(scans_ready, seen(2))
            with dve.Fori(0, HP) as hp:
                def link(ins):
                    n[0] += 1
                    ins.then_inc(links, 1)
                    dve.wait_ge(links, seen(hp * per_pair + n[0]))

                k, r, v = slot(4, hp), slot(0, hp), slot(8, hp)
                dve.wait_ge(bonus_out, seen(hp))
                link(dve.tensor_copy(par[:, 0:NPAR], par_all[:, ds(hp, 1), :].rearrange("p a c -> p (a c)")))
                dve.tensor_scalar(par[:, KAC:KAC + 1], par[:, KA:KA + 1], -1.0, 1.0, ALU.mult, ALU.add
                                  ).then_inc(written, 1)
                dve.wait_ge(written, seen(hp + 1))
                dve.wait_ge(summed, seen(hp + 1))
                dve.tensor_scalar(nrm[:], ps[:, 0:2 * HALF], 1e-24, None, ALU.max).then_inc(floored, 1)
                dve.wait_ge(rooted, seen(hp + 1))
                link(dve.reciprocal(nrm[:], nrm[:]))
                link(dve.tensor_tensor(kk[:], kk[:], nrm[:], ALU.mult))
                for d in range(2):
                    dve.wait_ge(sigs, seen(4 * hp + 4))
                    link(dve.tensor_tensor_scan(cs[:], reset[:], sg[d][:], 0.0, ALU.mult, ALU.add))
                    link(dve.tensor_scalar(half[:], by_chunk(cs)[:, :, CH - 1], 0.5, None, ALU.mult))
                    dve.wait_ge(gated, seen(2 * hp + d))
                    a0, b0 = (0, 1) if d == 0 else (1, 0)
                    dve.tensor_tensor(nxt[:, d, a0:a0 + NC - 1], half[:, 0:NC - 1], half[:, 1:NC], ALU.add)
                    edge = NC - 1 if d == 0 else 0
                    dve.tensor_copy(nxt[:, d, edge:edge + 1], half[:, edge:edge + 1]).then_inc(gate_in, 1)
                    link(dve.tensor_tensor(by_chunk(X), by_chunk(cs),
                                           half[:].unsqueeze(2).broadcast_to([P, NC, CH]), ALU.subtract))
                    dve.tensor_tensor(Y[:], X[:], sg[d][:], ALU.subtract).then_inc(xy, 1)
                    dve.wait_ge(kd_made, seen(2 * hp + d + 1))
                    link(dve.tensor_tensor(kd[d][:], kd[d][:], k, ALU.mult))
                    link(dve.tensor_tensor(a[d][:], a[d][:], kk[:], ALU.mult))
                    eA, eR = (Y, X) if d == 0 else (X, Y)
                    dve.wait_ge(exps, seen(6 * hp + 3 * d + 3))
                    dve.wait_ge(stored[d], seen(32 * hp))
                    dve.scalar_tensor_tensor(st[d][:, :, 1, :], by_chunk(kk), -1.0, by_chunk(eA),
                                             ALU.mult, ALU.mult).then_inc(staged[d], 1)
                    dve.tensor_tensor(st[d][:, :, 0, :], r.rearrange("p (c t) -> p c t", t=CH), by_chunk(eR),
                                      ALU.mult).then_inc(staged[d], 1)
                    dve.tensor_tensor(st[d][:, :, 2, :], by_chunk(a[d]), by_chunk(E), ALU.mult
                                      ).then_inc(staged[d], 1)
                    dve.tensor_tensor(st[d][:, :, 3, :], by_chunk(kd[d]), by_chunk(E), ALU.mult
                                      ).then_inc(staged[d], 1)
                    dve.wait_ge(staged[d], seen(4 * hp + 4))
                link(dve.tensor_tensor(kd[0][:], kd[0][:], kd[1][:], ALU.add))
                dve.scalar_tensor_tensor(X[:], kd[0][:], par[:, RK:RK + 1], r, ALU.mult, ALU.mult
                                         ).then_inc(bonus_in, 1)
                dve.wait_ge(bonus_sum, seen(hp + 1))
                dve.wait_ge(staged_v, seen(2 * hp + 2))
                dve.scalar_tensor_tensor(v, ps[:, 2 * HALF:4 * HALF], 0.5, v, ALU.mult, ALU.mult
                                         ).then_inc(bonus_out, 1)
            assert n[0] == per_pair


def run_chunks(nc, ps, feat, mixT, consts, chunks, gates, tri, tri_l):
    ident = consts["ident"]
    G = 2 * HP
    LEVELS = 5
    with ExitStack() as ctx:
        sb, sem = allocator(nc, ctx, "rc_"), Semaphores(nc, ctx, "rc_")
        stk = [sb(f"stk{b}", [P, G, 3, CH]) for b in range(2)]
        dia = [sb(f"dia{b}", [P, G, 4, P]) for b in range(2)]
        tri_s = sb("tri_s", [P, 2, 2, CH])
        tril_s = sb("tril_s", [P, 2, CH])
        eye = sb("eye", [P, CH])

        def stacked(name):
            return sb(name, [P, G, CH])

        def diagonal(name):
            return sb(name, [P, G, P])

        def in_slot(of, f):
            return of[:, f * SEQ:(f + 1) * SEQ].rearrange("p (g c) -> p g c", c=P)
        flat = mixT[:].rearrange("p k t -> p (k t)")
        nt_s, l_s, x_s, z_s, u_s, s_s = (stacked(n) for n in ("nt_s", "l_s", "x_s", "z_s", "u_s", "s_s"))
        nt_d, l_d, x_d, u_d, s_d = (diagonal(n) for n in ("nt_d", "l_d", "x_d", "u_d", "s_d"))
        rb_s, rk_s, v_s, r_s = ([stacked(f"{n}{b}") for b in range(2)] for n in ("rb_s", "rk_s", "v_s", "r_s"))
        mt_d = [diagonal(f"mt_d{b}") for b in range(2)]
        v_d, b_d = ([in_slot(flat, f + b) for b in range(2)] for f in (0, 2))
        k_d, a_d = ([in_slot(feat, f + b) for b in range(2)] for f in (12, 14))
        gs = sb("gs", [P, G])
        names = ("consts_in cleared made nt_masked seeded masked v_ready turned natural kept squares l_dia "
                 "nt_ready l_stk xprod xadded x_ready z_made z_copied u_made u_copied u_dia y_made "
                 "y_copied s_made gs_ready updated state apart")
        (consts_in, cleared, made, nt_masked, seeded, masked, v_ready, turned, natural, kept, squares, l_dia,
         nt_ready, l_stk, xprod, xadded, x_ready, z_made, z_copied, u_made, u_copied, u_dia, y_made,
         y_copied, s_made, gs_ready, updated, state, apart) = (sem(n) for n in names.split())
        loaded = [sem(f"loaded{b}") for b in range(2)]
        sem.start()
        block = ctx.enter_context(nc.Block())
        loads = 16 * 2 * (1 + 2 * HP)

        def bank(n, k=1):
            return ps[:, n * HALF:(n + k) * HALF]

        def pairs(ap, w=CH):
            return ap.rearrange("p (g c) -> p g c", c=w)

        def blocks(ap, s):
            rows = ap[s * HD:(s + 1) * HD]
            return rows if ap.shape[2] == CH else rows[:, :, s * CH:(s + 1) * CH]

        def atleast(eng, sem, value):
            if not isinstance(value, int) or value > 0:
                eng.wait_ge(sem, seen(value))

        def steps(eng, step):
            step(0, 0, True, False)
            with eng.Fori(0, (NC - 2) // 2) as j:
                for b in (1, 0):
                    step(2 * j + 2 - b, b, True, True)
            step(NC - 1, 1, True, True)
            step(NC, 0, False, True)

        def by_two(t, b):
            if isinstance(t, int):
                return loads * (t // 2 + 1)
            return (t + 2 - b) * (loads // 2)

        @block.sync
        def _(sp):
            for to, of in ((tri_s, tri), (tril_s, tri_l), (eye, consts["eye"])):
                sp.dma_start(to[:], of).then_inc(consts_in, 16)
            sp.wait_ge(cleared, seen(1))

            def load(t, back, b):
                for d in range(2):
                    of = chunks[d, ds(back if d else t, 1)].rearrange("o p (h x t) -> p (o h) x t", x=XS, t=CH)
                    sp.dma_start(stk[b][:, d * HP:(d + 1) * HP], of[:, :, 0:3]).then_inc(loaded[b], 16)
                    for s in range(2):
                        for h in range(HP):
                            sp.dma_start(dia[b][s * HD:(s + 1) * HD, d * HP + h, :, s * CH:(s + 1) * CH],
                                         of[s * HD:(s + 1) * HD, h, 1:5]).then_inc(loaded[b], 16)
            for b in range(2):
                load(b, NC - 1 - b, b)
            with sp.Fori(1, NC // 2) as j:
                for b in range(2):
                    sp.wait_ge(turned, seen(4 * j + 2 * b - 2))
                    sp.wait_ge(kept, seen(4 * j + 2 * b - 2))
                    load(2 * j + b, NC - 1 - b - 2 * j, b)

        @block.gpsimd
        def _(pool):
            for t in (nt_d, l_d, x_d, *mt_d, u_d, s_d):
                pool.memset(t[:], 0.0)
            pool.memset(s_s[:], 0.0)
            for b in range(2):
                last = pool.memset(dia[b][:], 0.0)
            last.then_inc(cleared, 1)

            def step(t, b, prepares, advances):
                if prepares:
                    atleast(pool, y_made, t - 1)
                    pool.wait_ge(loaded[b], seen(by_two(t, b)))
                    pool.sem_inc(apart, 1)
                    pool.tensor_copy(r_s[b][:], stk[b][:, :, 0, :]).then_inc(kept, 1)
                    pool.tensor_copy(a_d[b], dia[b][:, :, 0, :]).then_inc(kept, 1)
            steps(pool, step)

        @block.tensor
        def _(pe):
            pe.wait_ge(cleared, seen(1))

            def each_pair(n, w, lhs, rhs):
                for g in range(G):
                    last = pe.matmul(ps[:, n * HALF + g * w:n * HALF + (g + 1) * w], lhs(g), rhs(g),
                                     start=True, stop=True)
                return last

            def turn(n, lhs):
                for g in range(G):
                    last = pe.transpose(ps[:, n * HALF + g * P:n * HALF + (g + 1) * P], lhs(g), ident[:])
                return last

            def products(t, b):
                S, Dg = stk[b], dia[b]
                pe.wait_ge(loaded[b], seen(by_two(t, b)))
                atleast(pe, y_copied, t - 1)
                atleast(pe, state, t - 1)
                atleast(pe, x_ready, t)
                each_pair(0, P, lambda g: Dg[:, g, 1, :], lambda g: S[:, g, 0:2, :]).then_inc(made, 1)
                each_pair(4, CH, lambda g: Dg[:, g, 0, :], lambda g: S[:, g, 2, :]).then_inc(made, 1)
                each_pair(2, P, lambda g: Dg[:, g, 2, :], lambda g: S[:, g, 0:2, :]).then_inc(made, 1)
                turn(5, lambda g: Dg[:, g, 3, :]).then_inc(made, 1)

            def naturals(t, b):
                Dg = dia[b]
                pe.wait_ge(masked, seen(t + 1))
                turn(2, lambda g: Dg[:, g, 1, :]).then_inc(turned, 1)
                pe.wait_ge(v_ready, seen(t + 1))
                turn(5, lambda g: Dg[:, g, 2, :]).then_inc(turned, 1)

            def level(t, k):
                if k == 0:
                    pe.wait_ge(seeded, seen(t + 1))
                else:
                    pe.wait_ge(l_dia, seen(LEVELS * t + k))
                    pe.wait_ge(xadded, seen(LEVELS * t + k))
                    each_pair(4, CH, lambda g: l_d[:, g, :], lambda g: x_s[:, g, :]).then_inc(xprod, 1)
                if k == LEVELS:
                    return
                if k:
                    pe.wait_ge(nt_ready, seen(4 * t + k))
                    pe.wait_ge(l_stk, seen(4 * t + k))
                last = each_pair(1, CH, lambda g: nt_d[:, g, :], lambda g: l_s[:, g, :])
                if k < LEVELS - 1:
                    last = each_pair(0, CH, lambda g: l_d[:, g, :], lambda g: nt_s[:, g, :])
                last.then_inc(squares, 1)

            def sums(n, *terms):
                for g in range(G):
                    for i, (lhs, rhs) in enumerate(terms):
                        last = pe.matmul(ps[:, n * HALF + g * CH:n * HALF + (g + 1) * CH],
                                         lhs if lhs is ident_all else lhs[:, g, :], rhs[:, g, :],
                                         start=(i == 0), stop=(i == len(terms) - 1))
                return last
            ident_all = ident[:]

            def step(t, b, prepares, advances):
                p, o = t - 1, 1 - b
                if prepares:
                    products(t, b)
                    naturals(t, b)
                    level(t, 0)
                if advances:
                    if prepares:
                        pe.wait_ge(natural, seen(2 * t + 2))
                    pe.wait_ge(kept, seen(2 * t))
                    atleast(pe, state, p)
                    sums(2, (mt_d[o], v_s[o]), (a_d[o], s_s)).then_inc(z_made, 1)
                if prepares:
                    level(t, 1)
                if advances:
                    pe.wait_ge(z_copied, seen(p + 1))
                    pe.wait_ge(x_ready, seen(p + 1))
                    sums(3, (x_d, z_s)).then_inc(u_made, 1)
                if prepares:
                    level(t, 2)
                if advances:
                    pe.wait_ge(u_dia, seen(p + 1))
                    sums(5, (s_d, r_s[o]), (v_d[o], rk_s[o]), (u_d, rb_s[o])).then_inc(y_made, 1)
                if prepares:
                    level(t, 3)
                if advances:
                    pe.wait_ge(u_copied, seen(p + 1))
                    sums(6, (ident_all, s_s), (k_d[o], v_s[o]), (b_d[o], u_s)).then_inc(s_made, 1)
                if prepares:
                    level(t, 4)
                    level(t, 5)
            steps(pe, step)

        @block.vector
        def _(dve):
            dve.wait_ge(consts_in, seen(48))
            dve.wait_ge(cleared, seen(1))

            def tri_of(rows, x):
                return tri_s[rows, :, x, :].unsqueeze(2).broadcast_to([rows.stop - rows.start, 2, HP, CH])

            def tril_of(rows):
                return tril_s[rows].unsqueeze(2).broadcast_to([rows.stop - rows.start, 2, HP, CH])

            def by_dir(ap):
                return ap.rearrange("p (d h) c -> p d h c", d=2)

            def part(base, x):
                return bank(base, 2).rearrange("p (d h x c) -> p d h x c", d=2, x=2, c=CH)[:, :, :, x, :]
            every = slice(0, P)
            halves = [slice(s * HD, (s + 1) * HD) for s in range(2)]

            def mask_products(t, b):
                dve.wait_ge(made, seen(4 * t + 1))
                dve.tensor_tensor(by_dir(nt_s[:]), part(0, 1), tri_of(every, 1), ALU.mult).then_inc(nt_masked, 1)
                dve.tensor_tensor(by_dir(rb_s[b][:]), part(0, 0), tri_of(every, 0), ALU.mult)
                dve.wait_ge(made, seen(4 * t + 2))
                for s, rows in enumerate(halves):
                    dve.tensor_tensor(by_dir(blocks(l_d, s)), by_dir(pairs(bank(4)))[rows], tril_of(rows), ALU.mult)
                dve.tensor_tensor(by_dir(l_s[:]), by_dir(pairs(bank(4))), tril_of(every), ALU.mult)
                dve.wait_ge(nt_masked, seen(t + 1))
                for s in range(2):
                    last = dve.tensor_copy(blocks(nt_d, s), blocks(nt_s, s))
                last.then_inc(seeded, 1)
                dve.tensor_tensor(x_s[:], nt_s[:], eye[:].unsqueeze(1).broadcast_to([P, G, CH]), ALU.add
                                  ).then_inc(xadded, 1)
                dve.wait_ge(made, seen(4 * t + 3))
                for s, rows in enumerate(halves):
                    dve.tensor_tensor(by_dir(blocks(mt_d[b], s)), part(2, 1)[rows], tri_of(rows, 1), ALU.mult)
                dve.tensor_tensor(by_dir(rk_s[b][:]), part(2, 0), tri_of(every, 0), ALU.mult).then_inc(masked, 1)

            def keep_squares(t, k):
                dve.wait_ge(squares, seen(LEVELS * t + k))
                if k < LEVELS - 1:
                    dve.tensor_copy(nt_s[:], pairs(bank(0)))
                for s in range(2):
                    last = dve.tensor_copy(blocks(nt_d, s), pairs(bank(0))[halves[s]])
                last.then_inc(nt_ready, 1)

            def add_level(t, k):
                dve.wait_ge(xprod, seen(LEVELS * t + k))
                dve.wait_ge(xadded, seen(LEVELS * t + k))
                if k < LEVELS:
                    dve.tensor_tensor(x_s[:], x_s[:], pairs(bank(4)), ALU.add).then_inc(xadded, 1)
                    return
                for s in range(2):
                    last = dve.tensor_tensor(blocks(x_d, s), blocks(x_s, s), pairs(bank(4))[halves[s]], ALU.add)
                last.then_inc(x_ready, 1)

            def step(t, b, prepares, advances):
                p = t - 1
                if prepares:
                    mask_products(t, b)
                    keep_squares(t, 1)
                if advances:
                    dve.wait_ge(z_made, seen(p + 1))
                    dve.tensor_copy(z_s[:], pairs(bank(2))).then_inc(z_copied, 1)
                if prepares:
                    add_level(t, 1)
                    keep_squares(t, 2)
                    add_level(t, 2)
                    keep_squares(t, 3)
                    add_level(t, 3)
                    keep_squares(t, 4)
                if advances:
                    dve.tensor_copy(gs[:, 0:HP].unsqueeze(2), gates[:, 0, :, ds(p, 1)]).then_inc(gs_ready, 1)
                    dve.tensor_copy(gs[:, HP:G].unsqueeze(2), gates[:, 1, :, ds(NC - 1 - p, 1)]
                                    ).then_inc(gs_ready, 1)
                    dve.wait_ge(s_made, seen(p + 1))
                    dve.wait_ge(gs_ready, seen(2 * p + 2))
                    dve.tensor_tensor(s_s[:], pairs(bank(6)), gs[:].unsqueeze(2).broadcast_to([P, G, CH]),
                                      ALU.mult).then_inc(updated, 1)
                    dve.wait_ge(updated, seen(p + 1))
                    for s in range(2):
                        last = dve.tensor_copy(blocks(s_d, s), blocks(s_s, s))
                    last.then_inc(state, 1)
                if prepares:
                    add_level(t, 4)
                    add_level(t, 5)
            steps(dve, step)

        @block.scalar
        def _(act):
            halves = [slice(s * HD, (s + 1) * HD) for s in range(2)]

            def keep_squares(t, k):
                act.wait_ge(squares, seen(LEVELS * t + k))
                for s in range(2):
                    last = act.copy(blocks(l_d, s), pairs(bank(1))[halves[s]])
                last.then_inc(l_dia, 1)
                if k < LEVELS:
                    act.copy(l_s[:], pairs(bank(1))).then_inc(l_stk, 1)

            def step(t, b, prepares, advances):
                p = t - 1
                if prepares:
                    act.wait_ge(made, seen(4 * t + 4))
                    act.copy(v_d[b], pairs(bank(5, 2), P))
                    for s in range(2):
                        last = act.copy(blocks(v_s[b], s), pairs(bank(5, 2), P)[halves[s], :, s * CH:(s + 1) * CH])
                    last.then_inc(v_ready, 1)
                    act.wait_ge(turned, seen(2 * t + 1))
                    act.copy(b_d[b], pairs(bank(2, 2), P)).then_inc(natural, 1)
                    act.wait_ge(turned, seen(2 * t + 2))
                    act.copy(k_d[b], pairs(bank(5, 2), P)).then_inc(natural, 1)
                    keep_squares(t, 1)
                    keep_squares(t, 2)
                if advances:
                    act.wait_ge(u_made, seen(p + 1))
                    for s in range(2):
                        last = act.copy(blocks(u_d, s), pairs(bank(3))[halves[s]])
                    last.then_inc(u_dia, 1)
                    act.copy(u_s[:], pairs(bank(3))).then_inc(u_copied, 1)
                if prepares:
                    keep_squares(t, 3)
                if advances:
                    act.wait_ge(y_made, seen(p + 1))
                    act.copy(feat[:].rearrange("p (f t) -> p f t", t=SEQ)[:, 4:8, ds(p * CH, CH)],
                             pairs(bank(5))[:, 0:HP])
                    act.copy(mixT[:, 4:8, ds((NC - 1) * CH - p * CH, CH)], pairs(bank(5))[:, HP:G]
                             ).then_inc(y_copied, 1)
                if prepares:
                    keep_squares(t, 4)
                    keep_squares(t, 5)
            steps(act, step)


def finish_rwkv(nc, ps, feat, mixT, consts, params):
    ones = consts["ones"]
    with ExitStack() as ctx:
        sb, sem = allocator(nc, ctx, "fr_"), Semaphores(nc, ctx, "fr_")
        par_all = sb("par_all", [P, HP, NPAR])
        par = [sb(f"par{b}", [P, NPAR]) for b in range(2)]
        y = [sb(f"y{b}", [P, SEQ]) for b in range(2)]
        sq = [sb(f"sq{b}", [P, SEQ]) for b in range(2)]
        names = "par_in links added mean_made centred squared var_made floored rooted"
        (par_in, links, added, mean_made, centred, squared, var_made, floored,
         rooted) = (sem(n) for n in names.split())
        sem.start()
        block = ctx.enter_context(nc.Block())

        def slot(f, hp):
            return feat[:, ds((f + hp) * SEQ, SEQ)]

        def mixed(hp):
            return mixT[:].rearrange("p k t -> p (k t)")[:, ds((4 + hp) * SEQ, SEQ)]

        @block.sync
        def _(sp):
            sp.dma_start(par_all[:], params).then_inc(par_in, 16)
            sp.wait_ge(par_in, seen(16))

        def head_sums(pe, base, of, done):
            for h in range(2):
                last = pe.matmul(ps[:, (base + h) * HALF:(base + h + 1) * HALF], ones[:],
                                 of[:, h * HALF:(h + 1) * HALF], start=True, stop=True)
            last.then_inc(done, 1)

        @block.tensor
        def _(pe):
            with pe.Fori(0, HP // 2) as j:
                for b in range(2):
                    pe.wait_ge(added, seen(2 * j + b + 1))
                    head_sums(pe, 4 * b, y[b], mean_made)
                for b in range(2):
                    pe.wait_ge(squared, seen(2 * j + b + 1))
                    head_sums(pe, 4 * b + 2, sq[b], var_made)

        @block.scalar
        def _(act):
            with act.Fori(0, HP // 2) as j:
                for b in range(2):
                    act.wait_ge(centred, seen(2 * j + b + 1))
                    act.activation(sq[b][:], y[b][:], ACT.Square).then_inc(squared, 1)
                for b in range(2):
                    act.wait_ge(floored, seen(2 * j + b + 1))
                    act.activation(sq[b][:], sq[b][:], ACT.Sqrt).then_inc(rooted, 1)

        @block.vector
        def _(dve):
            per_two = 12
            dve.wait_ge(par_in, seen(16))
            with dve.Fori(0, HP // 2) as j:
                n = [0]

                def link(ins):
                    n[0] += 1
                    ins.then_inc(links, 1)
                    dve.wait_ge(links, seen(j * per_two + n[0]))

                for b in range(2):
                    hp = 2 * j + b
                    link(dve.tensor_copy(par[b][:], par_all[:, ds(hp, 1), :].rearrange("p a c -> p (a c)")))
                    dve.tensor_tensor(y[b][:], slot(4, hp), mixed(hp), ALU.add).then_inc(added, 1)
                for b in range(2):
                    dve.wait_ge(mean_made, seen(2 * j + b + 1))
                    dve.wait_ge(added, seen(2 * j + b + 1))
                    dve.scalar_tensor_tensor(y[b][:], ps[:, 4 * b * HALF:(4 * b + 2) * HALF], -1.0 / HD, y[b][:],
                                             ALU.mult, ALU.add).then_inc(centred, 1)
                for b in range(2):
                    dve.wait_ge(var_made, seen(2 * j + b + 1))
                    dve.tensor_scalar(sq[b][:], ps[:, (4 * b + 2) * HALF:(4 * b + 4) * HALF], 1.0 / HD, GN_EPS,
                                      ALU.mult, ALU.add).then_inc(floored, 1)
                for b in range(2):
                    hp = 2 * j + b
                    dve.wait_ge(rooted, seen(hp + 1))
                    link(dve.reciprocal(sq[b][:], sq[b][:]))
                    link(dve.tensor_tensor(y[b][:], y[b][:], sq[b][:], ALU.mult))
                    link(dve.tensor_scalar(y[b][:], y[b][:], par[b][:, LNG:LNG + 1], par[b][:, LNB:LNB + 1],
                                           ALU.mult, ALU.add))
                    link(dve.tensor_tensor(y[b][:], y[b][:], slot(8, hp), ALU.add))
                    link(dve.tensor_tensor(mixed(hp), y[b][:], slot(0, hp), ALU.mult))
                assert n[0] == per_two


class Norm:

    def __init__(self, sb, sem, name, apart):
        self.parts = sb(name + "_parts", [P, 2, 6])
        self.stat = sb(name + "_stat", [P, 4])
        self.summed, self.rooted = sem(name + "_summed"), sem(name + "_rooted")
        self.apart = apart

    def on_vector(self, dve, link, t, g, b, count):
        for h in range(2):
            last = dve.bn_stats(self.parts[:, h, :], t[:, h * HALF:(h + 1) * HALF])
        link(last)
        dve.sem_inc(self.apart, 1)
        link(dve.bn_aggr(self.stat[:, 0:2], self.parts[:]))
        dve.tensor_scalar(self.stat[:, 2:3], self.stat[:, 1:2], LN_EPS, None, ALU.add).then_inc(self.summed, 1)
        dve.wait_ge(self.rooted, seen(count + 1))
        link(dve.reciprocal(self.stat[:, 2:3], self.stat[:, 3:4]))
        link(dve.tensor_scalar(t[:], t[:], self.stat[:, 0:1], self.stat[:, 2:3], ALU.subtract, ALU.mult))
        link(dve.tensor_tensor(t[:], t[:], g[:], ALU.mult))
        return dve.tensor_tensor(t[:], t[:], b[:], ALU.add)

    LINKS = 5

    def on_scalar(self, act, count):
        act.wait_ge(self.summed, seen(count + 1))
        act.activation(self.stat[:, 3:4], self.stat[:, 2:3], ACT.Sqrt).then_inc(self.rooted, 1)


def mix_and_norm(nc, ps, mixT, consts, x, w_out, ln, attended, hidden, prefetch):
    with ExitStack() as ctx:
        sb, sem = allocator(nc, ctx, "mx_"), Semaphores(nc, ctx, "mx_")
        w = sb("w", [P, KT, D])
        lhs = [sb(f"lhs{b}", [P, KT, P]) for b in range(2)]
        xt = [sb(f"xt{b}", [P, D]) for b in range(4)]
        t = [sb(f"t{b}", [P, D]) for b in range(2)]
        g_b = [sb(n, [P, D]) for n in ("g", "b")]
        w_in, ln_in, staged, product, links, summed, normed, mix_in, apart = (
            sem(n) for n in "w_in ln_in staged product links summed normed mix_in apart".split())
        x_in = [sem(f"x_in{b}") for b in range(4)]
        stored = [sem(f"stored{b}", from_zero=True) for b in range(2)]
        norm = Norm(sb, sem, "ln", apart)
        sem.start()
        block = ctx.enter_context(nc.Block())

        @block.sync
        def _(sp):
            sp.dma_start(mixT[:, 0:4, :], attended).then_inc(mix_in, 16)
            sp.dma_start(w[:], w_out).then_inc(w_in, 16)
            for i in range(4):
                sp.dma_start(xt[i][:], x[i * P:(i + 1) * P, :]).then_inc(x_in[i], 16)
            for i in range(2):
                sp.dma_start(g_b[i][:], ln[i].partition_broadcast(P)).then_inc(ln_in, 16)
            prefetch(sp)
            for i in range(4):
                sp.wait_ge(summed, seen(i + 1))
                sp.dma_start(xt[i][:], x[(4 + i) * P:(5 + i) * P, :]).then_inc(x_in[i], 16)

        @block.gpsimd
        def _(pool):
            def store(i, b):
                pool.wait_ge(normed, seen(i + 1))
                pool.dma_start(hidden[ds(i * P, P), :], t[b][:]).then_inc(stored[b], 16)

            def stage(i, b):
                pool.sem_inc(apart, 1)
                pool.tensor_copy(lhs[b][:], mixT[:, :, ds(i * P, P)]).then_inc(staged, 1)
            pool.wait_ge(mix_in, seen(16))
            for b in range(2):
                stage(b, b)
            with pool.Fori(1, TT // 2) as j:
                for b in range(2):
                    pool.wait_ge(product, seen(2 * j + b - 1))
                    stage(2 * j + b, b)
                    store(2 * j + b - 2, b)
            for b in range(2):
                store(TT - 2 + b, b)
            for b in range(2):
                pool.wait_ge(stored[b], 16 * TT // 2)

        @block.tensor
        def _(pe):
            pe.wait_ge(w_in, seen(16))

            def tile(i, b):
                pe.wait_ge(staged, seen(i + 1))
                for n in range(2):
                    for k in range(KT):
                        last = pe.matmul(ps[:, (2 * b + n) * HALF:(2 * b + n + 1) * HALF], lhs[b][:, k, :],
                                         w[:, k, n * HALF:(n + 1) * HALF], start=(k == 0), stop=(k == KT - 1))
                last.then_inc(product, 1)
            for b in range(2):
                tile(b, b)
            with pe.Fori(1, TT // 2) as j:
                for b in range(2):
                    pe.wait_ge(summed, seen(2 * j + b - 1))
                    tile(2 * j + b, b)

        @block.scalar
        def _(act):
            with act.Fori(0, TT) as i:
                norm.on_scalar(act, i)

        @block.vector
        def _(dve):
            dve.wait_ge(ln_in, seen(32))
            n = [0]

            def tile(i, b, nth, linked):
                def link(ins):
                    n[0] += 1
                    ins.then_inc(links, 1)
                    dve.wait_ge(links, seen(linked + n[0]))
                m = b % 2
                dve.wait_ge(x_in[b], seen(16 * nth + 16))
                dve.wait_ge(product, seen(i + 1))
                if not isinstance(i, int) or i >= 2:
                    dve.wait_ge(stored[m], 8 * (i - m))
                dve.scalar_tensor_tensor(t[m][:], xt[b][:], ALPHA, ps[:, 2 * m * HALF:(2 * m + 2) * HALF],
                                         ALU.mult, ALU.add).then_inc(summed, 1)
                dve.wait_ge(summed, seen(i + 1))
                norm.on_vector(dve, link, t[m], *g_b, i).then_inc(normed, 1)
            for b in range(4):
                tile(b, b, 0, 0)
            with dve.Fori(1, TT // 4) as j:
                n[0] = 0
                for b in range(4):
                    tile(4 * j + b, b, j, 4 * Norm.LINKS * j)


def retrieve_experts(nc, ps, mixT, consts, hidden, wq, ky, wq_in, u, v, ln, out):
    ident = consts["ident"]
    with ExitStack() as ctx:
        sb, sem = allocator(nc, ctx, "ex_"), Semaphores(nc, ctx, "ex_")
        ahead = sb("ahead", [P, D])
        hT = sb("hT", [P, KT, P])
        q = sb("q", [P, 2, P])
        qT = sb("qT", [P, 2, P])
        sc = sb("sc", [P, 2, NK])
        s16 = sb("s16", [P, 2, TOPK])
        i16 = sb("i16", [P, 2, TOPK], U32)
        f16 = sb("f16", [P, 2, TOPK])
        cand = sb("cand", [P, TOPK, TOPK])
        hot = sb("hot", [P, 2, TOPK, TOPK])
        best = sb("best", [P, TOPK])
        at = sb("at", [P, TOPK], U32)
        part = sb("part", [P, 2, TOPK], U32)
        part_f = sb("part_f", [P, 2, TOPK])
        row = sb("row", [P, 2, TOPK])
        iota_i = sb("iota_i", [P, TOPK], U32)
        iota = sb("iota", [P, TOPK])
        total = sb("total", [P, 2, PH])
        idx = sb("idx", [P, TT * NSEL], U32)
        gate = sb("gate", [P, TT * NSEL])
        hc = sb("hc", [P, D])
        rows_u = mixT
        rows_v = sb("rows_v", [P, GRP, D])
        picks = [sb(f"picks{b}", [P, GRP], U32) for b in range(2)]
        z = sb("z", [P, 2, GRP])
        act_z = sb("act_z", [P, 2, GRP])
        wt = sb("wt", [P, 2, GRP])
        diag = sb("diag", [P, 2, GRP, P])
        zero = sb("zero", [P, P])
        keep = sb("keep", [P, P])
        t = sb("t", [P, D])
        g_b = [sb(n, [P, D]) for n in ("g", "b")]
        (iota_made, h_in, h_turned, h_kept, q_made, q_copied, q_turned, qT_copied, sc_made, sc_copied, sc_used,
         steps, chosen, expd, gated, links) = (sem(n) for n in (
             "iota_made h_in h_turned h_kept q_made q_copied q_turned qT_copied sc_made sc_copied sc_used "
             "steps chosen expd gated links").split())
        u_in = [sem(f"u_in{j}", from_zero=True) for j in range(GRP)]
        v_in = [sem(f"v_in{j}", from_zero=True) for j in range(GRP)]
        u_read = [sem(f"u_read{j}") for j in range(GRP)]
        v_read = [sem(f"v_read{j}") for j in range(GRP)]
        (ln_in, ready, picked, h_copied, bent, weighted, spread, summed, normed, stored, copied, apart) = (
            sem(n) for n in ("ln_in ready picked h_copied bent weighted spread summed normed stored "
                             "copied apart").split())
        norm = Norm(sb, sem, "ln", apart)
        sem.start()
        block = ctx.enter_context(nc.Block())
        QUERY, TURN, SCORE, HIDDEN = 2, 3, 4, 5

        def tiles(eng, head, before=None, after=None):
            with eng.Fori(0, PH) as e:
                head(None, e, 0)
            if after:
                after(None, 0)
            with eng.Fori(0, TT - 1) as i:
                if before:
                    before(i, i + 1)
                with eng.Fori(0, PH) as e:
                    head(i, e, i + 1)
                if after:
                    after(i, i + 1)
            if before:
                before(TT - 1, None)
            with eng.Fori(0, PH) as e:
                head(TT - 1, e, None)
            if after:
                after(TT - 1, None)

        @block.gpsimd
        def _(pool):
            pool.iota(iota_i[:], [[1, TOPK]], base=0, channel_multiplier=0).then_inc(iota_made, 1)
            pool.wait_ge(iota_made, seen(1))
            pool.tensor_copy(iota[:], iota_i[:]).then_inc(iota_made, 1)
            pool.memset(zero[:], 0.0).then_inc(ready, 1)
            with pool.Fori(0, TT) as i:
                with pool.Fori(0, PH) as e:
                    pool.wait_ge(chosen, seen(PH * i + e + 1))
                    for b in range(2):
                        n = NG * i + 2 * e + b
                        pool.sem_inc(apart, 1)
                        pool.tensor_copy(picks[b][:], idx[:, ds(i * NSEL + (2 * e + b) * GRP, GRP)]
                                         ).then_inc(picked, 1)
                        pool.wait_ge(picked, seen(n + 1))
                        pool.sem_inc(apart, 1)
                        for table, rows, landed, read in ((u, rows_u, u_in, u_read), (v, rows_v, v_in, v_read)):
                            for j in range(GRP):
                                pool.wait_ge(read[j], seen(n))
                                pool.sem_inc(apart, 1)
                                pool.indirect_dma_start(
                                    out=rows[:, j, :], out_offset=None, in_=table,
                                    in_offset=bass.IndirectOffsetOnAxis(ap=picks[b][:, j:j + 1], axis=0),
                                ).then_inc(landed[j], 16)

        @block.sync
        def _(sp):
            sp.dma_start(ahead[:], hidden[0:P, :]).then_inc(h_in, 16)
            for k in range(2):
                sp.dma_start(g_b[k][:], ln[k].partition_broadcast(P)).then_inc(ln_in, 16)
            sp.wait_ge(h_copied, seen(1))
            sp.wait_ge(h_turned, seen(1))
            sp.dma_start(ahead[:], hidden[P:2 * P, :]).then_inc(h_in, 16)
            with sp.Fori(1, TT - 1) as i:
                sp.wait_ge(h_copied, seen(i + 1))
                sp.wait_ge(h_turned, seen(i + 1))
                sp.dma_start(ahead[:], hidden[ds((i + 1) * P, P), :]).then_inc(h_in, 16)
                sp.wait_ge(normed, seen(i))
                sp.dma_start(out[ds((i - 1) * P, P), :], t[:]).then_inc(stored, 16)
            for i in range(TT - 2, TT):
                sp.wait_ge(normed, seen(i + 1))
                sp.dma_start(out[i * P:(i + 1) * P, :], t[:]).then_inc(stored, 16)
            sp.wait_ge(stored, seen(16 * TT))

        @block.tensor
        def _(pe):
            pe.wait_ge(wq_in, 16 * WQ_LOADS)
            pe.wait_ge(ready, seen(2))

            def turn_hidden(c):
                pe.wait_ge(h_in, seen(16 * c + 16))
                if not isinstance(c, int):
                    pe.wait_ge(h_kept, seen(c))
                for k in range(KT):
                    last = pe.transpose(ps[:, HIDDEN * HALF + k * P:HIDDEN * HALF + (k + 1) * P],
                                        ahead[:, k * P:(k + 1) * P], ident[:])
                last.then_inc(h_turned, 1)

            def query(c, e):
                pe.wait_ge(h_kept, seen(c + 1))
                pe.wait_ge(q_copied, seen(PH * c + e))
                for k in range(KT):
                    last = pe.matmul(ps[:, QUERY * HALF:QUERY * HALF + 2 * P], hT[:, k, :],
                                     wq[:, k, ds(e * 2 * P, 2 * P)], start=(k == 0), stop=(k == KT - 1))
                last.then_inc(q_made, 1)

            def turn_query(c, e):
                pe.wait_ge(q_copied, seen(PH * c + e + 1))
                for x in range(2):
                    last = pe.transpose(ps[:, TURN * HALF + x * P:TURN * HALF + (x + 1) * P], q[:, x, :], ident[:])
                last.then_inc(q_turned, 1)

            def score(c, e):
                pe.wait_ge(qT_copied, seen(PH * c + e + 1))
                pe.wait_ge(sc_copied, seen(PH * c + e))
                for x in range(2):
                    last = pe.matmul(ps[:, SCORE * HALF + x * NK:SCORE * HALF + (x + 1) * NK], qT[:, x, :],
                                     ky[:].rearrange("p m n -> p (m n)")[:, ds((2 * e + x) * NK, NK)],
                                     start=True, stop=True)
                last.then_inc(sc_made, 1)

            def before(i, c):
                if i is None:
                    return
                pe.wait_ge(h_copied, seen(i + 1))
                if not isinstance(i, int) or i:
                    pe.wait_ge(copied, seen(i))
                for n in range(2):
                    pe.matmul(ps[:, n * HALF:(n + 1) * HALF], zero[:], hc[:, n * HALF:(n + 1) * HALF],
                              start=True, stop=False)
                if c is not None:
                    turn_hidden(c)

            def head(i, e, c):
                if i is None:
                    query(c, e)
                    turn_query(c, e)
                    score(c, e)
                    return
                for b in range(2):
                    n = NG * i + 2 * e + b
                    for j in range(GRP):
                        if c is not None and b == 0:
                            if j == 0:
                                query(c, e)
                            if j == 3:
                                turn_query(c, e)
                            if j == 6:
                                score(c, e)
                        pe.wait_ge(v_in[j], 16 * n + 16)
                        pe.wait_ge(spread, seen(GRP * n + j + 1))
                        for m in range(2):
                            last = pe.matmul(ps[:, m * HALF:(m + 1) * HALF], diag[:, b, j, :],
                                             rows_v[:, j, m * HALF:(m + 1) * HALF], start=False, stop=False)
                        last.then_inc(v_read[j], 1)

            def after(i, c):
                if i is None:
                    return
                for n in range(2):
                    last = pe.matmul(ps[:, n * HALF:(n + 1) * HALF], keep[:], hc[:, n * HALF:(n + 1) * HALF],
                                     start=False, stop=True)
                last.then_inc(summed, 1)
            turn_hidden(0)
            tiles(pe, head, before, after)

        @block.scalar
        def _(act):
            act.wait_ge(ready, seen(1))
            act.mul(keep[:], ident[:], ALPHA).then_inc(ready, 1)

            def keep_hidden(c):
                act.wait_ge(h_turned, seen(c + 1))
                act.copy(hT[:], ps[:, HIDDEN * HALF:(HIDDEN + 2) * HALF].rearrange("p (k t) -> p k t", t=P)
                         ).then_inc(h_kept, 1)

            def choice(c, e):
                m = PH * c + e
                act.wait_ge(q_made, seen(m + 1))
                act.wait_ge(q_turned, seen(m))
                act.copy(q[:], ps[:, QUERY * HALF:QUERY * HALF + 2 * P].rearrange("p (x c) -> p x c", c=P)
                         ).then_inc(q_copied, 1)
                act.wait_ge(q_turned, seen(m + 1))
                act.wait_ge(sc_made, seen(m))
                act.copy(qT[:], ps[:, TURN * HALF:TURN * HALF + 2 * P].rearrange("p (x c) -> p x c", c=P)
                         ).then_inc(qT_copied, 1)
                act.wait_ge(sc_made, seen(m + 1))
                act.wait_ge(sc_used, seen(m))
                act.copy(sc[:], ps[:, SCORE * HALF:SCORE * HALF + 2 * NK].rearrange("p (x n) -> p x n", n=NK)
                         ).then_inc(sc_copied, 1)

            def before(i, c):
                if c is not None:
                    keep_hidden(c)

            def head(i, e, c):
                for b in range(2):
                    if i is not None:
                        n = NG * i + 2 * e + b
                        act.wait_ge(u_read[GRP - 1], seen(n + 1))
                        act.activation(act_z[:, b, :], z[:, b, :], ACT.Gelu).then_inc(bent, 1)
                        act.wait_ge(weighted, seen(n + 1))
                        for j in range(GRP):
                            act.activation(diag[:, b, j, :], ident[:], ACT.Copy, scale=wt[:, b, j:j + 1]
                                           ).then_inc(spread, 1)
                    if c is not None and b == 0:
                        choice(c, e)

            def after(i, c):
                if c is not None:
                    act.wait_ge(chosen, seen(PH * c + PH))
                    act.activation(gate[:, ds(c * NSEL, NSEL)], gate[:, ds(c * NSEL, NSEL)], ACT.Exp
                                   ).then_inc(expd, 1)
                if i is not None:
                    act.wait_ge(summed, seen(i + 1))
                    if not isinstance(i, int) or i:
                        act.wait_ge(stored, seen(16 * i))
                    act.copy(t[:], ps[:, 0:D]).then_inc(copied, 1)
                    norm.on_scalar(act, i)
            keep_hidden(0)
            tiles(act, head, before, after)

        @block.vector
        def _(dve):
            per_head, per_tile = 16, 2 + Norm.LINKS
            dve.wait_ge(iota_made, seen(2))
            dve.wait_ge(ln_in, seen(32))

            def choose(c, e):
                n = [0]

                def step(ins):
                    n[0] += 1
                    ins.then_inc(steps, 1)
                    dve.wait_ge(steps, seen(per_head * (PH * c + e) + n[0]))
                    dve.sem_inc(apart, 1)

                def top16(values, vals, idxs):
                    for v, o in zip(values, vals):
                        last = dve.max(o[:, 0:8], v)
                    step(last)
                    for v, o, p in zip(values, vals, idxs):
                        last = dve.max_index(p[:, 0:8], o[:, 0:8], v)
                    step(last)
                    for v, o in zip(values, vals):
                        last = dve.match_replace(v, o[:, 0:8], v, -3e38)
                    step(last)
                    for v, o in zip(values, vals):
                        last = dve.max(o[:, 8:16], v)
                    step(last)
                    for v, o, p in zip(values, vals, idxs):
                        last = dve.max_index(p[:, 8:16], o[:, 8:16], v)
                    return last
                dve.wait_ge(sc_copied, seen(PH * c + e + 1))
                dve.sem_inc(apart, 1)
                step(top16([sc[:, x, :] for x in range(2)], [s16[:, x, :] for x in range(2)],
                           [i16[:, x, :] for x in range(2)]))
                dve.tensor_copy(f16[:], i16[:]).then_inc(sc_used, 1)
                step(dve.tensor_tensor(cand[:], s16[:, 0, :].unsqueeze(2).broadcast_to([P, TOPK, TOPK]),
                                       s16[:, 1, :].unsqueeze(1).broadcast_to([P, TOPK, TOPK]), ALU.add))
                step(top16([cand[:].rearrange("p a b -> p (a b)")], [best[:]], [at[:]]))
                dve.tensor_scalar(part[:, 0], at[:], 4, None, ALU.logical_shift_right)
                step(dve.tensor_scalar(part[:, 1], at[:], TOPK - 1, None, ALU.bitwise_and))
                dve.tensor_scalar(gate[:, ds((PH * c + e) * TOPK, TOPK)], best[:], best[:, 0:1], None,
                                  ALU.subtract)
                step(dve.tensor_copy(part_f[:], part[:]))
                step(dve.tensor_tensor(hot[:], part_f[:].unsqueeze(3).broadcast_to([P, 2, TOPK, TOPK]),
                                       iota[:].unsqueeze(1).unsqueeze(1).broadcast_to([P, 2, TOPK, TOPK]),
                                       ALU.is_equal))
                step(dve.tensor_tensor(hot[:], hot[:], f16[:].unsqueeze(2).broadcast_to([P, 2, TOPK, TOPK]),
                                       ALU.mult))
                step(dve.tensor_reduce(row[:], hot[:], AX.X, ALU.add))
                dve.scalar_tensor_tensor(idx[:, ds((PH * c + e) * TOPK, TOPK)], row[:, 0], float(NK), row[:, 1],
                                         ALU.mult, ALU.add).then_inc(chosen, 1)
                assert n[0] == per_head, n[0]

            def before(i, c):
                dve.wait_ge(h_in, seen(16 * i + 16))
                if not isinstance(i, int) or i:
                    dve.wait_ge(summed, seen(i))
                dve.tensor_copy(hc[:], ahead[:]).then_inc(h_copied, 1)
                dve.wait_ge(h_copied, seen(i + 1))
                dve.sem_inc(apart, 1)

            def head(i, e, c):
                for b in range(2):
                    if i is not None:
                        n = NG * i + 2 * e + b
                        for j in range(GRP):
                            dve.wait_ge(u_in[j], 16 * n + 16)
                            dve.tensor_tensor_reduce(rows_u[:, j, :], rows_u[:, j, :], hc[:], 1.0, 0.0,
                                                     ALU.mult, ALU.add, z[:, b, j:j + 1]).then_inc(u_read[j], 1)
                        dve.wait_ge(bent, seen(n + 1))
                        dve.tensor_tensor(wt[:, b, :], act_z[:, b, :],
                                          gate[:, ds(i * NSEL + (2 * e + b) * GRP, GRP)], ALU.mult
                                          ).then_inc(weighted, 1)
                    if c is not None and b == 1:
                        choose(c, e)

            def after(i, c):
                n = [0]
                tile = 0 if i is None else i + 1

                def link(ins):
                    n[0] += 1
                    ins.then_inc(links, 1)
                    dve.wait_ge(links, seen(per_tile * tile - (Norm.LINKS if i is not None else 0) + n[0]))
                if c is not None:
                    gates = gate[:, ds(c * NSEL, NSEL)].rearrange("p (h k) -> p h k", k=TOPK)
                    dve.wait_ge(expd, seen(c + 1))
                    link(dve.tensor_reduce(total[:, 0, :], gates, AX.X, ALU.add))
                    link(dve.reciprocal(total[:, 1, :], total[:, 0, :]))
                    dve.tensor_tensor(gates, gates, total[:, 1, :].unsqueeze(2).broadcast_to([P, PH, TOPK]),
                                      ALU.mult).then_inc(gated, 1)
                    dve.wait_ge(gated, seen(c + 1))
                if i is not None:
                    dve.wait_ge(copied, seen(i + 1))
                    norm.on_vector(dve, link, t, *g_b, i).then_inc(normed, 1)
            tiles(dve, head, before, after)


def program(nc, x, x_t, w_tiles, rope, masks, sink, perm, mu, low_rank, params, tri, tri_l, eye, ident_in,
            ones_in, w_out, ln1, wq, keys, u, v, ln2, out):
    with ExitStack() as ctx:
        sb = allocator(nc, ctx)
        ps = ctx.enter_context(nc.psum_tensor("ps", [P, 8 * HALF], F32))
        banks = [ps[:, n * HALF:(n + 1) * HALF] for n in range(8)]
        mixT = sb("mixT", [P, KT, SEQ])
        ident = sb("ident", [P, P])
        ones = sb("ones", [P, P])
        chunks = nc.dram_tensor("chunks", [2, NC, P, HP * XS * CH], F32, kind="Internal").ap()
        attended = nc.dram_tensor("attended", [P, 4, SEQ], F32, kind="Internal").ap()
        consts = {"ident": ident, "ones": ones, "eye": eye}
        consts_in = ctx.enter_context(nc.semaphore("consts_in"))
        with nc.Block() as block:
            @block.sync
            def _(sp):
                sp.dma_start(ident[:], ident_in).then_inc(consts_in, 16)
                sp.dma_start(ones[:], ones_in).then_inc(consts_in, 16)
                sp.wait_ge(consts_in, 32)
        with ExitStack() as mixer:
            msb = allocator(nc, mixer)
            feat = msb("feat", [P, 16 * SEQ])
            with ExitStack() as attention:
                asb = allocator(nc, attention)
                at = asb("at", [P, NAT * SEQ])
                with ExitStack() as projection:
                    xT = allocator(nc, projection)("xT", [P, KT, SEQ])
                    project(nc, banks, x_t, w_tiles, xT, feat, at, mu)
                attend(nc, banks, at, mixT, consts, rope, masks, sink, perm, attended)
            gates = msb("gates", [P, 2, HP, NC])
            prepare_chunks(nc, ps, feat, consts, low_rank, params, chunks, gates)
            run_chunks(nc, ps, feat, mixT, consts, chunks, gates, tri, tri_l)
            finish_rwkv(nc, ps, feat, mixT, consts, params)
        hidden = nc.dram_tensor("hidden", [SEQ, D], F32, kind="Internal").ap()
        wq_s = sb("wq_s", [P, KT, 2 * PH * P])
        keys_s = sb("keys_s", [P, 2 * PH, NK])
        wq_in = ctx.enter_context(nc.semaphore("wq_in"))

        def prefetch(sp):
            sp.dma_start(keys_s[:], keys).then_inc(wq_in, 16)
            for k in range(0, KT, 2):
                sp.dma_start(wq_s[:, k:k + 2, :], wq[:, k:k + 2, :]).then_inc(wq_in, 16)
        mix_and_norm(nc, ps, mixT, consts, x, w_out, ln1, attended, hidden, prefetch)
        retrieve_experts(nc, ps, mixT, consts, hidden, wq_s, keys_s, wq_in, u, v, ln2, out)


def constants():
    f = np.float32
    pos = np.arange(SEQ, dtype=f)
    inv = f(10000.0) ** (-np.arange(0, HD, 2, dtype=f) / f(HD))
    ang = np.concatenate([pos[:, None] * inv[None, :]] * 2, -1).astype(f)
    cos, sin = np.cos(ang).T, np.sin(ang).T.copy()
    sin[:HD // 2] *= -1
    rope = np.stack([np.tile(cos, (2, 1)), np.tile(sin, (2, 1))]).astype(f)
    perm = np.zeros((P, P), f)
    for m in range(P):
        perm[m // HD * HD + (m % HD + HD // 2) % HD, m] = 1
    q, k = np.arange(P)[:, None], np.arange(WIN)[None] - P
    masks = np.zeros((P, TT, WIN), f)
    for n in range(TT):
        at = k + n * P
        masks[:, n] = np.where((abs(q - k) <= P) & (at >= 0) & (at < SEQ), 0, NEG)
    j, t = np.meshgrid(np.arange(CH), np.arange(CH), indexing="ij")
    tri = np.stack([np.stack([j <= t, j < t], 1), np.stack([j >= t, j > t], 1)], 1).astype(f)
    tri_l = np.stack([j > t, j < t], 1).astype(f)
    pair = np.kron(np.eye(2, dtype=f), np.ones((HD, HD), f))
    return {"rope": rope, "masks": masks, "perm": perm, "tri": np.tile(tri, (2, 1, 1, 1)),
            "tri_l": np.tile(tri_l, (2, 1, 1)), "eye": np.tile(np.eye(CH, dtype=f), (2, 1)),
            "ident_in": np.eye(P, dtype=f), "ones_in": pair}


def layouts(inp):
    f = np.float32
    o = {"x": inp["x"][0]}
    o["x_t"] = np.ascontiguousarray(inp["x"][0].T.reshape(KT, P, SEQ).transpose(1, 0, 2))
    attn = (NH + 2 * 2) * HD
    n_rwkv = inp["mu_prev"].shape[-1]
    pair_cols = [c for p in range(NH // 2) for s in range(2) for c in range((4 * s + p) * HD, (4 * s + p + 1) * HD)]
    order = list(range(attn, attn + n_rwkv)) + [-1] * (NFT * P - n_rwkv) + pair_cols + list(range(NH * HD, attn))
    w = np.concatenate([inp["w_in"][0], np.zeros((D, 1), f)], 1)[:, order]
    o["w_tiles"] = np.ascontiguousarray(w.reshape(KT, P, NFT + NAT, P).transpose(2, 1, 0, 3))
    mu = np.zeros((2, NFT * P), f)
    mu[0, :n_rwkv], mu[1, :n_rwkv] = inp["mu_prev"][0], inp["mu_next"][0]
    o["mu"] = np.ascontiguousarray(mu.reshape(2, NFT, P).transpose(0, 2, 1))
    lr = np.zeros((HP, P, 5, P), f)
    for hp in range(HP):
        c = slice(hp * P, hp * P + P)
        for n, part in enumerate((inp["w2"][0, 0], inp["w2"][0, 1], inp["a2"][0, 0], inp["a2"][0, 1])):
            lr[hp, 32 * n:32 * n + 32, n] = part[:, c]
        lr[hp, :inp["g2"].shape[1], 4] = inp["g2"][0][:, c]
    o["low_rank"] = lr
    cols = [inp["w0"][0, 0], inp["w0"][0, 1], inp["a0"][0, 0], inp["a0"][0, 1], inp["k_k"][0], inp["k_a"][0],
            inp["r_k"][0].reshape(-1), inp["lnx_g"][0], inp["lnx_b"][0]]
    o["params"] = np.stack([c.reshape(HP, P).T for c in cols], -1)
    o["sink"] = inp["sink"][0].reshape(2, NH // 2).T.reshape(-1)
    rows = pair_cols + list(range(NH * HD, 2 * NH * HD))
    o["w_out"] = np.ascontiguousarray(inp["w_out"][0][rows].reshape(KT, P, D).transpose(1, 0, 2))
    o["ln1"] = np.stack([inp["ln1_g"][0], inp["ln1_b"][0]])
    o["ln2"] = np.stack([inp["ln2_g"][0], inp["ln2_b"][0]])
    o["wq"] = np.ascontiguousarray(inp["peer_wq"][0].reshape(KT, P, 2 * PH * P).transpose(1, 0, 2))
    o["keys"] = np.ascontiguousarray(inp["peer_keys"][0].reshape(2 * PH, NK, P).transpose(2, 0, 1))
    o["u"], o["v"] = inp["peer_u"][0], inp["peer_v"][0]
    return o


_ORDER = ["x", "x_t", "w_tiles", "rope", "masks", "sink", "perm", "mu", "low_rank", "params", "tri", "tri_l",
          "eye", "ident_in", "ones_in", "w_out", "ln1", "wq", "keys", "u", "v", "ln2"]


def kernel(**inputs):
    from concourse import bacc
    from concourse.bass_utils import run_bass_kernel_spmd

    arrays = layouts({k: np.asarray(a) for k, a in inputs.items()})
    arrays.update(constants())
    nc = bacc.Bacc("TRN2", target_bir_lowering=False, num_devices=1)
    args = []
    for name in _ORDER:
        a = arrays[name] = np.ascontiguousarray(arrays[name])
        args.append(nc.dram_tensor("in_" + name, a.shape, mybir.dt.from_np(a.dtype), kind="ExternalInput").ap())
    args.append(nc.dram_tensor("out_y", (SEQ, D), F32, kind="ExternalOutput").ap())
    program(nc, *args)
    r = run_bass_kernel_spmd(nc, [{"in_" + n: arrays[n] for n in _ORDER}], core_ids=[0])
    return r.results[0]["out_y"].reshape(1, SEQ, D)
```
